# Optimizing a Trainium2 kernel written in Bass

```python
import functools
import jax, jax.numpy as jnp
from jax import lax
import numpy as np

D_MODEL = 1024
BATCH = 1
SEQ = 512
DEPTH = 2
DEC_BATCH = 8
DEC_SEQ = 8
PAST_LEN = 256
PAGE_SIZE = 128

D_MIX = D_MODEL
D_CONV = D_MIX // 4
N_HEADS = 8
HEAD_DIM = 64
N_KV = 2
GROUP = N_HEADS // N_KV
D_ATT = N_HEADS * HEAD_DIM
D_POOL = D_MIX - D_CONV - D_ATT
N_POOL = 4
POOL_GD = D_POOL // N_POOL
POOL_WINDOWS = (2, 4, 8, 16)
POOL_MAX = 16
CONV_W = 31
L_BLK = 64
TOP_N = 16
WINDOW = 512
Q_BLOCK = 128
DEC_Q_BLOCK = 1
FORCE = 1e4
NEG = -1e30
TINY = 1e-30
ATT_SCALE = HEAD_DIM ** -0.5
D_FF = 2816
N_EXPERTS = 8
TOP_K = 2
D_FF_E = 1408
ALPHA = (2 * DEPTH) ** 0.25
BETA = (8 * DEPTH) ** -0.25
LN_EPS = 1e-5
OFF_GLU = 2 * D_CONV
OFF_Q = OFF_GLU + D_ATT
OFF_KC = OFF_Q + 2 * N_KV * HEAD_DIM
OFF_KS = OFF_KC + 2 * N_KV * HEAD_DIM
OFF_KW = OFF_KS + 2 * N_KV * HEAD_DIM
OFF_GATE = OFF_KW + 3 * N_HEADS
D_IN = OFF_GATE + D_POOL
IN_SPLITS = (OFF_GLU, OFF_Q, OFF_KC, OFF_KS, OFF_KW, OFF_GATE)

kernel_name = 'hymba_conv_nsa_pool_deepnorm_step'

def layer_norm(x, g, b):
    xf = x.astype(jnp.float32)
    mu = jnp.mean(xf, -1, keepdims=True)
    var = jnp.mean(jnp.square(xf - mu), -1, keepdims=True)
    return ((xf - mu) * lax.rsqrt(var + LN_EPS) * g.astype(jnp.float32) + b.astype(jnp.float32)).astype(x.dtype)

def masked_softmax(s, ok):
    s = jnp.where(ok, s, NEG)
    m = jnp.max(s, -1, keepdims=True)
    e = jnp.where(ok, jnp.exp(s - m), 0.0)
    return e / jnp.maximum(jnp.sum(e, -1, keepdims=True), TINY)

def alibi_slopes():
    h = jnp.arange(1, N_HEADS + 1, dtype=jnp.float32)
    return jnp.exp2(-8.0 * h / N_HEADS).reshape(N_KV, GROUP)

def last_rows(x, n):
    if x.shape[1] >= n:
        return x[:, x.shape[1] - n:]
    pad = [(0, 0)] * x.ndim
    pad[1] = (n - x.shape[1], 0)
    return jnp.pad(x, pad)

def gather_pages(pool, page_table):
    g = pool[page_table]
    return g.reshape(g.shape[0], -1, *pool.shape[2:])

def swiglu(h, w_gu, w_dn):
    g, u = jnp.split(h @ w_gu, 2, axis=-1)
    return (jax.nn.silu(g) * u) @ w_dn

def moe_ffn(h, w_r, b_r, w_gu, w_dn):
    logits = jnp.einsum('btd,de->bte', h, w_r).astype(jnp.float32) + b_r.astype(jnp.float32)
    top_v, top_i = lax.top_k(logits, TOP_K)
    gate = jax.nn.softmax(top_v, axis=-1)
    comb = jnp.einsum('btk,btke->bte', gate, jax.nn.one_hot(top_i, N_EXPERTS, dtype=jnp.float32)).astype(h.dtype)
    out = jnp.zeros_like(h)
    for e in range(N_EXPERTS):
        out = out + comb[..., e:e + 1] * swiglu(h, w_gu[e], w_dn[e])
    return out

def conv_module(glu_in, conv_buf, dw_w, dw_b, ln_g, ln_b, pw_w, pw_b):
    a, g = jnp.split(glu_in, 2, axis=-1)
    u = a * jax.nn.sigmoid(g)
    u_ext = jnp.concatenate([conv_buf.astype(u.dtype), u], axis=1)
    y = lax.conv_general_dilated(u_ext, dw_w[:, None, :].astype(u.dtype), (1,), 'VALID',
                                 dimension_numbers=('NWC', 'WIO', 'NWC'),
                                 feature_group_count=D_CONV) + dw_b
    y = jax.nn.silu(layer_norm(y, ln_g, ln_b))
    return y @ pw_w + pw_b, u_ext[:, u_ext.shape[1] - (CONV_W - 1):]

def pool_mixer(u, pool_buf, pos0, w_grp, scale):
    B, T, _ = u.shape
    P = POOL_MAX - 1
    u_ext = jnp.concatenate([pool_buf.astype(u.dtype), u], axis=1)
    uf = u_ext.astype(jnp.float32)
    cs = jnp.pad(jnp.cumsum(uf, axis=1), ((0, 0), (1, 0), (0, 0)))
    pos = pos0 + jnp.arange(T)
    outs = []
    for gi, w in enumerate(POOL_WINDOWS):
        c0, c1 = gi * POOL_GD, (gi + 1) * POOL_GD
        wsum = cs[:, P + 1:P + 1 + T, c0:c1] - cs[:, P + 1 - w:P + 1 - w + T, c0:c1]
        cnt = jnp.minimum(pos + 1, w).astype(jnp.float32)[None, :, None]
        outs.append(wsum / cnt - uf[:, P:, c0:c1])
    pooled = jnp.stack(outs, axis=2).astype(u.dtype)
    y = jnp.einsum('btgc,gcd->btgd', pooled, w_grp).reshape(B, T, D_POOL) * scale
    return y, u_ext[:, u_ext.shape[1] - P:]

def compress_blocks(kv, pe, w):
    B, L = kv.shape[:2]
    nb = L // L_BLK
    blk = kv[:, :nb * L_BLK].reshape(B, nb, L_BLK, 2, N_KV, HEAD_DIM)
    blk = blk + jnp.transpose(pe, (1, 0, 2))[:, :, None, :]
    return jnp.einsum('bnlchd,clde->bnche', blk, w.reshape(2, L_BLK, HEAD_DIM, HEAD_DIM))

def nsa_compressed_select(q, qpos, kv_full, pe, w):
    L = kv_full.shape[1]
    nb = L // L_BLK
    slopes = alibi_slopes()
    cmp = compress_blocks(kv_full, pe, w)
    s = jnp.einsum('bthgd,bnhd->bthgn', q, cmp[:, :, 0]).astype(jnp.float32)
    centre = jnp.arange(nb, dtype=jnp.float32) * L_BLK + (L_BLK - 1) / 2
    blk_end = (jnp.arange(nb) + 1) * L_BLK - 1
    dist = qpos[:, None].astype(jnp.float32) - centre[None, :]
    s = s - slopes[None, None, :, :, None] * dist[None, :, None, None, :]
    ok = (blk_end[None, :] <= qpos[:, None])[None, :, None, None, :]
    p = masked_softmax(s, ok)
    o_cmp = jnp.einsum('bthgn,bnhd->bthgd', p.astype(q.dtype), cmp[:, :, 1])
    nsel = -(-L // L_BLK)
    imp = jnp.pad(jnp.sum(p, axis=3), ((0, 0), (0, 0), (0, 0), (0, nsel - nb)))
    j = jnp.arange(nsel)
    cur = qpos // L_BLK
    forced = (j[None, :] == 0) | (j[None, :] == cur[:, None]) | (j[None, :] == cur[:, None] - 1)
    score = imp + jnp.where(forced, FORCE, 0.0)[None, :, None, :]
    score = jnp.where((j[None, :] <= cur[:, None])[None, :, None, :], score, NEG)
    _, sel = lax.top_k(score, min(TOP_N, nsel))
    sel_ok = sel <= cur[None, :, None, None]
    return o_cmp, sel, sel_ok

def nsa_sparse_branches(q, qpos0, sel, sel_ok, kv_slc, kv_swa, swa_pos0, q_block):
    B, Tq = q.shape[:2]
    L = kv_slc.shape[1]
    nsel = -(-L // L_BLK)
    slopes = alibi_slopes()
    kvb = jnp.pad(kv_slc, ((0, 0), (0, nsel * L_BLK - L), (0, 0), (0, 0), (0, 0)))
    kvb = kvb.reshape(B, nsel, L_BLK, 2, N_KV, HEAD_DIM).transpose(0, 4, 1, 2, 3, 5)
    swa_pad = jnp.pad(kv_swa, ((0, 0), (WINDOW, 0), (0, 0), (0, 0), (0, 0)))
    nqb = Tq // q_block
    bi = jnp.arange(B)[:, None, None, None]
    hi = jnp.arange(N_KV)[None, None, :, None]

    def blocks(a):
        return jnp.moveaxis(a.reshape(B, nqb, q_block, *a.shape[2:]), 1, 0)

    def one_block(args):
        qb, sb, okb, t0 = args
        tpos = t0 + jnp.arange(q_block)
        g = kvb[bi, hi, sb]
        kpos = sb[..., None] * L_BLK + jnp.arange(L_BLK)
        dist = tpos[None, :, None, None, None] - kpos
        ok = okb[..., None] & (dist >= 0)
        s = jnp.einsum('bthgd,bthkld->bthgkl', qb, g[..., 0, :]).astype(jnp.float32)
        s = s - slopes[None, None, :, :, None, None] * dist[:, :, :, None].astype(jnp.float32)
        nk = s.shape[-2] * L_BLK
        p = masked_softmax(s.reshape(B, q_block, N_KV, GROUP, nk), ok.reshape(B, q_block, N_KV, 1, nk))
        o_slc = jnp.einsum('bthgn,bthnd->bthgd', p.astype(qb.dtype), g[..., 1, :].reshape(B, q_block, N_KV, nk, HEAD_DIM))
        wkv = lax.dynamic_slice_in_dim(swa_pad, t0 - swa_pos0, WINDOW + q_block, axis=1)
        wpos = t0 - WINDOW + jnp.arange(WINDOW + q_block)
        wd = tpos[:, None] - wpos[None, :]
        wok = (wd >= 0) & (wd < WINDOW) & (wpos >= swa_pos0)[None, :]
        s = jnp.einsum('bthgd,bshd->bthgs', qb, wkv[:, :, 0]).astype(jnp.float32)
        s = s - slopes[None, None, :, :, None] * wd[None, :, None, None, :].astype(jnp.float32)
        p = masked_softmax(s, wok[None, :, None, None, :])
        o_swa = jnp.einsum('bthgs,bshd->bthgd', p.astype(qb.dtype), wkv[:, :, 1])
        return o_slc, o_swa

    t0s = qpos0 + jnp.arange(nqb, dtype=jnp.int32) * q_block
    o_slc, o_swa = lax.map(one_block, (blocks(q), blocks(sel), blocks(sel_ok), t0s))
    unb = lambda o: jnp.moveaxis(o, 0, 1).reshape(B, Tq, N_KV, GROUP, HEAD_DIM)
    return unb(o_slc), unb(o_swa)

def trunk_layer(h, pos0, past, q_block, wbuf, lw, ffn):
    B, T, _ = h.shape
    z = h @ lw['w_in'] + lw['b_in']
    glu_in, q, kv_c, kv_s, kv_w, gate, u_pool = jnp.split(z, IN_SPLITS, axis=-1)
    q = q.reshape(B, T, N_KV, GROUP, HEAD_DIM) * ATT_SCALE
    kv_c = kv_c.reshape(B, T, 2, N_KV, HEAD_DIM)
    kv_s = kv_s.reshape(B, T, 2, N_KV, HEAD_DIM)
    kv_w = kv_w.reshape(B, T, 2, N_KV, HEAD_DIM)
    gate = jax.nn.sigmoid(gate.astype(jnp.float32)).reshape(B, T, N_KV, GROUP, 3).astype(h.dtype)
    qpos = pos0 + jnp.arange(T)
    if past is None:
        kc_full, ks_full, kw_ext, swa_pos0 = kv_c, kv_s, kv_w, pos0
        conv_buf = jnp.zeros((B, CONV_W - 1, D_CONV), h.dtype)
        pool_buf = jnp.zeros((B, POOL_MAX - 1, D_POOL), h.dtype)
    else:
        cmp_past, slc_past, swa_buf, conv_buf, pool_buf = past
        kc_full = jnp.concatenate([cmp_past.astype(kv_c.dtype), kv_c], axis=1)
        ks_full = jnp.concatenate([slc_past.astype(kv_s.dtype), kv_s], axis=1)
        kw_ext = jnp.concatenate([swa_buf.astype(kv_w.dtype), kv_w], axis=1)
        swa_pos0 = pos0 - swa_buf.shape[1]
    o_cmp, sel, sel_ok = nsa_compressed_select(q, qpos, kc_full, lw['cmp_pe'], lw['cmp_w'])
    o_slc, o_swa = nsa_sparse_branches(q, pos0, sel, sel_ok, ks_full, kw_ext, swa_pos0, q_block)
    o_att = (gate[..., 0:1] * o_cmp + gate[..., 1:2] * o_slc + gate[..., 2:3] * o_swa).reshape(B, T, D_ATT)
    y_conv, conv_new = conv_module(glu_in, conv_buf, lw['conv_dw_w'], lw['conv_dw_b'], lw['conv_ln_g'],
                                   lw['conv_ln_b'], lw['conv_pw_w'], lw['conv_pw_b'])
    y_pool, pool_new = pool_mixer(u_pool, pool_buf, pos0, lw['pool_w'], lw['pool_scale'])
    mix = jnp.concatenate([y_conv, o_att, y_pool], axis=-1) @ lw['w_out'] + lw['b_out']
    h = layer_norm(ALPHA * h + mix, lw['ln1_g'], lw['ln1_b'])
    h = layer_norm(ALPHA * h + ffn(h), lw['ln2_g'], lw['ln2_b'])
    return h, (kv_c, kv_s, last_rows(kw_ext, wbuf), conv_new, pool_new)

def setup_inputs(seed: int = 0) -> dict:
    key = jax.random.key(seed)
    ks = jax.random.split(key, 40)

    def nrm(i, shape, scale):
        return scale * jax.random.normal(ks[i], shape, jnp.float32)

    n_pages = PAST_LEN // PAGE_SIZE
    n_used = DEC_BATCH * n_pages
    n_phys = n_used + max(1, n_used // 4)
    wbuf = min(WINDOW, PAST_LEN)
    n_dense = (DEPTH + 1) // 2
    n_moe = DEPTH // 2
    page_table = jax.random.permutation(ks[7], n_phys)[:n_used].reshape(DEC_BATCH, n_pages).astype(jnp.int32)
    return {
        'x_prompt': nrm(0, (BATCH, SEQ, D_MODEL), 1.0),
        'x_sample': nrm(1, (DEC_BATCH, DEC_SEQ, D_MODEL), 1.0),
        'cache_cmp_kv': nrm(2, (DEPTH, n_phys, PAGE_SIZE, 2, N_KV, HEAD_DIM), 1.0),
        'cache_slc_kv': nrm(3, (DEPTH, n_phys, PAGE_SIZE, 2, N_KV, HEAD_DIM), 1.0),
        'cache_swa_kv': nrm(4, (DEPTH, DEC_BATCH, wbuf, 2, N_KV, HEAD_DIM), 1.0),
        'state_conv': nrm(5, (DEPTH, DEC_BATCH, CONV_W - 1, D_CONV), 0.5),
        'state_pool': nrm(6, (DEPTH, DEC_BATCH, POOL_MAX - 1, D_POOL), 1.0),
        'page_table': page_table,
        'ln_in_g': 1.0 + nrm(8, (D_MODEL,), 0.05),
        'ln_in_b': nrm(9, (D_MODEL,), 0.02),
        'w_in': nrm(10, (DEPTH, D_MODEL, D_IN), D_MODEL ** -0.5),
        'b_in': nrm(11, (DEPTH, D_IN), 0.02),
        'conv_dw_w': nrm(12, (DEPTH, CONV_W, D_CONV), CONV_W ** -0.5),
        'conv_dw_b': nrm(13, (DEPTH, D_CONV), 0.02),
        'conv_ln_g': 1.0 + nrm(14, (DEPTH, D_CONV), 0.05),
        'conv_ln_b': nrm(15, (DEPTH, D_CONV), 0.02),
        'conv_pw_w': nrm(16, (DEPTH, D_CONV, D_CONV), D_CONV ** -0.5),
        'conv_pw_b': nrm(17, (DEPTH, D_CONV), 0.02),
        'cmp_pe': nrm(18, (DEPTH, 2, L_BLK, HEAD_DIM), 0.1),
        'cmp_w': nrm(19, (DEPTH, 2, L_BLK * HEAD_DIM, HEAD_DIM), (L_BLK * HEAD_DIM) ** -0.5),
        'pool_w': nrm(20, (DEPTH, N_POOL, POOL_GD, POOL_GD), POOL_GD ** -0.5),
        'pool_scale': 1.0 + nrm(21, (DEPTH, D_POOL), 0.1),
        'w_out': nrm(22, (DEPTH, D_MIX, D_MODEL), BETA * D_MIX ** -0.5),
        'b_out': nrm(23, (DEPTH, D_MODEL), 0.02),
        'ln1_g': 1.0 + nrm(24, (DEPTH, D_MODEL), 0.05),
        'ln1_b': nrm(25, (DEPTH, D_MODEL), 0.02),
        'ln2_g': 1.0 + nrm(26, (DEPTH, D_MODEL), 0.05),
        'ln2_b': nrm(27, (DEPTH, D_MODEL), 0.02),
        'ffn_w_gu': nrm(28, (n_dense, D_MODEL, 2 * D_FF), D_MODEL ** -0.5),
        'ffn_w_dn': nrm(29, (n_dense, D_FF, D_MODEL), BETA * D_FF ** -0.5),
        'moe_w_router': nrm(30, (n_moe, D_MODEL, N_EXPERTS), D_MODEL ** -0.5),
        'moe_b_router': nrm(31, (n_moe, N_EXPERTS), 0.01),
        'moe_w_gu': nrm(32, (n_moe, N_EXPERTS, D_MODEL, 2 * D_FF_E), D_MODEL ** -0.5),
        'moe_w_dn': nrm(33, (n_moe, N_EXPERTS, D_FF_E, D_MODEL), BETA * D_FF_E ** -0.5),
    }

def reference(x_prompt, x_sample, cache_cmp_kv, cache_slc_kv, cache_swa_kv, state_conv, state_pool, page_table,
              ln_in_g, ln_in_b, w_in, b_in, conv_dw_w, conv_dw_b, conv_ln_g, conv_ln_b, conv_pw_w, conv_pw_b,
              cmp_pe, cmp_w, pool_w, pool_scale, w_out, b_out, ln1_g, ln1_b, ln2_g, ln2_b,
              ffn_w_gu, ffn_w_dn, moe_w_router, moe_b_router, moe_w_gu, moe_w_dn):
    wbuf = cache_swa_kv.shape[2]
    hp = layer_norm(x_prompt, ln_in_g, ln_in_b)
    hs = layer_norm(x_sample, ln_in_g, ln_in_b)
    st_p, st_s = [], []
    for l in range(DEPTH):
        lw = {'w_in': w_in[l], 'b_in': b_in[l], 'conv_dw_w': conv_dw_w[l], 'conv_dw_b': conv_dw_b[l],
              'conv_ln_g': conv_ln_g[l], 'conv_ln_b': conv_ln_b[l], 'conv_pw_w': conv_pw_w[l],
              'conv_pw_b': conv_pw_b[l], 'cmp_pe': cmp_pe[l], 'cmp_w': cmp_w[l], 'pool_w': pool_w[l],
              'pool_scale': pool_scale[l], 'w_out': w_out[l], 'b_out': b_out[l], 'ln1_g': ln1_g[l],
              'ln1_b': ln1_b[l], 'ln2_g': ln2_g[l], 'ln2_b': ln2_b[l]}
        if l % 2 == 0:
            ffn = functools.partial(swiglu, w_gu=ffn_w_gu[l // 2], w_dn=ffn_w_dn[l // 2])
        else:
            ffn = functools.partial(moe_ffn, w_r=moe_w_router[l // 2], b_r=moe_b_router[l // 2],
                                    w_gu=moe_w_gu[l // 2], w_dn=moe_w_dn[l // 2])
        hp, sp = trunk_layer(hp, 0, None, min(Q_BLOCK, hp.shape[1]), wbuf, lw, ffn)
        past = (gather_pages(cache_cmp_kv[l], page_table), gather_pages(cache_slc_kv[l], page_table),
                cache_swa_kv[l], state_conv[l], state_pool[l])
        hs, ss = trunk_layer(hs, PAST_LEN, past, DEC_Q_BLOCK, wbuf, lw, ffn)
        st_p.append(sp)
        st_s.append(ss)
    stk = lambda sts, i: jnp.stack([s[i] for s in sts], axis=0)
    return (hp, hs, stk(st_p, 0), stk(st_s, 0), stk(st_p, 1), stk(st_s, 1), stk(st_p, 2), stk(st_s, 2),
            stk(st_p, 3), stk(st_s, 3), stk(st_p, 4), stk(st_s, 4))


_drawn_inputs = setup_inputs


def setup_inputs(seed=0):
    import zlib

    import numpy as np

    out = dict(_drawn_inputs(seed))
    spreads = {}
    factors = {'conv_dw_b': 5.621,
     'conv_ln_g': 3.677,
     'conv_ln_b': 6.955,
     'conv_pw_b': 5.26,
     'moe_b_router': 3.44}
    for name, (base, spread) in spreads.items():
        noise = np.random.default_rng([zlib.crc32(name.encode()), seed]).standard_normal(out[name].shape)
        drawn = base * np.exp(spread * noise) if base else spread * noise
        out[name] = __import__('jax').numpy.asarray(drawn.astype(out[name].dtype))
    for name, factor in factors.items():
        out[name] = (out[name] * factor).astype(out[name].dtype)
    return out
```

```python
import concourse.bass as bass
import numpy as np
from concourse import mybir
from contextlib import ExitStack

F32 = mybir.dt.float32
I32 = mybir.dt.int32
ALU = mybir.AluOpType
ACT = mybir.ActivationFunctionType
AX = mybir.AxisListType

P = 128
D = 1024
KD = D // P
SEQ, NB, TB = 512, 8, 8
NS = NB * TB
TOK = SEQ + NS
HALF = TOK // 2
DEPTH = 2
HD, NKV, GRP = 64, 2, 4
NH = NKV * GRP
PAST, PAGE = 256, 128
NPG = PAST // PAGE
LB = 64
NBP, NBS = SEQ // LB, PAST // LB
NBLK = NBP + NB * NBS
CW, PW = 31, 16
ALPHA = float((2 * DEPTH) ** 0.25)
EPS = 1e-5
FLOOR, TINY, BIG = -1e29, 1e-30, 3e32
DFF, DFE, NE = 2816, 1408, 8
NFC = DFF // 256
NEC = 6
CH = 128
ROWS = 2 * TOK
NT = NE + ROWS // CH
WINDOWS = (2, 4, 8, 16)
UP, US = CW - 1 + SEQ, CW - 1 + TB
EP, ES = PW - 1 + SEQ, PW - 1 + TB
EXT = EP + NB * ES
NPAIR = NB // 2
SLOPE = [2.0 ** -(h + 1) for h in range(NH)]

TILES = ["g0", "g1", "a0", "a1", "wk", "wv", "p0", "p1", "ck", "cv", "sk", "sv", "q0", "q1", "q2", "q3", "gate"]


def columns(widths):
    at, out = 0, {}
    for name, w in widths:
        out[name] = at
        at += w
    return out, at


PAR, NPAR = columns([("bin", 17), ("cw", 2 * CW), ("cb", 2), ("clg", 2), ("clb", 2), ("pwb", 2), ("psc", 2),
                     ("bo", KD), ("g1", KD), ("b1", KD), ("g2", KD), ("b2", KD)])
CON, NCON = columns([("ident", P), ("invw", 2), ("invt", 2 * PW), ("hmask", NH),
                     ("cbias", 4 * NKV * GRP * NBP), ("spast", PAST), ("snew", NPAIR * NS), ("scmp", NPAIR * NBLK)])
MCON, NMCON = columns([("ustrict", P), ("ones", P), ("rev", NE), ("iota", NE), ("task", NE * NT), ("rb", NE)])


def schedule():
    out = [("lm", "lnc"), ("lv", "act")]
    for l in range(DEPTH):
        own = {"g": "act", "a": "dve", "w": "act", "p": "act", "c": "act", "s": "act", "q": "dve"}
        out += [(f"{n}.{l}", "act" if n == "gate" else own[n[0]]) for n in TILES]
        out += [(f"vt{t}.{l}", "act") for t in range(5)]
        out += [(f"cmp{c}.{l}", "dve") for c in range(2)]
        out += [(f"vct.{l}", "act"), (f"gs.{l}", "dve")]
        out += [(f"pm{c}.{l}", "act") for c in range(2)]
        out += [(f"cm.{l}", "lnc"), (f"cvar.{l}", "act")]
        out += [(f"pw{c}.{l}", "act") for c in range(2)]
        out += [(f"o{m}.{l}", "dve") for m in range(KD)]
        out += [(f"lm1.{l}", "lnc"), (f"lv1.{l}", "act")]
        if l == 0:
            for c in range(NFC + 1):
                if c < NFC:
                    out += [(f"fg0.{c}", "act"), (f"fu0.{c}", "dve"), (f"fg1.{c}", "act"), (f"fu1.{c}", "dve")]
                if c > 0:
                    out += [(f"fd{m}.{c - 1}", "dve") for m in range(KD)]
            out += [("lm2", "lnc"), ("lv2", "act")]
        else:
            out += [("rt", "dve")] + [(f"ht{t}", "act") for t in range(5)] + [("rk", "dve")]
    return out


def in_order(eng, own):
    counts = {}

    def done(ins, event=own, start=0):
        ins.then_inc(event, 1)
        counts[id(event)] = counts[id(event)] + 1 if id(event) in counts else 1
        eng.wait_ge(event, start + counts[id(event)])

    return done


def program(nc, a):
    sched = schedule()
    ZI = {name: n for n, (name, _) in enumerate(sched)}
    ctx = ExitStack()
    with ctx:
        def sb(name, width, rows=P, dt=F32):
            return ctx.enter_context(nc.sbuf_tensor(name, [rows, width], dt))

        H = sb("h", KD * TOK)
        X = sb("x", KD * TOK)
        YT = sb("yt", KD * TOK)
        WR = [sb(f"w{i}", 4096) for i in range(3)]
        QA = sb("qarena", 5 * D)
        KVZ = sb("kvz", 4 * TOK)
        KCS = sb("kcs", 2 * NS)
        CA = sb("carena", 4096)
        VG = sb("vtok", 5 * 280)
        UE = sb("uext", 2 * (UP + NB * US))
        PA = sb("parena", 5632)
        BIAS = sb("bias", NH * SEQ)
        PAR_ = sb("par", DEPTH * NPAR + 2 * KD)
        CON_ = sb("con", NCON)
        MEAN = sb("mean", P)
        MEANC = sb("meanc", P)
        CCT = sb("cct", 2 * NBLK)
        VC = sb("vc", P, rows=NBLK)
        PC = sb("pc", 2 * NBLK)
        SM = sb("sm", 64)
        BQ = sb("bq", 4 * DEPTH)
        PT = sb("pages", NB * NPG, rows=1, dt=I32)
        SLOT = sb("slot", 10, dt=I32)
        TASK = sb("task", 2 * NT + 1, rows=1, dt=I32)
        PS = ctx.enter_context(nc.psum_tensor("ps", [P, 8, 512], F32))
        x_dram = nc.dram_tensor("sorted_rows", [ROWS + CH, D], F32).ap()
        y_dram = nc.dram_tensor("expert_rows", [ROWS + CH, D], F32).ap()

        h = H[:, :].rearrange("p (k n) -> p k n", k=KD)
        x = X[:, :].rearrange("p (k n) -> p k n", k=KD)
        yt = YT[:, :].rearrange("p (k n) -> p k n", k=KD)
        conv = X[:, 0:2 * TOK].rearrange("p (c n) -> p c n", c=2)
        sig = X[:, 2 * TOK:4 * TOK].rearrange("p (c n) -> p c n", c=2)
        pooled = sig
        ext = X[:, 4 * TOK:4 * TOK + 2 * EXT].rearrange("p (c n) -> p c n", c=2)
        gT = X[0:24, 4 * TOK + 2 * EXT:5 * TOK + 2 * EXT]
        wgate = X[:, 5 * TOK + 2 * EXT:5 * TOK + 2 * EXT + 192].rearrange("p (k n) -> p k n", k=KD)
        gx = YT[0:24, 4 * EXT + 96:4 * EXT + 96 + NPAIR * P]
        win_a = YT[:, 0:2 * EXT].rearrange("p (c n) -> p c n", c=2)
        win_b = YT[:, 2 * EXT:4 * EXT].rearrange("p (c n) -> p c n", c=2)
        qz = QA[:, 0:NKV * GRP * SEQ].rearrange("p (g j n) -> p g j n", g=NKV, j=GRP)
        qs = QA[:, NKV * GRP * SEQ:].rearrange("p (a b r) -> p a b r", a=NPAIR, b=2)
        kvz = KVZ[:, :].rearrange("p (k n) -> p k n", k=4)
        kcs = KCS[:, :].rearrange("p (c n) -> p c n", c=2)
        cpair = CA[:, :].rearrange("p (s w b g n) -> p s w b g n", s=2, w=2, b=2, g=NPG)
        vg = VG[:, :].rearrange("p (t n) -> p t n", t=5)
        ue = UE[:, :].rearrange("p (c n) -> p c n", c=2)
        cmpt = PA[:, 0:2 * (NBLK + 1) * LB].rearrange("p (c n l) -> p c n l", c=2, l=LB)
        pr = [ap.rearrange("p (j n) -> p j n", j=GRP) for ap in (PA[:, 0:2048], PA[:, 2048:4096], X[:, 4 * TOK:4 * TOK + 2048])]
        pcmp = [PC[:, NBLK * i:NBLK * (i + 1)] for i in range(2)]
        ptr = PA[:, 4096:5632].rearrange("p (s n) -> p s n", s=3)
        hid = PA[:, 0:4 * TOK].rearrange("p (s k n) -> p s k n", s=2, k=2)
        silu = PA[:, 4 * TOK:5 * TOK]
        sq = PA[:, 5 * TOK:7 * TOK].rearrange("p (s n) -> p s n", s=2)
        std = PA[:, 7 * TOK:8 * TOK]
        poolw = PA[:, 0:2 * P].rearrange("p (c n) -> p c n", c=2)
        pww = PA[:, 2 * P:6 * P].rearrange("p (c n) -> p c n", c=2)
        wd = CA[:, :].rearrange("p (s k n) -> p s k n", s=2, k=2)
        bias = BIAS[:, :].rearrange("p (h n) -> p h n", h=NH)
        cct = CCT[:, :].rearrange("p (c n) -> p c n", c=2)
        ident = CON_[:, 0:P]
        cbias = CON_[:, CON["cbias"]:CON["cbias"] + 256].rearrange("p (i g n) -> p i g n", i=4, g=NKV)
        htok = QA[:, :].rearrange("p (t n) -> p t n", t=5)
        xg = PA[:, 0:2 * D].rearrange("p (s n) -> p s n", s=2)
        xgT = PA[:, 2 * D:3 * D].rearrange("p (k n) -> p k n", k=KD)
        ehT = PA[:, 3 * D:3 * D + 512].rearrange("p (s k n) -> p s k n", s=2, k=2)
        esil = PA[:, 3584:4096].rearrange("p (s n) -> p s n", s=2)
        ehid = PA[:, 4096:4608].rearrange("p (s n) -> p s n", s=2)
        ysb = PA[:, 4608:5632]
        MC = KVZ[:, 0:NMCON]
        RT = KVZ[:, 640:1664]
        wrt = KVZ[:, 1664:1728].rearrange("p (k n) -> p k n", k=KD)
        ygat = X[:, 0:4096].rearrange("p (s w n) -> p s w n", s=2, w=2)
        xf = YT[:, 0:2048].rearrange("p (s n) -> p s n", s=2)
        lnrow = YT[:, 2048:4096].rearrange("p (s n) -> p s n", s=2)
        zrow = CA[:, 0:D]

        def par(name, l, n=0, rows=P):
            at = l * NPAR + PAR[name] + n
            return PAR_[0:rows, at:at + 1]

        def z_pair(name):
            return 2 * (ZI[name] % 4)

        def pair(name, rows=P):
            b = z_pair(name)
            return PS[0:rows, b:b + 2, 0:HALF]

        def less(s, j, n=1):
            return SM[:, 5 * s + j:5 * s + j + n]

        def total(s, j, n=1):
            return SM[:, 16 + 5 * s + j:16 + 5 * s + j + n]

        def flat(ap):
            return ap.rearrange("p (a n) -> p a n", a=2)

        def pieces(name, rows=slice(0, P)):
            b = z_pair(name)
            return [(PS[rows, b, 0:HALF], 0, HALF), (PS[rows, b + 1, 0:SEQ - HALF], HALF, SEQ),
                    (PS[rows, b + 1, SEQ - HALF:HALF], SEQ, TOK)]

        def ev(name):
            return ctx.enter_context(nc.semaphore(name))

        def freed(name):
            n = ZI[name]
            return ln_done(name) if sched[n][1] == "lnc" else sum(o == sched[n][1] for _, o in sched[:n + 1])

        w_loaded = [ctx.enter_context(nc.semaphore(f"w_loaded{i}")) for i in range(3)]
        d_loaded = [ctx.enter_context(nc.semaphore(f"d_loaded{i}")) for i in range(2)]
        half_read = ev("half_read")
        z_full = ev("z_full")
        act_own, dve_own, pool_own = (ctx.enter_context(nc.semaphore(n)) for n in ("act_own", "dve_own", "pool_own"))
        consts_in, x_in = (ctx.enter_context(nc.semaphore(n)) for n in ("consts_in", "x_in"))
        states_in, pages_in, mixw_in = (ctx.enter_context(nc.semaphore(n)) for n in ("states_in", "pages_in", "mixw_in"))
        pair_in = [ctx.enter_context(nc.semaphore(f"pair_in{i}")) for i in range(2)]
        pt_in, out_kv, out_state, out_past = (ctx.enter_context(nc.semaphore(n)) for n in ("pt_in", "out_kv", "out_state", "out_past"))
        ones_set, qz_zeroed, zeros_set = ev("ones_set"), ev("qz_zeroed"), ev("zeros_set")
        ln_centered, ln_squared, ln_sq_used, ln_scaled, ln_out = (
            ev(n) for n in ("ln_centered", "ln_squared", "ln_sq_used", "ln_scaled", "ln_out"))
        z_free = {"act": ev("z_free_act"), "dve": ev("z_free_dve"), "lnc": ln_centered}
        conv_done, pooled_ready = (ev(n) for n in ("conv_done", "pooled_ready"))
        s_full, s_read, p_max, p_exp, p_ready, t_full, t_out, av_done, o_out = (
            ev(n) for n in ("s_full", "s_read", "p_max", "p_exp", "p_ready", "t_full", "t_out", "av_done", "o_out"))
        h_scaled, gate_spread = ev("h_scaled"), ev("gate_spread")
        slot_ready, task_ready, route_masks = (ev(n) for n in ("slot_ready", "task_ready", "route_masks"))
        moe_rb, moe_in, xd_zero, scattered = (ctx.enter_context(nc.semaphore(n)) for n in ("moe_rb", "moe_in", "xd_zero", "scattered"))
        x_loaded, y_stored, lnrow_in = (ctx.enter_context(nc.semaphore(n)) for n in ("x_loaded", "y_stored", "lnrow_in"))
        x_turned, xT_ready, e_full, e_silu, e_hid, eT_full, eT_ready, e_down, e_yout = (
            ctx.enter_context(nc.semaphore(n)) for n in ("x_turned", "xT_ready", "e_full", "e_silu", "e_hid", "eT_full",
                                                         "eT_ready", "e_down", "e_yout"))
        ysb_free = ctx.enter_context(nc.semaphore("ysb_free"))
        dve_loop, act_loop = (ctx.enter_context(nc.semaphore(n)) for n in ("dve_loop", "act_loop"))
        y_gathered = [ctx.enter_context(nc.semaphore(f"y_gathered{i}")) for i in range(2)]
        gate_exp, var_ready, dev_ready = (ev(n) for n in ("gate_exp", "var_ready", "dev_ready"))
        fin_ready, out_y = ev("fin_ready"), [ctx.enter_context(nc.semaphore(f"out_y{i}")) for i in range(2)]

        chunk_of = {}
        for l in range(DEPTH):
            for n in ["glu", "kwp", "kcks", "q", "cmp0", "cmp1", "cmp2", "cmp3", "wo0", "wo1"]:
                chunk_of[n, l] = len(chunk_of)
            if l == 0:
                for c in range(NFC):
                    chunk_of["ffn", c] = len(chunk_of)
        NWC = len(chunk_of)
        last_read = {("glu", "a1"), ("kwp", "p1"), ("kcks", "sv"), ("q", "q3"), ("cmp1", "cmp0"), ("cmp3", "cmp1"),
                     ("wo0", "o3"), ("wo1", "o7")}
        chunk_read = {}
        for l in range(DEPTH):
            for n, z in last_read:
                chunk_read[chunk_of[n, l]] = z_full, ZI[f"{z}.{l}"] + 1
            for i, n in enumerate(("cmp0", "cmp2")):
                chunk_read[chunk_of[n, l]] = half_read, 2 * l + i + 1
        for c in range(NFC):
            chunk_read[chunk_of["ffn", c]] = z_full, ZI[f"fu1.{c}"] + 1
        ln_order = [("lm", KD), ("cm.0", 2), ("lm1.0", KD), ("lm2", KD), ("cm.1", 2), ("lm1.1", KD)]
        ln_before = {}
        for i, (n, _) in enumerate(ln_order):
            ln_before[n] = (i, sum(k for _, k in ln_order[:i]))
        LN_ALL = sum(k for _, k in ln_order)

        def ln_done(name):
            i, before = ln_before[name]
            return before + dict(ln_order)[name]

        units = [(i, g, w) for i in range(4) for g in range(NKV) for w in range(2)]
        NU = len(units)
        S_L = NU * GRP + NU // 2 + 3 * NPAIR
        T_P = sum(i + 1 for i, _, _ in units) + NU // 2
        T_L = T_P + 2 * NPAIR

        def tiles_through(u):
            if u >= NU:
                return T_P + u - NU + 1
            return sum(i + 1 + (w == 0) for i, _, w in units[:u + 1])

        U_L = NU + 2 * NPAIR
        O_L = NU // 2 + NPAIR
        block = ctx.enter_context(nc.Block())

        @block.sync
        def _(sp):
            sp.dma_start(x, a["xt"]).then_inc(x_in, 16)
            sp.dma_start(PAR_[:, :], a["par"]).then_inc(consts_in, 16)
            sp.dma_start(CON_[:, :], a["con"]).then_inc(consts_in, 16)
            sp.dma_start(PT[:, :], a["page_table"]).then_inc(pt_in, 16)
            sp.dma_start(BIAS[:, :], a["bias"]).then_inc(consts_in, 16)

            def load_w(key, src, n=4096):
                c = chunk_of[key]
                if c >= 3:
                    done, count = chunk_read[c - 3]
                    sp.wait_ge(done, count)
                sp.dma_start(WR[c % 3][:, 0:n], src).then_inc(w_loaded[c % 3], 16)

            sp.wait_ge(pt_in, 16)
            page = [sp.value_load(PT[0:1, n:n + 1], min_val=0, max_val=a["cmp_pages"].shape[1] - 1) for n in range(NB * NPG)]

            def load_pair(l, n):
                if n >= 2:
                    sp.wait_ge(av_done, l * T_L + T_P + 2 * (n - 1))
                if l == 1 and n == 0:
                    sp.wait_ge(z_full, ZI[f"fd{KD - 1}.{NFC - 1}"] + 1)
                for b in range(2):
                    for g in range(NPG):
                        sp.dma_start(cpair[:, n % 2, 0, b, g, :],
                                     a["slc_pages"][l, bass.ds(page[(2 * n + b) * NPG + g], 1), :, :].rearrange("a p n -> (a p) n")
                                     ).then_inc(pair_in[n % 2], 16)
                sp.dma_start(cpair[:, n % 2, 1], a["swa_pairs"][l, n]).then_inc(pair_in[n % 2], 16)

            for l in range(DEPTH):
                load_w(("glu", l), a["w_in"][l, 0])
                load_w(("kwp", l), a["w_in"][l, 1])
                load_w(("kcks", l), a["w_in"][l, 2])
                sp.wait_ge(ln_out, ln_done("lm" if l == 0 else "lm2"))
                sp.dma_start(wgate, a["w_gate"][l]).then_inc(states_in, 16)
                for c in range(2):
                    sp.dma_start(ext[:, c, EP:].rearrange("p (b n) -> p b n", b=NB)[:, :, 0:PW - 1],
                                 a["state_pool"][l, :, c]).then_inc(states_in, 16)
                if l == 1:
                    sp.wait_ge(conv_done, 2)
                    sp.wait_ge(out_state, 16 * 8)
                for c in range(2):
                    sp.dma_start(ue[:, c, UP:].rearrange("p (b n) -> p b n", b=NB)[:, :, 0:CW - 1],
                                 a["state_conv"][l, :, c]).then_inc(states_in, 16)
                for b in range(NB):
                    for g in range(NPG):
                        at = NBP + b * NBS + g * (PAGE // LB)
                        sp.dma_start(cmpt[:, :, at:at + PAGE // LB, :],
                                     a["cmp_pages"][l, bass.ds(page[b * NPG + g], 1)].rearrange("a p c n -> (a p) c n")
                                     ).then_inc(pages_in, 16)
                sp.dma_start(cmpt[:, :, NBLK, :], a["pe"][l]).then_inc(pages_in, 16)
                load_w(("q", l), a["w_in"][l, 3])
                for c in range(4):
                    load_w((f"cmp{c}", l), a["cmp_w"][l, c])
                load_pair(l, 0)
                load_pair(l, 1)
                sp.dma_start(a["out_past"][l], a["swa_cache"][l, :, TB:PAST, :]).then_inc(out_past, 16)
                for c in range(2):
                    load_w((f"wo{c}", l), a["w_out"][l, c])
                if l == 0:
                    load_w(("ffn", 0), a["ffn_gu"][0])
                load_pair(l, 2)
                load_pair(l, 3)
                sp.wait_ge(av_done, T_L * (l + 1))
                sp.dma_start(poolw, a["pool_w"][l]).then_inc(mixw_in, 16)
                sp.dma_start(pww, a["pw_w"][l]).then_inc(mixw_in, 16)
                if l == 0:
                    for c in range(NFC):
                        if c > 0:
                            load_w(("ffn", c), a["ffn_gu"][c])
                        if c >= 2:
                            sp.wait_ge(z_full, ZI[f"fd{KD - 1}.{c - 2}"] + 1)
                        sp.dma_start(wd[:, c % 2], a["ffn_dn"][c]).then_inc(d_loaded[c % 2], 16)
            sp.wait_ge(out_kv, 16 * 16)
            sp.wait_ge(av_done, T_L * DEPTH)
            sp.dma_start(MC[:, 0:MCON["rb"]], a["mcon"]).then_inc(moe_in, 16)
            sp.dma_start(wrt, a["w_router"]).then_inc(moe_in, 16)
            sp.dma_start(MC[:, MCON["rb"]:MCON["rb"] + NE], a["rb_row"].broadcast_to([P, NE])).then_inc(moe_rb, 16)
            sp.wait_ge(z_full, ZI["o7.1"] + 1)
            for i in range(2):
                sp.dma_start(lnrow[:, i, :], a["ln_rows"][i:i + 1, :].broadcast_to([P, D])).then_inc(lnrow_in, 16)
            sp.wait_ge(task_ready, 1)
            T = sp.value_load(TASK[0:1, 2 * NT:2 * NT + 1], min_val=1, max_val=NT)
            sp.wait_ge(xd_zero, 32)
            sp.wait_ge(z_full, ZI["o7.1"] + 1)

            def load_up(e, c, t):
                k = NWC + c
                slot = WR[k % 3]
                wide = 4096 if c < NEC - 1 else 2048
                src = a["moe_gu"][bass.ds(e, 1), c] if c < NEC - 1 else a["moe_gu_last"][bass.ds(e, 1)]
                if t is not None:
                    sp.wait_ge(e_full, t * NEC + (c + 1))
                sp.dma_start(slot[:, 0:wide], src.rearrange("a p n -> (a p) n")).then_inc(w_loaded[k % 3], 16)

            first = sp.value_load(TASK[0:1, 0:1], min_val=0, max_val=NE - 1)
            load_up(first, 0, None)
            load_up(first, 1, None)
            with sp.Fori(0, T) as t:
                e = sp.value_load(TASK[0:1, bass.ds(t, 1)], min_val=0, max_val=NE - 1)
                e_next = sp.value_load(TASK[0:1, bass.ds(t + 1, 1)], min_val=0, max_val=NE - 1)
                for c in range(NEC):
                    if c + 2 < NEC:
                        load_up(e, c + 2, t)
                    else:
                        load_up(e_next, c + 2 - NEC, t + 1)
                    k = NFC + c
                    sp.wait_ge(e_down, t * NEC + (c + 1))
                    src = a["moe_dn"][bass.ds(e, 1), c] if c < NEC - 1 else a["moe_dn_last"][bass.ds(e, 1)]
                    kk = 2 if c < NEC - 1 else 1
                    sp.dma_start(CA[:, (k % 2) * 2048:(k % 2) * 2048 + kk * D],
                                 src.rearrange("a p n -> (a p) n")).then_inc(d_loaded[k % 2], 16)
            for t in range(5):
                r = P if t < 4 else NS
                sp.wait_ge(fin_ready, t + 1)
                sp.dma_start(a["out_y"][t * P:t * P + r, :], xf[0:r, t % 2, :]).then_inc(out_y[t % 2], 16)
            sp.wait_ge(out_y[0], 16 * 3)
            sp.wait_ge(out_y[1], 16 * 2)
            sp.wait_ge(out_past, 16 * DEPTH)
            sp.wait_ge(out_kv, 16 * 16)
            sp.wait_ge(out_state, 16 * 16)

        @block.gpsimd
        def _(pool):
            done = in_order(pool, pool_own)
            done(nc.gpsimd.memset(MEAN[:, :], 1.0 / D))
            done(nc.gpsimd.memset(MEANC[:, :], 1.0 / (2 * P)), ones_set)
            done(nc.gpsimd.memset(ue[:, :, 0:CW - 1], 0.0))
            done(nc.gpsimd.memset(SM[:, :], 0.0))
            done(nc.gpsimd.memset(QA[:, :], 0.0), qz_zeroed)
            pool.wait_ge(consts_in, 48)
            for l in range(DEPTH):
                pool.wait_ge(states_in, 16 * 5 * (l + 1))
                for c in range(2):
                    pool.wait_ge(z_free["dve"], freed(f"a{c}.{l}"))
                    pool.dma_start(a["out_conv_p"][l, c], ue[:, c, SEQ:UP]).then_inc(out_state, 16)
                    pool.dma_start(a["out_conv_s"][l, c],
                                   ue[:, c, UP:].rearrange("p (b n) -> p b n", b=NB)[:, :, TB:US]).then_inc(out_state, 16)
                    pool.wait_ge(z_free["act"], freed(f"p{c}.{l}"))
                    pool.dma_start(a["out_pool_p"][l, c], ext[:, c, SEQ:EP]).then_inc(out_state, 16)
                    pool.dma_start(a["out_pool_s"][l, c],
                                   ext[:, c, EP:].rearrange("p (b n) -> p b n", b=NB)[:, :, TB:ES]).then_inc(out_state, 16)
            pool.wait_ge(av_done, T_L * DEPTH)
            done(nc.gpsimd.memset(zrow, 0.0), zeros_set)
            pool.dma_start(x_dram[ROWS:ROWS + CH, :], zrow).then_inc(xd_zero, 16)
            pool.dma_start(y_dram[ROWS:ROWS + CH, :], zrow).then_inc(xd_zero, 16)
            pool.wait_ge(slot_ready, 1)
            for t in range(5):
                r = P if t < 4 else NS
                pool.wait_ge(z_free["act"], freed(f"ht{t}"))
                for k in range(2):
                    pool.indirect_dma_start(x_dram[:, :], bass.IndirectOffsetOnAxis(SLOT[0:r, 2 * t + k:2 * t + k + 1], 0),
                                            htok[0:r, t, :], None).then_inc(scattered, 16)
            pool.wait_ge(scattered, 160)
            pool.wait_ge(xd_zero, 32)
            pool.wait_ge(task_ready, 1)
            T = pool.value_load(TASK[0:1, 2 * NT:2 * NT + 1], min_val=1, max_val=NT)
            pool.wait_ge(ln_out, LN_ALL)
            r0 = pool.value_load(TASK[0:1, NT:NT + 1], min_val=0, max_val=ROWS)
            pool.dma_start(xg[:, 0, :], x_dram[bass.ds(r0, CH), :]).then_inc(x_loaded, 16)
            pool.sem_inc(ysb_free, 1)
            with pool.Fori(0, T) as t:
                pool.wait_ge(x_turned, t + 1)
                nxt = pool.value_load(TASK[0:1, bass.ds(t + (NT + 1), 1)], min_val=0, max_val=ROWS)
                pool.dma_start(xg[:, 0, :], x_dram[bass.ds(nxt, CH), :]).then_inc(x_loaded, 16)
                pool.wait_ge(e_yout, t + 2)
                row = pool.value_load(TASK[0:1, bass.ds(t + NT, 1)], min_val=0, max_val=ROWS)
                pool.dma_start(y_dram[bass.ds(row, CH), :], ysb).then_inc(y_stored, 16)
                pool.wait_ge(y_stored, t * 16 + 16)
                pool.sem_inc(ysb_free, 1)
            for t in range(5):
                r = P if t < 4 else NS
                if t >= 2:
                    pool.wait_ge(fin_ready, t - 1)
                for k in range(2):
                    pool.indirect_dma_start(ygat[0:r, t % 2, k, :], None, y_dram[:, :],
                                            bass.IndirectOffsetOnAxis(SLOT[0:r, 2 * t + k:2 * t + k + 1], 0)
                                            ).then_inc(y_gathered[t % 2], 16)

        @block.scalar
        def _(act):
            done = in_order(act, act_own)

            def wait_z(name):
                act.wait_ge(z_full, ZI[name] + 1)

            def free_z(ins):
                done(ins, z_free["act"])

            def norm(lm, lv, src, dst, K, gname, bname, l, func):
                i, before = ln_before[lm]
                for k in range(K):
                    act.wait_ge(ln_centered, before + k + 1)
                    if k >= 2:
                        act.wait_ge(ln_sq_used, before - i + k - 1)
                    done(nc.scalar.activation(sq[:, k % 2, :], src[:, k, :], ACT.Square), ln_squared)
                wait_z(lv)
                free_z(nc.scalar.activation(flat(std), pair(lv), ACT.Sqrt, bias=eps))
                for k in range(K):
                    act.wait_ge(ln_scaled, before + k + 1)
                    if gname is None:
                        g, b = PAR_[:, DEPTH * NPAR + k:DEPTH * NPAR + k + 1], PAR_[:, DEPTH * NPAR + KD + k:DEPTH * NPAR + KD + k + 1]
                    else:
                        g, b = par(gname, l, k), par(bname, l, k)
                    done(nc.scalar.activation(dst[:, k, :], src[:, k, :], func, bias=b, scale=g), ln_out)

            eps = SM[:, 42:43]
            act.wait_ge(qz_zeroed, 1)
            done(nc.scalar.activation(eps, SM[:, 41:42], ACT.Copy, bias=EPS))
            act.wait_ge(consts_in, 48)
            norm("lm", "lv", x, h, KD, None, None, 0, ACT.Identity)
            for l in range(DEPTH):
                for c in range(2):
                    wait_z(f"g{c}.{l}")
                    free_z(nc.scalar.activation(flat(sig[:, c, :]), pair(f"g{c}.{l}"), ACT.Sigmoid, bias=par("bin", l, c)))
                for n, name in enumerate(("wk", "wv")):
                    wait_z(f"{name}.{l}")
                    if l == 1 and n == 0:
                        act.wait_ge(out_kv, 16 * 8)
                    free_z(nc.scalar.activation(flat(kvz[:, n, :]), pair(f"{name}.{l}"), ACT.Identity, bias=par("bin", l, 4 + n)))
                    act.dma_start(a["out_kv"][l, 4 + n], kvz[:, n, :]).then_inc(out_kv, 16)
                for c in range(2):
                    wait_z(f"p{c}.{l}")
                    for ps, lo, hi in pieces(f"p{c}.{l}"):
                        if hi <= SEQ:
                            done(nc.scalar.activation(ext[:, c, PW - 1 + lo:PW - 1 + hi], ps, ACT.Identity, bias=par("bin", l, 6 + c)))
                        else:
                            free_z(nc.scalar.activation(
                                ext[:, c, EP:].rearrange("p (b n) -> p b n", b=NB)[:, :, PW - 1:],
                                ps.rearrange("p (b n) -> p b n", b=NB), ACT.Identity, bias=par("bin", l, 6 + c)))
                for c, name in enumerate(("ck", "cv")):
                    wait_z(f"{name}.{l}")
                    if c == 0:
                        act.wait_ge(ln_out, ln_done("lm" if l == 0 else "lm2"))
                    for ps, lo, hi in pieces(f"{name}.{l}"):
                        dst = PA[:, c * (NBLK + 1) * LB + lo:c * (NBLK + 1) * LB + hi] if hi <= SEQ else kcs[:, c, :]
                        ins = nc.scalar.activation(dst, ps, ACT.Identity, bias=par("bin", l, 8 + c))
                        (done if hi <= SEQ else free_z)(ins)
                    act.dma_start(a["out_kv"][l, c, :, 0:SEQ], PA[:, c * (NBLK + 1) * LB:c * (NBLK + 1) * LB + SEQ]).then_inc(out_kv, 16)
                    act.dma_start(a["out_kv"][l, c, :, SEQ:TOK], kcs[:, c, :]).then_inc(out_kv, 16)
                for n, name in enumerate(("sk", "sv")):
                    wait_z(f"{name}.{l}")
                    free_z(nc.scalar.activation(flat(kvz[:, 2 + n, :]), pair(f"{name}.{l}"), ACT.Identity, bias=par("bin", l, 10 + n)))
                    act.dma_start(a["out_kv"][l, 2 + n], kvz[:, 2 + n, :]).then_inc(out_kv, 16)
                wait_z(f"gate.{l}")
                free_z(nc.scalar.activation(flat(gT), pair(f"gate.{l}", 24), ACT.Sigmoid, bias=par("bin", l, 16, 24)))
                for a_ in range(NPAIR):
                    src = gT[:, SEQ + 2 * TB * a_:SEQ + 2 * TB * (a_ + 1)].rearrange("p (b n) -> p b n", b=2)
                    ins = nc.scalar.activation(gx[:, a_ * P:(a_ + 1) * P].rearrange("p (b h n) -> p b h n", b=2, h=NH),
                                               src.unsqueeze(2).to_broadcast([24, 2, NH, TB]), ACT.Copy)
                    if a_ == NPAIR - 1:
                        done(ins, gate_spread)
                    else:
                        done(ins)
                for t in range(5):
                    r = P if t < 4 else NS
                    wait_z(f"vt{t}.{l}")
                    free_z(nc.scalar.activation(vg[0:r, t, :], PS[0:r, z_pair(f"vt{t}.{l}"), 0:280], ACT.Copy))
                wait_z(f"vct.{l}")
                free_z(nc.scalar.activation(VC[:, :], PS[0:NBLK, z_pair(f"vct.{l}"), 0:P], ACT.Copy))
                for m in range(KD):
                    done(nc.scalar.activation(h[:, m, :], h[:, m, :], ACT.Identity, bias=par("bo", l, m), scale=ALPHA), h_scaled)

                tt, pm = [l * T_L], [0]

                def turned(copies):
                    n = tt[0]
                    act.wait_ge(t_full, n + 1)
                    if n - l * T_L >= 3:
                        act.wait_ge(av_done, n - 2)
                    for i, (dst, src) in enumerate(copies(n)):
                        ins = nc.scalar.activation(dst, src, ACT.Copy)
                        if i == len(copies(n)) - 1:
                            done(ins, t_out)
                        else:
                            done(ins)
                    tt[0] += 1

                def exps(u, kind):
                    act.wait_ge(p_max, l * U_L + u + 1)
                    s, pc = u % 3, pcmp[u // 2 % 2]
                    if kind == "prompt":
                        i, g, w = units[u]
                        if w == 0:
                            done(nc.scalar.activation(pc[:, 0:GRP * NBP], pc[:, 0:GRP * NBP], ACT.Exp))
                        for j in range(GRP):
                            ins = nc.scalar.activation(pr[s][:, j, 0:(i + 1) * P], pr[s][:, j, 0:(i + 1) * P], ACT.Exp,
                                                       bias=less(s, j), accum_out=total(s, j))
                            if j == GRP - 1:
                                done(ins, p_exp)
                            else:
                                done(ins)
                    else:
                        if kind == 0:
                            done(nc.scalar.activation(pc[:, 0:NBLK], pc[:, 0:NBLK], ACT.Exp, bias=less(s, 4), accum_out=total(s, 4)))
                        done(nc.scalar.activation(pr[s][:, 0, 0:PAST + NS], pr[s][:, 0, 0:PAST + NS], ACT.Exp,
                                                  bias=less(s, 0), accum_out=total(s, 0)), p_exp)

                def outs(u, kind):
                    if kind == "prompt":
                        i, g, w = units[u]
                        if w == 0:
                            turned(lambda n: [(ptr[0:NBP, n % 3, :], PS[0:NBP, 4 + n % 2, :])])
                        for k in range(i + 1):
                            turned(lambda n: [(ptr[:, n % 3, :], PS[:, 4 + n % 2, :])])
                    else:
                        c = lambda n: [(ptr[:, n % 3, 0:256], PS[:, 4 + n % 2, 0:256]),
                                       (ptr[0:NS, n % 3, 256:384], PS[0:NS, 4 + n % 2, 256:384])] + (
                            [(ptr[0:NBLK, n % 3, 384:512], PS[0:NBLK, 4 + n % 2, 384:512])] if kind == 0 else [])
                        turned(c)

                kinds = ["prompt"] * NU + [0, 1] * NPAIR
                for u in range(U_L + 2):
                    if u >= 2:
                        outs(u - 2, kinds[u - 2])
                    if u < U_L:
                        exps(u, kinds[u])
                for c in range(2):
                    wait_z(f"pm{c}.{l}")
                    free_z(nc.scalar.activation(flat(yt[:, 6 + c, :]), pair(f"pm{c}.{l}"), ACT.Identity, scale=par("psc", l, c)))
                norm(f"cm.{l}", f"cvar.{l}", conv, conv, 2, "clg", "clb", l, ACT.Silu)
                for c in range(2):
                    wait_z(f"pw{c}.{l}")
                    free_z(nc.scalar.activation(flat(yt[:, c, :]), pair(f"pw{c}.{l}"), ACT.Identity, bias=par("pwb", l, c)))
                norm(f"lm1.{l}", f"lv1.{l}", h, h, KD, "g1", "b1", l, ACT.Identity)
                if l == 0:
                    for c in range(NFC):
                        for m in range(2):
                            wait_z(f"fg{m}.{c}")
                            if 2 * c + m >= 1:
                                act.wait_ge(z_free["dve"], freed(f"fu{1 - m}.{c - 1 + m}"))
                            free_z(nc.scalar.activation(flat(silu), pair(f"fg{m}.{c}"), ACT.Silu))
                    norm("lm2", "lv2", x, h, KD, "g2", "b2", 0, ACT.Identity)
            for t in range(5):
                r = P if t < 4 else NS
                wait_z(f"ht{t}")
                b = z_pair(f"ht{t}")
                free_z(nc.scalar.activation(htok[0:r, t, :].rearrange("p (a n) -> p a n", a=2), PS[0:r, b:b + 2, :], ACT.Copy))
            act.wait_ge(route_masks, 1)
            done(nc.scalar.activation(RT[:, 360:365], RT[:, 365:370], ACT.Exp), gate_exp)
            act.wait_ge(task_ready, 1)
            T = act.value_load(TASK[0:1, 2 * NT:2 * NT + 1], min_val=1, max_val=NT)
            with act.Fori(0, T) as t:
                loop = in_order(act, act_loop)
                act.wait_ge(x_turned, t + 1)
                loop(nc.scalar.activation(xgT.rearrange("p (a k) n -> p a (k n)", a=2), PS[:, 0:2, :], ACT.Copy), xT_ready, t)

                def turn_out(c):
                    k = 2 if c < NEC - 1 else 1
                    act.wait_ge(eT_full, t * NEC + (c + 1))
                    act.wait_ge(e_down, t * NEC + (c + 1))
                    loop(nc.scalar.activation(ehT[:, c % 2, 0:k, :],
                                                     PS[:, 4 + c % 2, 0:k * P].rearrange("p (k n) -> p k n", k=k), ACT.Copy), eT_ready, t * NEC)

                for c in range(NEC):
                    w = 256 if c < NEC - 1 else P
                    act.wait_ge(e_full, t * NEC + (c + 4))
                    if c >= 2:
                        act.wait_ge(e_hid, t * NEC + (c - 1))
                    loop(nc.scalar.activation(esil[:, c % 2, 0:w], PS[:, 2 + c % 2, 0:w], ACT.Silu), e_silu, t * NEC)
                    if c > 0:
                        turn_out(c - 1)
                turn_out(NEC - 1)
            for t in range(5):
                r = P if t < 4 else NS
                act.wait_ge(var_ready, t + 1)
                done(nc.scalar.activation(RT[0:r, 915:916], RT[0:r, 914:915], ACT.Sqrt), dev_ready)

        @block.vector
        def _(dve):
            done = in_order(dve, dve_own)
            V = nc.vector

            def wait_z(name):
                dve.wait_ge(z_full, ZI[name] + 1)

            def free_z(ins):
                done(ins, z_free["dve"])

            def norm(lm, lv, src, K):
                wait_z(lm)
                for k in range(K):
                    done(V.tensor_tensor(flat(src[:, k, :]), flat(src[:, k, :]), pair(lm), ALU.subtract), ln_centered)
                dve.wait_ge(z_free["act"], freed(lv))
                done(V.reciprocal(std, std))
                for k in range(K):
                    done(V.tensor_tensor(src[:, k, :], src[:, k, :], std, ALU.mult), ln_scaled)

            def samples(ap):
                return ap.rearrange("p (b n) -> p b n", b=NB)

            dve.wait_ge(x_in, 16)
            dve.wait_ge(consts_in, 48)
            norm("lm", "lv", x, KD)
            for l in range(DEPTH):
                if l == 1:
                    dve.wait_ge(out_state, 16 * 8)
                for c in range(2):
                    dve.wait_ge(z_free["act"], freed(f"g{c}.{l}"))
                    wait_z(f"a{c}.{l}")
                    for ps, lo, hi in pieces(f"a{c}.{l}"):
                        if hi <= SEQ:
                            done(V.scalar_tensor_tensor(out=ue[:, c, CW - 1 + lo:CW - 1 + hi], in0=ps, scalar=par("bin", l, 2 + c),
                                                             in1=sig[:, c, lo:hi], op0=ALU.add, op1=ALU.mult))
                        else:
                            free_z(V.scalar_tensor_tensor(out=samples(ue[:, c, UP:])[:, :, CW - 1:], in0=samples(ps),
                                                          scalar=par("bin", l, 2 + c), in1=samples(sig[:, c, lo:hi]),
                                                          op0=ALU.add, op1=ALU.mult))
                dve.wait_ge(states_in, 16 * 5 * (l + 1))
                for c in range(2):
                    views = [(conv[:, c, 0:SEQ], lambda k: ue[:, c, k:k + SEQ]),
                             (samples(conv[:, c, SEQ:TOK]), lambda k: samples(ue[:, c, UP:])[:, :, k:k + TB])]
                    for out_, src in views:
                        done(V.tensor_scalar(out_, src(0), par("cw", l, c * CW), par("cb", l, c), ALU.mult, ALU.add))
                    for k in range(1, CW):
                        for i, (out_, src) in enumerate(views):
                            ins = V.scalar_tensor_tensor(out=out_, in0=src(k), scalar=par("cw", l, c * CW + k), in1=out_,
                                                         op0=ALU.mult, op1=ALU.add)
                            (done(ins, conv_done) if k == CW - 1 and i == 1 else done(ins))
                dve.wait_ge(ln_out, ln_done("lm" if l == 0 else "lm2"))
                done(V.memset(ext[:, :, 0:PW - 1], 0.0))
                dve.wait_ge(states_in, 16 * 5 * (l + 1))
                dve.wait_ge(z_free["act"], freed(f"p1.{l}"))
                done(V.tensor_copy(win_a[:, :, 0:1], ext[:, :, 0:1]))
                done(V.tensor_tensor(win_a[:, :, 1:], ext[:, :, 1:], ext[:, :, 0:EXT - 1], ALU.add))
                done(V.tensor_copy(win_b[:, :, 0:2], win_a[:, :, 0:2]))
                done(V.tensor_tensor(win_b[:, :, 2:], win_a[:, :, 2:], win_a[:, :, 0:EXT - 2], ALU.add))
                done(V.tensor_copy(win_a[:, 1, 0:4], win_b[:, 1, 0:4]))
                done(V.tensor_tensor(win_a[:, 1, 4:], win_b[:, 1, 4:], win_b[:, 1, 0:EXT - 4], ALU.add))
                done(V.tensor_tensor(win_b[64:P, 1, 8:], win_a[64:P, 1, 8:], win_a[64:P, 1, 0:EXT - 8], ALU.add))
                done(V.tensor_copy(win_b[0:64, :, :], win_a[0:64, :, :]))
                for c in range(2):
                    inv = CON_[:, CON["invw"] + c:CON["invw"] + c + 1]
                    done(V.scalar_tensor_tensor(out=pooled[:, c, 0:SEQ], in0=win_b[:, c, PW - 1:EP], scalar=inv,
                                                     in1=ext[:, c, PW - 1:EP], op0=ALU.mult, op1=ALU.subtract))
                    done(V.scalar_tensor_tensor(out=samples(pooled[:, c, SEQ:]), in0=samples(win_b[:, c, EP:])[:, :, PW - 1:],
                                                     scalar=inv, in1=samples(ext[:, c, EP:])[:, :, PW - 1:],
                                                     op0=ALU.mult, op1=ALU.subtract))
                first = pooled[:, :, 0:PW]
                invt = CON_[:, CON["invt"]:CON["invt"] + 2 * PW].rearrange("p (c n) -> p c n", c=2)
                done(V.tensor_tensor(first, win_b[:, :, PW - 1:2 * PW - 1], invt, ALU.mult))
                done(V.tensor_tensor(first, first, ext[:, :, PW - 1:2 * PW - 1], ALU.subtract), pooled_ready)
                for j in range(GRP):
                    name = f"q{j}.{l}"
                    wait_z(name)
                    for g in range(NKV):
                        rows = slice(HD * g, HD * g + HD)
                        b = PAR_[rows, l * NPAR + PAR["bin"] + 12 + j:l * NPAR + PAR["bin"] + 13 + j]
                        for ps, lo, hi in pieces(name, rows):
                            if hi <= SEQ:
                                done(V.tensor_scalar(qz[rows, g, j, lo:hi], ps, b, HD ** -0.5, ALU.add, ALU.mult))
                            else:
                                for b2 in range(2):
                                    at = b2 * HD + g * 32 + j * TB
                                    ins = V.tensor_scalar(qs[rows, :, b2, at:at + TB],
                                                          ps.rearrange("p (a b n) -> p a b n", a=NPAIR, b=2)[:, :, b2, :],
                                                          b, HD ** -0.5, ALU.add, ALU.mult)
                                    (free_z if g == 1 and b2 == 1 else done)(ins)
                for c in range(2):
                    wait_z(f"cmp{c}.{l}")
                    bk = z_pair(f"cmp{c}.{l}")
                    done(V.tensor_copy(SM[:, 40:41], PS[:, bk, NBLK:NBLK + 1]))
                    free_z(V.tensor_scalar(cct[:, c, :], PS[:, bk, 0:NBLK], SM[:, 40:41], None, ALU.add))
                wait_z(f"gs.{l}")
                gs = SM[:, 48:60].rearrange("p (a w) -> p a w", a=NPAIR)
                gsel = YT[:, 4 * EXT:4 * EXT + 96].rearrange("p (a h w) -> p a h w", a=NPAIR, h=NH)
                hmask = CON_[:, CON["hmask"]:CON["hmask"] + NH]
                done(V.tensor_tensor(gsel.rearrange("p a h w -> p a w h"),
                                          PS[:, z_pair(f"gs.{l}"), 0:96].rearrange("p (a h w) -> p a w h", a=NPAIR, h=NH),
                                          hmask.unsqueeze(1).unsqueeze(1).to_broadcast([P, NPAIR, 3, NH]), ALU.mult))
                free_z(V.tensor_reduce(gs, gsel.rearrange("p a h w -> p a w h"), AX.X, ALU.add))

                entry, group = [l * S_L], [0]
                dve.wait_ge(out_kv, 16 * 8 * (l + 1))

                def score():
                    e = entry[0]
                    dve.wait_ge(s_full, e + 1)
                    entry[0] += 1
                    return PS[:, e % 4, :]

                mx = SM[:, 44:48]

                def maxes(u):
                    s, pc = u % 3, pcmp[u // 2 % 2]
                    if u >= 3:
                        dve.wait_ge(t_full, l * T_L + tiles_through(u - 3))
                    if u < NU:
                        i, g, w = units[u]
                        n = (i + 1) * P
                        if w == 0:
                            ps = score()
                            pc3 = pc[:, 0:GRP * NBP].rearrange("p (j n) -> p j n", j=GRP)
                            done(V.tensor_tensor(pc[:, 0:GRP * NBP], ps[:, 0:GRP * NBP], cbias[:, i, g, :], ALU.add), s_read)
                            done(V.tensor_reduce(mx, pc3, AX.X, ALU.max))
                            done(V.tensor_scalar(mx, mx, FLOOR, None, ALU.max))
                            done(V.tensor_tensor(pc3, pc3, mx.unsqueeze(2).to_broadcast([P, GRP, NBP]), ALU.subtract))
                        for j in range(GRP):
                            ps = score()
                            done(V.tensor_tensor_reduce(out=pr[s][:, j, 0:n], in0=bias[:, g * GRP + j, SEQ - n:SEQ], in1=ps[:, 0:n],
                                                               scale=1.0, scalar=FLOOR, op0=ALU.add, op1=ALU.max,
                                                               accum_out=mx[:, j:j + 1]), s_read)
                        done(V.tensor_scalar(less(s, 0, GRP), mx, -1.0, None, ALU.mult), p_max)
                    else:
                        a_, w = divmod(u - NU, 2)
                        if w == 0:
                            ps = score()
                            done(V.tensor_tensor_reduce(
                                out=pc[:, 0:NBLK], in0=CON_[:, CON["scmp"] + a_ * NBLK:CON["scmp"] + (a_ + 1) * NBLK], in1=ps[:, 0:NBLK],
                                scale=1.0, scalar=FLOOR, op0=ALU.add, op1=ALU.max, accum_out=mx[:, 0:1]), s_read)
                            done(V.tensor_scalar(less(s, 4), mx[:, 0:1], -1.0, None, ALU.mult))
                        ps = score()
                        done(V.tensor_tensor_reduce(
                            out=pr[s][:, 0, 0:PAST], in0=CON_[:, CON["spast"]:CON["spast"] + PAST], in1=ps[:, 0:PAST],
                            scale=1.0, scalar=FLOOR, op0=ALU.add, op1=ALU.max, accum_out=mx[:, 0:1]))
                        done(V.tensor_tensor_reduce(
                            out=pr[s][:, 0, PAST:PAST + NS], in0=CON_[:, CON["snew"] + a_ * NS:CON["snew"] + (a_ + 1) * NS],
                            in1=ps[:, PAST:PAST + NS], scale=1.0, scalar=FLOOR, op0=ALU.add, op1=ALU.max, accum_out=mx[:, 1:2]), s_read)
                        done(V.tensor_tensor(mx[:, 0:1], mx[:, 0:1], mx[:, 1:2], ALU.max))
                        done(V.tensor_scalar(less(s, 0), mx[:, 0:1], -1.0, None, ALU.mult), p_max)

                rs, rc = SM[:, 32:36], SM[:, 36:40]

                def factors(sums, gate, n):
                    done(V.tensor_scalar(rs[:, 0:n], sums, TINY, None, ALU.max))
                    done(V.reciprocal(rc[:, 0:n], rs[:, 0:n]))
                    done(V.tensor_tensor(rc[:, 0:n], rc[:, 0:n], gate, ALU.mult))

                def ready(u):
                    s, pc = u % 3, pcmp[u // 2 % 2]
                    dve.wait_ge(p_exp, l * U_L + u + 1)
                    if u < NU:
                        i, g, w = units[u]
                        n = (i + 1) * P
                        gates = vg[:, i, 256 + 12 * g:268 + 12 * g].rearrange("p (j w) -> p j w", w=3)
                        if w == 0:
                            pc3 = pc[:, 0:GRP * NBP].rearrange("p (j n) -> p j n", j=GRP)
                            done(V.tensor_reduce(mx, pc3, AX.X, ALU.add))
                            factors(mx, gates[:, :, 0], GRP)
                            done(V.tensor_tensor(pc3, pc3, rc.unsqueeze(2).to_broadcast([P, GRP, NBP]), ALU.mult))
                        factors(total(s, 0, GRP), gates[:, :, 1 + w], GRP)
                        for j in range(GRP):
                            ins = V.tensor_scalar(pr[s][:, j, 0:n], pr[s][:, j, 0:n], rc[:, j:j + 1], None, ALU.mult)
                            if j == GRP - 1:
                                done(ins, p_ready)
                            else:
                                done(ins)
                    else:
                        a_, w = divmod(u - NU, 2)
                        if w == 0:
                            factors(total(s, 4), gs[:, a_, 0:1], 1)
                            done(V.tensor_scalar(pc[:, 0:NBLK], pc[:, 0:NBLK], rc[:, 0:1], None, ALU.mult))
                        factors(total(s, 0), gs[:, a_, 1 + w:2 + w], 1)
                        done(V.tensor_scalar(pr[s][:, 0, 0:PAST + NS], pr[s][:, 0, 0:PAST + NS], rc[:, 0:1], None, ALU.mult), p_ready)

                def out(u):
                    o = group[0] + l * O_L
                    dve.wait_ge(av_done, l * T_L + tiles_through(u))
                    ps = PS[:, 6 + o % 2, :]
                    if u < NU:
                        i, g, _ = units[u]
                        rows = slice(HD * g, HD * g + HD)
                        done(V.tensor_copy(yt[rows, 2:6, i * P:(i + 1) * P], ps[rows, :].rearrange("p (j n) -> p j n", j=GRP)), o_out)
                    else:
                        a_ = (u - NU) // 2
                        for g in range(NKV):
                            rows = slice(HD * g, HD * g + HD)
                            ins = V.tensor_copy(
                                yt[rows, 2:6, SEQ + 2 * TB * a_:SEQ + 2 * TB * (a_ + 1)].rearrange("p j (b n) -> p j b n", b=2),
                                ps[rows, 0:P].rearrange("p (b g j n) -> p g j b n", b=2, g=NKV, j=GRP)[:, g])
                            if g == 1:
                                done(ins, o_out)
                            else:
                                done(ins)
                    group[0] += 1

                dve.wait_ge(out_state, 16 * 8 * (l + 1))
                for u in range(U_L + 2):
                    if u < U_L:
                        maxes(u)
                    if 1 <= u <= U_L:
                        ready(u - 1)
                    if u >= 3 and u % 2 == 0:
                        out(u - 3)
                out(U_L - 1)
                assert entry[0] == (l + 1) * S_L
                norm(f"cm.{l}", f"cvar.{l}", conv, 2)
                dve.wait_ge(h_scaled, KD * (l + 1))
                for m in range(KD):
                    wait_z(f"o{m}.{l}")
                    free_z(V.tensor_tensor(flat(h[:, m, :]), flat(h[:, m, :]), pair(f"o{m}.{l}"), ALU.add))
                norm(f"lm1.{l}", f"lv1.{l}", h, KD)
                if l == 0:
                    dve.wait_ge(out_state, 16 * 8)
                    for c in range(NFC + 1):
                        if c < NFC:
                            for m in range(2):
                                dve.wait_ge(z_free["act"], freed(f"fg{m}.{c}"))
                                wait_z(f"fu{m}.{c}")
                                if c >= 2:
                                    wait_z(f"fd{KD - 1}.{c - 2}")
                                free_z(V.tensor_tensor(flat(hid[:, c % 2, m, :]), flat(silu), pair(f"fu{m}.{c}"), ALU.mult))
                        if c > 0:
                            for m in range(KD):
                                wait_z(f"fd{m}.{c - 1}")
                                if c == 1:
                                    dve.wait_ge(ln_out, ln_done("lm1.0"))
                                    free_z(V.scalar_tensor_tensor(out=flat(x[:, m, :]), in0=flat(h[:, m, :]), scalar=ALPHA,
                                                                  in1=pair(f"fd{m}.{c - 1}"), op0=ALU.mult, op1=ALU.add))
                                else:
                                    free_z(V.tensor_tensor(flat(x[:, m, :]), flat(x[:, m, :]), pair(f"fd{m}.{c - 1}"), ALU.add))
                    norm("lm2", "lv2", x, KD)

            dve.wait_ge(moe_in, 32)
            mc = lambda name: MC[:, MCON[name]:MCON[name] + NE]
            cols = lambda i: RT[:, 40 * i:40 * i + 40].rearrange("p (t e) -> p t e", e=NE)
            each = lambda i: RT[:, 320 + 5 * i:325 + 5 * i]
            wide = lambda ap: ap.unsqueeze(2).to_broadcast([P, 5, NE])
            rev = mc("rev").unsqueeze(1).to_broadcast([P, 5, NE])
            lg, a1, a2, tmp, rank, off = (cols(i) for i in range(6))
            m1, m2, r1, ex, g1, g2, nd = each(0), each(1), each(2), each(8), each(3), each(4), each(9)
            dve.wait_ge(moe_rb, 16)
            done(V.memset(RT[:, :], 0.0))
            wait_z("rt")
            bk = z_pair("rt")
            done(V.tensor_tensor(lg[:, 0:4, :], PS[:, bk, 0:32].rearrange("p (t e) -> p t e", e=NE),
                                      mc("rb").unsqueeze(1).to_broadcast([P, 4, NE]), ALU.add))
            free_z(V.tensor_tensor(lg[0:NS, 4, :], PS[0:NS, bk, 32:40], MC[0:NS, MCON["rb"]:MCON["rb"] + NE], ALU.add))
            for a_, m in ((a1, m1), (a2, m2)):
                done(V.tensor_reduce(m, lg, AX.X, ALU.max))
                done(V.tensor_tensor(tmp, lg, wide(m), ALU.is_equal))
                done(V.tensor_tensor(tmp, tmp, rev, ALU.mult))
                done(V.tensor_reduce(r1, tmp, AX.X, ALU.max))
                done(V.tensor_tensor(a_, tmp, wide(r1), ALU.is_equal))
                if a_ is a1:
                    done(V.scalar_tensor_tensor(out=lg, in0=a1, scalar=-BIG, in1=lg, op0=ALU.mult, op1=ALU.add))
            done(V.memset(RT[NS:P, 72:80], 0.0))
            done(V.memset(RT[NS:P, 112:120], 0.0))
            done(V.tensor_tensor(nd, m2, m1, ALU.subtract))
            done(V.tensor_tensor(tmp, a1, a2, ALU.add), route_masks)
            dve.wait_ge(gate_exp, 1)
            done(V.tensor_scalar(g2, ex, 1.0, None, ALU.add))
            done(V.reciprocal(g1, g2))
            done(V.tensor_tensor(g2, g1, ex, ALU.mult))
            wait_z("rk")
            bk = z_pair("rk")
            done(V.tensor_copy(RT[:, 160:192], PS[:, bk, 0:32]))
            done(V.tensor_copy(RT[0:NS, 192:200], PS[0:NS, bk, 32:40]))
            cnt = RT[:, 400:408]
            free_z(V.tensor_copy(cnt, PS[:, bk, 40:48]))

            def before(dst, src, at):
                s0, s1 = RT[:, at:at + 12], RT[:, at + 12:at + 24]
                done(V.tensor_copy(s0[:, 5:12], src[:, 0:7]))
                done(V.tensor_tensor(s1[:, 4:12], s0[:, 4:12], s0[:, 3:11], ALU.add))
                done(V.tensor_tensor(s0[:, 4:12], s1[:, 4:12], s1[:, 2:10], ALU.add))
                done(V.tensor_tensor(dst, s0[:, 4:12], s0[:, 0:8], ALU.add))

            offs = RT[:, 408:416]
            before(offs, cnt, 420)
            done(V.tensor_tensor(rank, rank, offs.unsqueeze(1).to_broadcast([P, 5, NE]), ALU.add))
            for k, a_ in enumerate((a1, a2)):
                done(V.tensor_tensor(tmp, a_, rank, ALU.mult))
                done(V.tensor_reduce(r1, tmp, AX.X, ALU.add))
                ins = V.tensor_copy(SLOT[:, :].rearrange("p (t k) -> p t k", k=2)[:, :, k], r1)
                (done(ins, slot_ready) if k else done(ins))
            nch, cb, ce, hit = RT[:, 450:458], RT[:, 458:466], RT[:, 466:474], RT[:, 474:482]
            done(V.tensor_scalar(nch, cnt, 0.0, None, ALU.is_gt))
            for m in range(1, -(-TOK // CH)):
                done(V.tensor_scalar(hit, cnt, float(m * CH), None, ALU.is_gt))
                done(V.tensor_tensor(nch, nch, hit, ALU.add))
            before(cb, nch, 490)
            done(V.tensor_tensor(ce, cb, nch, ALU.add))
            tb = lambda i: RT[0:1, 520 + NT * NE * i:520 + NT * NE * (i + 1)].rearrange("p (t e) -> p t e", e=NE)
            over = lambda ap: ap[0:1, :].unsqueeze(1).to_broadcast([1, NT, NE])
            tk = MC[0:1, MCON["task"]:MCON["task"] + NE * NT].rearrange("p (t e) -> p t e", e=NE)
            ind, sel = tb(0), tb(1)
            done(V.tensor_tensor(ind, tk, over(cb), ALU.is_ge))
            done(V.tensor_tensor(sel, tk, over(ce), ALU.is_lt))
            done(V.tensor_tensor(ind, ind, sel, ALU.mult))
            done(V.tensor_tensor(sel, ind, over(mc("iota")), ALU.mult))
            num = RT[0:1, 800:800 + 2 * NT + 1]
            done(V.tensor_reduce(num[:, 0:NT], sel, AX.X, ALU.add))
            done(V.tensor_tensor(sel, tk, over(cb), ALU.subtract))
            done(V.scalar_tensor_tensor(out=sel, in0=sel, scalar=float(CH), in1=over(offs), op0=ALU.mult, op1=ALU.add))
            done(V.tensor_tensor(sel, sel, ind, ALU.mult))
            done(V.tensor_reduce(num[:, NT:2 * NT], sel, AX.X, ALU.add))
            done(V.tensor_copy(num[:, 2 * NT:2 * NT + 1], ce[0:1, NE - 1:NE]))
            done(V.tensor_copy(TASK[:, :], num), task_ready)
            T = dve.value_load(TASK[0:1, 2 * NT:2 * NT + 1], min_val=1, max_val=NT)
            dve.sem_inc(e_yout, 1)
            with dve.Fori(0, T) as t:
                loop = in_order(dve, dve_loop)
                for c in range(NEC):
                    n = 256 if c < NEC - 1 else P
                    dve.wait_ge(e_silu, t * NEC + (c + 1))
                    if c >= 2:
                        dve.wait_ge(eT_full, t * NEC + (c - 1))
                    loop(V.tensor_tensor(ehid[:, c % 2, 0:n], esil[:, c % 2, 0:n], PS[:, 2 + c % 2, n:2 * n], ALU.mult), e_hid, t * NEC)
                dve.wait_ge(e_down, t * NEC + (NEC + 2))
                dve.wait_ge(ysb_free, t + 1)
                loop(V.tensor_copy(ysb.rearrange("p (a n) -> p a n", a=2), PS[:, 6:8, :]), e_yout, t + 1)

            dve.wait_ge(lnrow_in, 32)
            st, ag = RT[:, 900:912], RT[:, 912:916]
            for t in range(5):
                r = P if t < 4 else NS
                s = t % 2
                if t >= 2:
                    dve.wait_ge(out_y[s], 16 * (t // 2))
                y = xf[0:r, s, :]
                done(V.tensor_scalar(y, htok[0:r, t, :], ALPHA, None, ALU.mult))
                dve.wait_ge(y_gathered[s], 32 * (t // 2 + 1))
                for k, g in enumerate((g1, g2)):
                    done(V.scalar_tensor_tensor(out=y, in0=ygat[0:r, s, k, :], scalar=g[0:r, t:t + 1], in1=y,
                                                     op0=ALU.mult, op1=ALU.add))
                for k in range(2):
                    done(V.bn_stats(st[0:r, 6 * k:6 * k + 6], y[:, 512 * k:512 * k + 512]))
                done(V.bn_aggr(ag[0:r, 0:2], st[0:r, :]))
                done(V.tensor_scalar(ag[0:r, 2:3], ag[0:r, 1:2], EPS, None, ALU.add), var_ready)
                dve.wait_ge(dev_ready, t + 1)
                done(V.reciprocal(ag[0:r, 3:4], ag[0:r, 3:4]))
                done(V.tensor_scalar(y, y, ag[0:r, 0:1], ag[0:r, 3:4], ALU.subtract, ALU.mult))
                done(V.tensor_tensor(y, y, lnrow[0:r, 0, :], ALU.mult))
                done(V.tensor_tensor(y, y, lnrow[0:r, 1, :], ALU.add), fin_ready)

        @block.tensor
        def _(pe):
            M = nc.tensor.matmul

            def take(name):
                n = ZI[name]
                if n >= 4:
                    prev, owner = sched[n - 4]
                    pe.wait_ge(z_free[owner], freed(prev))
                return z_pair(name)

            def full(ins):
                ins.then_inc(z_full, 1)

            def halves():
                return [(0, slice(0, HALF)), (1, slice(HALF, TOK))]

            def product(name, steps, rows=P):
                b = take(name)
                for i, (w, act_) in enumerate(steps):
                    for n, cols in halves():
                        last = M(PS[0:rows, b + n, 0:HALF], w, act_[:, cols], start=(i == 0), stop=(i == len(steps) - 1))
                full(last)

            def norm(lm, lv, src, K, mean):
                i, before = ln_before[lm]
                product(lm, [(mean[:, :], src[:, k, :]) for k in range(K)])
                b = take(lv)
                for k in range(K):
                    pe.wait_ge(ln_squared, before + k + 1)
                    for n, cols in halves():
                        last = M(PS[:, b + n, 0:HALF], mean[:, :], sq[:, k % 2, cols], start=(k == 0), stop=(k == K - 1))
                    if k < K - 1:
                        last.then_inc(ln_sq_used, 1)
                full(last)

            def weights(key):
                c = chunk_of[key]
                pe.wait_ge(w_loaded[c % 3], 16 * (c // 3 + 1))
                return WR[c % 3][:, :].rearrange("p (k n) -> p k n", k=KD)

            pe.wait_ge(x_in, 16)
            pe.wait_ge(ones_set, 1)
            norm("lm", "lv", x, KD, MEAN)
            for l in range(DEPTH):
                pe.wait_ge(ln_out, ln_done("lm" if l == 0 else "lm2"))
                for key, names in (("glu", TILES[0:4]), ("kwp", TILES[4:8]), ("kcks", TILES[8:12]), ("q", TILES[12:16])):
                    w = weights((key, l))
                    for i, name in enumerate(names):
                        product(f"{name}.{l}", [(w[:, k, i * P:(i + 1) * P], h[:, k, :]) for k in range(KD)])
                pe.wait_ge(states_in, 16 * 5 * (l + 1))
                product(f"gate.{l}", [(wgate[:, k, :], h[:, k, :]) for k in range(KD)], rows=24)
                pe.wait_ge(z_free["act"], freed(f"gate.{l}"))
                for t in range(5):
                    r = P if t < 4 else NS
                    b = take(f"vt{t}.{l}")
                    cols = slice(t * P, t * P + r)
                    nc.tensor.transpose(PS[0:r, b, 0:P], kvz[:, 3, cols], ident)
                    nc.tensor.transpose(PS[0:r, b, P:2 * P], kvz[:, 1, cols], ident)
                    full(nc.tensor.transpose(PS[0:r, b, 256:280], gT[:, cols], ident[0:24, 0:24]))
                pe.wait_ge(pages_in, 16 * (NB * NPG + 1) * (l + 1))
                for c in range(2):
                    b = take(f"cmp{c}.{l}")
                    for n in range(2):
                        ch = chunk_of[f"cmp{2 * c + n}", l]
                        pe.wait_ge(w_loaded[ch % 3], 16 * (ch // 3 + 1))
                        w = WR[ch % 3][:, :].rearrange("p (l n) -> p l n", n=P)
                        for i in range(LB // 2):
                            at = n * (LB // 2) + i
                            last = M(PS[:, b, 0:NBLK + 1], w[:, i, :], cmpt[:, c, :, at], start=(at == 0), stop=(at == LB - 1))
                        if n == 0:
                            last.then_inc(half_read, 1)
                    full(last)
                b = take(f"vct.{l}")
                pe.wait_ge(z_free["dve"], freed(f"cmp1.{l}"))
                full(nc.tensor.transpose(PS[0:NBLK, b, 0:P], cct[:, 1, :], ident))
                b = take(f"gs.{l}")
                pe.wait_ge(gate_spread, l + 1)
                for a_ in range(NPAIR):
                    last = nc.tensor.transpose(PS[:, b, 24 * a_:24 * a_ + 24], gx[:, a_ * P:(a_ + 1) * P], ident[0:24, 0:24])
                full(last)

                pe.wait_ge(z_free["act"], freed(f"vct.{l}"))
                pe.wait_ge(z_free["dve"], freed(f"gs.{l}"))
                entry, tile = [l * S_L], [l * T_L]

                def score_bank():
                    e = entry[0]
                    if e - l * S_L >= 4:
                        pe.wait_ge(s_read, e - 3)
                    entry[0] += 1
                    return PS[:, e % 4, :]

                def scores(u):
                    if u < NU:
                        i, g, w = units[u]
                        cols = slice(i * P, (i + 1) * P)
                        if w == 0:
                            ps = score_bank()
                            for j in range(GRP):
                                last = M(ps[:, NBP * j:NBP * (j + 1)], qz[:, g, j, cols], cct[:, 0, 0:NBP], start=True, stop=True)
                            last.then_inc(s_full, 1)
                        for j in range(GRP):
                            ps = score_bank()
                            M(ps[:, 0:(i + 1) * P], qz[:, g, j, cols], kvz[:, 2 - 2 * w, 0:(i + 1) * P],
                              start=True, stop=True).then_inc(s_full, 1)
                    else:
                        a_, w = divmod(u - NU, 2)
                        if w == 0:
                            pe.wait_ge(pair_in[a_ % 2], 16 * 5 * (l * 2 + a_ // 2 + 1))
                            ps = score_bank()
                            for b2 in range(2):
                                last = M(ps[:, 0:NBLK], qs[:, a_, b2, :], cct[:, 0, :], start=(b2 == 0), stop=(b2 == 1))
                            last.then_inc(s_full, 1)
                        ps = score_bank()
                        for b2 in range(2):
                            M(ps[:, 0:PAST].rearrange("p (g n) -> p g n", g=NPG), qs[:, a_, b2, :], cpair[:, a_ % 2, w, b2, :, 0:P],
                              start=(b2 == 0), stop=(b2 == 1))
                        for b2 in range(2):
                            last = M(ps[:, PAST:PAST + NS], qs[:, a_, b2, :], kvz[:, 2 - 2 * w, SEQ:TOK], start=(b2 == 0), stop=(b2 == 1))
                        last.then_inc(s_full, 1)

                def turn(u, part):
                    n, s, pc = tile[0], u % 3, pcmp[u // 2 % 2]
                    if n - l * T_L >= 2:
                        pe.wait_ge(t_out, n - 1)
                    ps = PS[:, 4 + n % 2, :]
                    if u < NU:
                        for j in range(GRP):
                            if part < 0:
                                last = nc.tensor.transpose(ps[0:NBP, j * P:(j + 1) * P], pc[:, NBP * j:NBP * (j + 1)], ident)
                            else:
                                last = nc.tensor.transpose(ps[:, j * P:(j + 1) * P], pr[s][:, j, part * P:(part + 1) * P], ident)
                    else:
                        if u % 2 == 0:
                            nc.tensor.transpose(ps[0:NBLK, 384:512], pc[:, 0:NBLK], ident)
                        nc.tensor.transpose(ps[:, 0:P], pr[s][:, 0, 0:P], ident)
                        nc.tensor.transpose(ps[:, P:2 * P], pr[s][:, 0, P:2 * P], ident)
                        last = nc.tensor.transpose(ps[0:NS, 256:384], pr[s][:, 0, 2 * P:2 * P + NS], ident)
                    last.then_inc(t_full, 1)
                    tile[0] += 1

                def add_values(u, part, n, o):
                    pe.wait_ge(t_out, n + 1)
                    ps, p_ = PS[:, 6 + o % 2, :], ptr[:, n % 3, :]
                    if u < NU:
                        i, g, w = units[u]
                        if part < 0:
                            last = M(ps, VC[0:NBP, :], p_[0:NBP, :], start=True, stop=False)
                        else:
                            last = M(ps, vg[:, part, w * P:(w + 1) * P], p_, start=False, stop=(w == 1 and part == i))
                    else:
                        a_, w = divmod(u - NU, 2)
                        out = ps[:, 0:P]
                        if w == 0:
                            M(out, VC[:, :], p_[0:NBLK, 384:512], start=True, stop=False, skip_group_check=True)
                        for g in range(NPG):
                            for b2 in range(2):
                                cols = slice(b2 * HD, (b2 + 1) * HD)
                                M(out[:, cols], cpair[:, a_ % 2, w, b2, g, P:2 * P], p_[:, g * P + b2 * HD:g * P + (b2 + 1) * HD],
                                  start=False, stop=False, skip_group_check=True)
                        last = M(out, vg[0:NS, 4, w * P:(w + 1) * P], p_[0:NS, 256:384], start=False, stop=(w == 1), skip_group_check=True)
                    last.then_inc(av_done, 1)

                for u in range(U_L + 2):
                    v = u - 2
                    if v >= 0:
                        pe.wait_ge(p_ready, l * U_L + v + 1)
                        parts = ([-1] if units[v][2] == 0 else []) + list(range(units[v][0] + 1)) if v < NU else [0]
                        turn(v, parts[0])
                    if u < U_L:
                        scores(u)
                    if v < 0:
                        continue
                    o = l * O_L + v // 2
                    if v % 2 == 0 and v >= 4:
                        pe.wait_ge(o_out, o - 1)
                    for i, part in enumerate(parts):
                        n = tile[0] - 1
                        if i + 1 < len(parts):
                            turn(v, parts[i + 1])
                        add_values(v, part, n, o)
                pe.wait_ge(s_read, S_L * (l + 1))
                pe.wait_ge(o_out, O_L * (l + 1))

                pe.wait_ge(mixw_in, 32 * (l + 1))
                pe.wait_ge(pooled_ready, l + 1)
                for c in range(2):
                    product(f"pm{c}.{l}", [(poolw[:, c, :], pooled[:, c, :])])
                pe.wait_ge(conv_done, 2 * (l + 1))
                norm(f"cm.{l}", f"cvar.{l}", conv, 2, MEANC)
                pe.wait_ge(ln_out, ln_done(f"cm.{l}"))
                for c in range(2):
                    product(f"pw{c}.{l}", [(pww[:, k, c * P:(c + 1) * P], conv[:, k, :]) for k in range(2)])
                pe.wait_ge(z_free["act"], freed(f"pw1.{l}"))
                for n in range(2):
                    w = weights((f"wo{n}", l))
                    for i in range(4):
                        product(f"o{4 * n + i}.{l}", [(w[:, k, i * P:(i + 1) * P], yt[:, k, :]) for k in range(KD)])
                pe.wait_ge(z_free["dve"], freed(f"o{KD - 1}.{l}"))
                norm(f"lm1.{l}", f"lv1.{l}", h, KD, MEAN)
                pe.wait_ge(ln_out, ln_done(f"lm1.{l}"))
                if l == 0:
                    for c in range(NFC + 1):
                        if c < NFC:
                            w = weights(("ffn", c))
                            for m, name in enumerate(("fg0", "fu0", "fg1", "fu1")):
                                product(f"{name}.{c}", [(w[:, k, m * P:(m + 1) * P], h[:, k, :]) for k in range(KD)])
                        if c > 0:
                            pe.wait_ge(z_free["dve"], freed(f"fu1.{c - 1}"))
                            pe.wait_ge(d_loaded[(c - 1) % 2], 16 * ((c - 1) // 2 + 1))
                            for m in range(KD):
                                product(f"fd{m}.{c - 1}", [(wd[:, (c - 1) % 2, k, m * P:(m + 1) * P], hid[:, (c - 1) % 2, k, :])
                                                           for k in range(2)])
                    pe.wait_ge(z_free["dve"], freed(f"fd{KD - 1}.{NFC - 1}"))
                    norm("lm2", "lv2", x, KD, MEAN)

            pe.wait_ge(moe_in, 32)
            b = take("rt")
            for t in range(5):
                r = P if t < 4 else NS
                for k in range(KD):
                    last = M(PS[0:r, b, NE * t:NE * (t + 1)], h[:, k, t * P:t * P + r], wrt[:, k, :], start=(k == 0), stop=(k == KD - 1))
            full(last)
            for t in range(5):
                r = P if t < 4 else NS
                b = take(f"ht{t}")
                for k in range(KD):
                    last = nc.tensor.transpose(PS[0:r, b + k // 4, (k % 4) * P:(k % 4 + 1) * P], h[:, k, t * P:t * P + r], ident)
                full(last)
            b = take("rk")
            pe.wait_ge(route_masks, 1)
            masks = RT[:, 120:160].rearrange("p (t e) -> p t e", e=NE)
            ustrict, ones = MC[:, MCON["ustrict"]:MCON["ustrict"] + P], MC[:, MCON["ones"]:MCON["ones"] + P]
            for t in range(5):
                r = P if t < 4 else NS
                for j in range(t):
                    M(PS[0:r, b, NE * t:NE * (t + 1)], ones[:, 0:r], masks[:, j, :], start=(j == 0), stop=False)
                M(PS[0:r, b, NE * t:NE * (t + 1)], ustrict[:, 0:r], masks[:, t, :], start=(t == 0), stop=True)
            for j in range(5):
                last = M(PS[:, b, 40:48], ones, masks[:, j, :], start=(j == 0), stop=(j == 4))
            full(last)
            pe.wait_ge(z_free["dve"], freed("rk"))
            pe.wait_ge(z_free["act"], freed("ht4"))
            pe.wait_ge(task_ready, 1)
            T = pe.value_load(TASK[0:1, 2 * NT:2 * NT + 1], min_val=1, max_val=NT)
            pe.sem_inc(e_full, 3)
            pe.sem_inc(e_down, 2)
            with pe.Fori(0, T) as t:
                pe.wait_ge(x_loaded, t * 16 + 16)
                for k in range(KD):
                    last = nc.tensor.transpose(PS[:, k // 4, (k % 4) * P:(k % 4 + 1) * P], xg[:, 0, k * P:(k + 1) * P], ident)
                last.then_inc(x_turned, 1)
                pe.wait_ge(xT_ready, t + 1)

                def up(c):
                    k_ = NWC + c
                    n = 512 if c < NEC - 1 else 256
                    pe.wait_ge(w_loaded[k_ % 3], t * (16 * NEC // 3) + 16 * (k_ // 3 + 1))
                    w = WR[k_ % 3][:, 0:KD * n].rearrange("p (k n) -> p k n", k=KD)
                    for k in range(KD):
                        last = M(PS[:, 2 + c % 2, 0:n], xgT[:, k, :], w[:, k, :], start=(k == 0), stop=(k == KD - 1))
                    last.then_inc(e_full, 1)

                def turn_hidden(c):
                    pe.wait_ge(e_hid, t * NEC + (c + 1))
                    for k in range(2 if c < NEC - 1 else 1):
                        last = nc.tensor.transpose(PS[:, 4 + c % 2, k * P:(k + 1) * P], ehid[:, c % 2, k * P:(k + 1) * P], ident)
                    last.then_inc(eT_full, 1)

                def down(c):
                    k_ = NFC + c
                    pe.wait_ge(d_loaded[k_ % 2], t * (16 * NEC // 2) + 16 * (k_ // 2 + 1))
                    pe.wait_ge(eT_ready, t * NEC + (c + 1))
                    if c == 0:
                        pe.wait_ge(e_yout, t + 1)
                    for k in range(2 if c < NEC - 1 else 1):
                        for n in range(2):
                            at = (k_ % 2) * 2048 + k * D + n * 512
                            last = M(PS[:, 6 + n, :], ehT[:, c % 2, k, :], CA[:, at:at + 512], start=(c == 0 and k == 0), stop=(c == NEC - 1))
                    last.then_inc(e_down, 1)

                for c in range(NEC):
                    up(c)
                    if c >= 1:
                        turn_hidden(c - 1)
                    if c >= 2:
                        down(c - 2)
                turn_hidden(NEC - 1)
                down(NEC - 2)
                down(NEC - 1)


_OUTS = {
    "out_y": (TOK, D), "out_kv": (DEPTH, 6, P, TOK), "out_past": (DEPTH, NB, PAST - TB, 2 * P),
    "out_conv_p": (DEPTH, 2, P, CW - 1), "out_conv_s": (DEPTH, 2, P, NB, CW - 1),
    "out_pool_p": (DEPTH, 2, P, PW - 1), "out_pool_s": (DEPTH, 2, P, NB, PW - 1),
}


def constants():
    f = np.float32
    slope = np.array(SLOPE)
    p = np.arange(P)
    dist = (p[:, None] + 384 - np.arange(SEQ)[None, :]).astype(np.float64)
    bias = -slope[None, :, None] * dist[:, None, :]
    bias = np.where(dist[:, None, :] < 0, -1e30, bias)
    con = np.zeros((P, NCON))

    def put(name, v):
        v = np.asarray(v).reshape(P, -1)
        con[:, CON[name]:CON[name] + v.shape[1]] = v

    put("ident", np.eye(P))
    w = np.array([[WINDOWS[2 * c + (q >= 64)] for c in range(2)] for q in range(P)], float)
    put("invw", 1.0 / w)
    put("invt", 1.0 / np.minimum(np.arange(PW)[None, None, :] + 1, w[:, :, None]))
    row_b, row_h, row_t = p // 64, p % 64 // TB, p % TB
    put("hmask", row_h[:, None] == np.arange(NH)[None, :])
    n = np.arange(NBP)
    pos = (np.arange(4)[:, None] * P + p[None, :]).T
    cd = pos[:, :, None] - (n * LB + (LB - 1) / 2)[None, None, :]
    ok = ((n + 1) * LB - 1)[None, None, :] <= pos[:, :, None]
    cb = -slope[None, None, :, None] * cd[:, :, None, :]
    put("cbias", np.where(ok[:, :, None, :], cb, -1e30))
    sl = slope[row_h]
    put("spast", -sl[:, None] * (PAST + row_t[:, None] - np.arange(PAST)[None, :]))
    key_b, key_t = np.arange(NS) // TB, np.arange(NS) % TB
    seq = 2 * np.arange(NPAIR)[None, :] + row_b[:, None]
    d = row_t[:, None, None] - key_t[None, None, :]
    ok = (key_b[None, None, :] == seq[:, :, None]) & (d >= 0)
    put("snew", np.where(ok, -sl[:, None, None] * d, -1e30))
    blk = np.arange(NBLK)
    blk_b = np.where(blk < NBP, -1, (blk - NBP) // NBS)
    centre = ((blk - NBP) % NBS) * LB + (LB - 1) / 2
    ok = blk_b[None, None, :] == seq[:, :, None]
    sc = -sl[:, None, None] * (PAST + row_t[:, None, None] - centre[None, None, :])
    put("scmp", np.where(ok, sc, -1e30))
    mcon = np.zeros((P, NMCON))
    mcon[:, MCON["ustrict"]:MCON["ustrict"] + P] = p[:, None] < p[None, :]
    mcon[:, MCON["ones"]:MCON["ones"] + P] = 1
    mcon[:, MCON["rev"]:MCON["rev"] + NE] = NE - np.arange(NE)
    mcon[:, MCON["iota"]:MCON["iota"] + NE] = np.arange(NE)
    mcon[:, MCON["task"]:MCON["task"] + NT * NE] = np.repeat(np.arange(NT), NE)
    return bias.astype(f), con.astype(f), mcon[:, 0:MCON["rb"]].astype(f)


def layout(v):
    out = {}
    tok = np.concatenate([v["x_prompt"].reshape(SEQ, D), v["x_sample"].reshape(NS, D)])
    rows = lambda w: np.ascontiguousarray(w.reshape(-1, P, w.shape[-1]).transpose(1, 0, 2))
    out["xt"] = rows(np.ascontiguousarray(tok.T))
    heads = [512 + HD * hh + np.arange(HD) for j in range(GRP) for hh in (j, j + GRP)]
    order = {"glu": np.r_[256:512, 0:256], "kwp": np.r_[1536:1792, 1816:2072], "kcks": np.r_[1024:1536], "q": np.concatenate(heads)}
    gate = np.r_[1792:1816]
    out["w_in"] = np.stack([np.stack([rows(w[:, order[n]]).reshape(P, -1) for n in ("glu", "kwp", "kcks", "q")]) for w in v["w_in"]])
    out["w_gate"] = np.stack([rows(w[:, gate]) for w in v["w_in"]])
    cw = v["cmp_w"].reshape(DEPTH, 2, LB, HD, HD)
    bd = np.zeros((DEPTH, 2, NKV, HD, LB, NKV, HD), np.float32)
    for g in range(NKV):
        bd[:, :, g, :, :, g, :] = cw.transpose(0, 1, 3, 2, 4)
    out["cmp_w"] = np.ascontiguousarray(bd.reshape(DEPTH, 2, P, 2, LB // 2, P).transpose(0, 1, 3, 2, 4, 5)).reshape(DEPTH, 4, P, 4096)
    att = np.concatenate([256 + HD * hh + np.arange(HD) for j in range(GRP) for hh in (j, j + GRP)])
    mixed = np.concatenate([np.arange(256), att, np.arange(768, D)])
    out["w_out"] = np.stack([np.stack([rows(w[mixed][:, 512 * c:512 * (c + 1)]).reshape(P, -1) for c in range(2)]) for w in v["w_out"]])
    gu, dn = v["ffn_w_gu"][0], v["ffn_w_dn"][0]
    two = lambda w, f, c, n: np.concatenate([w[:, 256 * c + P * i:256 * c + P * (i + 1)] if s == 0 else w[:, f + 256 * c + P * i:f + 256 * c + P * (i + 1)]
                                             for i in range(n) for s in range(2)], 1)
    out["ffn_gu"] = np.stack([rows(two(gu, DFF, c, 2)).reshape(P, -1) for c in range(NFC)])
    out["ffn_dn"] = np.stack([rows(dn[256 * c:256 * (c + 1)]) for c in range(NFC)])
    mg, md = v["moe_w_gu"][0], v["moe_w_dn"][0]
    gate_up = lambda w, c, n: np.concatenate([w[:, 256 * c:256 * c + n], w[:, DFE + 256 * c:DFE + 256 * c + n]], 1)
    out["moe_gu"] = np.stack([np.stack([rows(gate_up(w, c, 256)).reshape(P, -1) for c in range(NEC - 1)]) for w in mg])
    out["moe_gu_last"] = np.stack([rows(gate_up(w, NEC - 1, P)).reshape(P, -1) for w in mg])
    out["moe_dn"] = np.stack([np.stack([rows(w[256 * c:256 * (c + 1)]).reshape(P, -1) for c in range(NEC - 1)]) for w in md])
    out["moe_dn_last"] = np.stack([rows(w[256 * (NEC - 1):]).reshape(P, -1) for w in md])
    out["w_router"] = rows(v["moe_w_router"][0])
    kt = lambda kv, c: kv[..., :, c, :, :].reshape(*kv.shape[:-4], PAGE, P)
    sw = lambda a: np.swapaxes(a, -1, -2)
    cmp_ = v["cache_cmp_kv"]
    out["cmp_pages"] = np.ascontiguousarray(np.stack([sw(kt(cmp_, 0)), sw(kt(cmp_, 1))], 3))
    slc = v["cache_slc_kv"]
    out["slc_pages"] = np.ascontiguousarray(np.concatenate([sw(kt(slc, 0)), kt(slc, 1)], -1))
    swa = v["cache_swa_kv"].reshape(DEPTH, NPAIR, 2, NPG, PAGE, 2, NKV, HD)
    out["swa_pairs"] = np.ascontiguousarray(np.concatenate([sw(kt(swa, 0)), kt(swa, 1)], -1).transpose(0, 1, 4, 2, 3, 5))
    out["swa_cache"] = v["cache_swa_kv"].reshape(DEPTH, NB, PAST, 2 * P)
    pe = v["cmp_pe"].transpose(0, 3, 1, 2)
    out["pe"] = np.ascontiguousarray(np.concatenate([pe, pe], 1))
    chan = lambda s: np.ascontiguousarray(s.reshape(DEPTH, NB, s.shape[2], 2, P).transpose(0, 4, 3, 1, 2))
    out["state_conv"], out["state_pool"] = chan(v["state_conv"]), chan(v["state_pool"])
    pw = np.zeros((DEPTH, 2, 2, HD, 2, HD), np.float32)
    for g in range(2):
        pw[:, :, g, :, g, :] = v["pool_w"].reshape(DEPTH, 2, 2, HD, HD)[:, :, g]
    out["pool_w"] = np.ascontiguousarray(pw.reshape(DEPTH, 2, P, P).transpose(0, 2, 1, 3))
    out["pw_w"] = np.stack([rows(w) for w in v["conv_pw_w"]])
    col = lambda a: a.reshape(-1, P).T
    parts = []
    for l in range(DEPTH):
        b = v["b_in"][l]
        bg = np.zeros((P, 1), np.float32)
        bg[0:24, 0] = b[gate]
        parts += [col(b[np.concatenate([order[n] for n in ("glu", "kwp", "kcks", "q")])]), bg,
                  np.ascontiguousarray(v["conv_dw_w"][l].reshape(CW, 2, P).transpose(2, 1, 0)).reshape(P, -1)]
        parts += [col(v[n][l]) for n in ("conv_dw_b", "conv_ln_g", "conv_ln_b", "conv_pw_b", "pool_scale", "b_out",
                                         "ln1_g", "ln1_b", "ln2_g", "ln2_b")]
    out["par"] = np.ascontiguousarray(np.concatenate(parts + [col(v["ln_in_g"]), col(v["ln_in_b"])], 1))
    out["ln_rows"] = np.stack([v["ln2_g"][1], v["ln2_b"][1]])
    out["rb_row"] = v["moe_b_router"].reshape(1, NE)
    out["page_table"] = v["page_table"].reshape(1, -1).astype(np.int32)
    out["bias"], out["con"], out["mcon"] = constants()
    return out


def kernel(**inputs):
    from concourse import bacc
    from concourse.bass_utils import run_bass_kernel_spmd

    v = {n: np.asarray(x) for n, x in inputs.items()}
    arrays = {f"in_{n}": np.ascontiguousarray(x) for n, x in layout(v).items()}
    nc = bacc.Bacc("TRN2", target_bir_lowering=False, num_devices=1)
    aps = {n[3:]: nc.dram_tensor(n, x.shape, mybir.dt.from_np(x.dtype), kind="ExternalInput").ap() for n, x in arrays.items()}
    for n, shape in _OUTS.items():
        aps[n] = nc.dram_tensor(n, shape, F32, kind="ExternalOutput").ap()
    program(nc, aps)
    r = run_bass_kernel_spmd(nc, [arrays], core_ids=[0]).results[0]
    y, kv, past = r["out_y"], r["out_kv"], r["out_past"]
    rows = kv.reshape(DEPTH, 3, 2, NKV, HD, TOK).transpose(1, 0, 5, 2, 3, 4)
    prompt, new = rows[:, :, :SEQ], rows[:, :, SEQ:].reshape(3, DEPTH, NB, TB, 2, NKV, HD)
    swa = np.concatenate([past.reshape(DEPTH, NB, PAST - TB, 2, NKV, HD), new[2]], 2)
    back = lambda s: s.transpose(0, 3, 4, 1, 2).reshape(DEPTH, NB, s.shape[4], 2 * P)
    return (y[:SEQ].reshape(1, SEQ, D), y[SEQ:].reshape(NB, TB, D),
            prompt[0][:, None], new[0], prompt[1][:, None], new[1],
            prompt[2][:, None, SEQ - PAST:], swa,
            r["out_conv_p"].transpose(0, 3, 1, 2).reshape(DEPTH, 1, CW - 1, 2 * P), back(r["out_conv_s"]),
            r["out_pool_p"].transpose(0, 3, 1, 2).reshape(DEPTH, 1, PW - 1, 2 * P), back(r["out_pool_s"]))
```

```python
import concourse.bass as bass
import numpy as np
from concourse import mybir
from contextlib import ExitStack

F32 = mybir.dt.float32
F32R = mybir.dt.float32r
I32 = mybir.dt.int32
ALU = mybir.AluOpType
ACT = mybir.ActivationFunctionType
AX = mybir.AxisListType

P = 128
D = 1024
KD = D // P
SEQ, NB, TB = 512, 8, 8
NS = NB * TB
TOK = SEQ + NS
HALF = TOK // 2
DEPTH = 2
HD, NKV, GRP = 64, 2, 4
NH = NKV * GRP
PAST, PAGE = 256, 128
NPG = PAST // PAGE
LB = 64
NBP, NBS = SEQ // LB, PAST // LB
NBLK = NBP + NB * NBS
CW, PW = 31, 16
ALPHA = float((2 * DEPTH) ** 0.25)
EPS = 1e-5
FLOOR, TINY, BIG = -1e29, 1e-30, 3e32
DFF, DFE, NE = 2816, 1408, 8
NFC = DFF // 256
NEC = 6
CH = 128
ROWS = 2 * TOK
NT = NE + ROWS // CH
WINDOWS = (2, 4, 8, 16)
UP, US = CW - 1 + SEQ, CW - 1 + TB
EP, ES = PW - 1 + SEQ, PW - 1 + TB
EXT = EP + NB * ES
NPAIR = NB // 2
SLOPE = [2.0 ** -(h + 1) for h in range(NH)]

TILES = {"glu": ("g0", "g1", "a0", "a1"), "kcks": ("ck", "cv", "sk", "sv"), "kwp": ("wk", "wv", "p0", "p1"), "q": ("q0", "q1", "q2", "q3")}


def columns(widths):
    at, out = 0, {}
    for name, w in widths:
        out[name] = at
        at += w
    return out, at


PAR, NPAR = columns([("bin", 17), ("cw", 2 * CW), ("cb", 2), ("clg", 2), ("clb", 2), ("pwb", 2), ("psc", 2),
                     ("bo", KD), ("g1", KD), ("b1", KD), ("g2", KD), ("b2", KD)])
CON, NCON = columns([("ident", P), ("invw", 2), ("invt", 2 * PW), ("hmask", NH),
                     ("cbias", 4 * NKV * GRP * NBP), ("spast", PAST), ("snew", NPAIR * NS), ("scmp", NPAIR * NBLK)])
MCON, NMCON = columns([("ustrict", P), ("ones", P), ("rev", NE), ("iota", NE), ("task", NE * NT), ("rb", NE)])


def schedule():
    out = [("lm", "lnc"), ("lv", "act")]
    for l in range(DEPTH):
        out += [(f"{n}.{l}", "dve" if n[0] == "a" else "act") for key in ("glu", "kcks", "kwp") for n in TILES[key]]
        out += [(f"gate.{l}", "act"), (f"cmp0.{l}", "dve"), (f"q0.{l}", "dve"), (f"q1.{l}", "dve"), (f"cm.{l}", "lnc")]
        out += [(f"q2.{l}", "dve"), (f"q3.{l}", "dve"), (f"cvar.{l}", "act")]
        out += [(f"vt{t}.{l}", "act") for t in range(5)]
        out += [(f"cmp1.{l}", "dve"), (f"pm0.{l}", "act"), (f"pm1.{l}", "act"), (f"vct.{l}", "act"), (f"gs.{l}", "dve")]
        out += [(f"pw{c}.{l}", "act") for c in range(2)]
        out += [(f"o{m}.{l}", "dve") for m in range(KD)]
        out += [(f"lm1.{l}", "lnc"), (f"lv1.{l}", "act")]
        if l == 0:
            for c in range(NFC + 1):
                if c < NFC:
                    out += [(f"fg0.{c}", "act"), (f"fu0.{c}", "dve"), (f"fg1.{c}", "act"), (f"fu1.{c}", "dve")]
                if c > 0:
                    out += [(f"fd{m}.{c - 1}", "dve") for m in range(KD)]
            out += [("lm2", "lnc"), ("lv2", "act")]
        else:
            out += [("rl", "act"), ("rt", "dve"), ("ht0", "act"), ("ht1", "act"), ("rk", "dve")] + [(f"ht{t}", "act") for t in range(2, 5)]
    return out


def in_order(eng, own):
    counts = {}

    def done(ins, event=own, start=0):
        ins.then_inc(event, 1)
        counts[id(event)] = counts[id(event)] + 1 if id(event) in counts else 1
        eng.wait_ge(event, start + counts[id(event)])

    return done


def program(nc, a):
    sched = schedule()
    ZI = {name: n for n, (name, _) in enumerate(sched)}
    ctx = ExitStack()
    with ctx:
        def sb(name, width, rows=P, dt=F32):
            return ctx.enter_context(nc.sbuf_tensor(name, [rows, width], dt))

        def in_place_of_next(name, width):
            with nc.sbuf_tensor(name, [P, width], F32R) as t:
                return t

        H = sb("h", KD * TOK)
        MHI = in_place_of_next("mixed_high", KD * TOK)
        X = sb("x", KD * TOK)
        HHI = in_place_of_next("h_high", KD * TOK)
        YT = sb("yt", KD * TOK)
        WHI = in_place_of_next("w_high", 4096)
        WR = [sb("w0", 4096), sb("w1", 4096)]
        WLO = in_place_of_next("w_low", 4096)
        WR.append(sb("w2", 4096))
        HLO = in_place_of_next("h_low", KD * TOK)
        QA = sb("qarena", 5 * D)
        KVZ = sb("kvz", 4 * TOK)
        KCS = sb("kcs", 2 * NS)
        GHI = in_place_of_next("hidden_high", 4 * TOK)
        CA = sb("carena", 4096)
        VG = sb("vtok", 5 * 280)
        UE = sb("uext", 2 * (UP + NB * US))
        GLO = in_place_of_next("hidden_low", KD * TOK)
        PA = sb("parena", 5632)
        BIAS = sb("bias", NH * SEQ)
        PAR_ = sb("par", DEPTH * NPAR + 2 * KD)
        CON_ = sb("con", NCON)
        MEAN = sb("mean", P)
        MEANC = sb("meanc", P)
        CCT = sb("cct", 2 * NBLK)
        VC = sb("vc", P, rows=NBLK)
        PC = sb("pc", 2 * NBLK)
        SM = sb("sm", 96)
        BQ = sb("bq", 4 * DEPTH)
        PT = sb("pages", NB * NPG, rows=1, dt=I32)
        SLOT = sb("slot", 10, dt=I32)
        TASK = sb("task", 2 * NT + 1, rows=1, dt=I32)
        PS = ctx.enter_context(nc.psum_tensor("ps", [P, 8, 512], F32))
        x_dram = nc.dram_tensor("sorted_rows", [ROWS + CH, D], F32).ap()
        y_dram = nc.dram_tensor("expert_rows", [ROWS + CH, D], F32).ap()

        h = H[:, :].rearrange("p (k n) -> p k n", k=KD)
        x = X[:, :].rearrange("p (k n) -> p k n", k=KD)
        yt = YT[:, :].rearrange("p (k n) -> p k n", k=KD)
        conv = X[:, 0:2 * TOK].rearrange("p (c n) -> p c n", c=2)
        sig = X[:, 2 * TOK:4 * TOK].rearrange("p (c n) -> p c n", c=2)
        pooled = sig
        ext = X[:, 4 * TOK:4 * TOK + 2 * EXT].rearrange("p (c n) -> p c n", c=2)
        gT = X[0:24, 4 * TOK + 2 * EXT:5 * TOK + 2 * EXT]
        wgate = X[:, 5 * TOK + 2 * EXT:5 * TOK + 2 * EXT + 192].rearrange("p (k n) -> p k n", k=KD)
        gx = YT[0:24, 4 * EXT + 96:4 * EXT + 96 + NPAIR * P]
        win_a = YT[:, 0:2 * EXT].rearrange("p (c n) -> p c n", c=2)
        win_b = YT[:, 2 * EXT:4 * EXT].rearrange("p (c n) -> p c n", c=2)
        qz = QA[:, 0:NKV * GRP * SEQ].rearrange("p (g j n) -> p g j n", g=NKV, j=GRP)
        qs = QA[:, NKV * GRP * SEQ:].rearrange("p (a b r) -> p a b r", a=NPAIR, b=2)
        kvz = KVZ[:, :].rearrange("p (k n) -> p k n", k=4)
        kcs = KCS[:, :].rearrange("p (c n) -> p c n", c=2)
        cpair = CA[:, :].rearrange("p (s w b g n) -> p s w b g n", s=2, w=2, b=2, g=NPG)
        vg = VG[:, :].rearrange("p (t n) -> p t n", t=5)
        ue = UE[:, :].rearrange("p (c n) -> p c n", c=2)
        cmpt = PA[:, 0:2 * (NBLK + 1) * LB].rearrange("p (c n l) -> p c n l", c=2, l=LB)
        pr = [ap.rearrange("p (j n) -> p j n", j=GRP)
              for ap in (PA[:, 0:2048], PA[:, 2048:4096], X[:, 4 * TOK:4 * TOK + 2048], X[:, 0:2048])]
        pcmp = [PC[:, NBLK * i:NBLK * (i + 1)] for i in range(2)]
        ptr = PA[:, 4096:5632].rearrange("p (s n) -> p s n", s=3)
        MIXED = (0, 1, 6, 7, 2, 3, 4, 5)
        tiles = lambda t: t[:, :].rearrange("p (k n) -> p k n", k=KD)
        h_parts = tiles(HHI), tiles(HLO)
        mixed_parts = tiles(MHI), tiles(GLO)
        hid_parts = tuple(t[:, 0:4 * TOK].rearrange("p (s k n) -> p s k n", s=2, k=2) for t in (GHI, GLO))
        hid = PA[:, 5 * TOK:6 * TOK]
        piece_raw = [WR[1][:, D * i:D * (i + 1)] for i in range(4)]
        piece_parts = [(WHI[:, D * i:D * (i + 1)], WLO[:, D * i:D * (i + 1)]) for i in range(4)]
        silu = PA[:, 4 * TOK:5 * TOK]
        sq = PA[:, 5 * TOK:7 * TOK].rearrange("p (s n) -> p s n", s=2)
        std = PA[:, 7 * TOK:8 * TOK]
        poolw = CA[:, 2048:2048 + 2 * P].rearrange("p (c n) -> p c n", c=2)
        pww = CA[:, 2048 + 2 * P:2048 + 6 * P].rearrange("p (c n) -> p c n", c=2)
        cstd = CA[:, 2048 + 6 * P:2048 + 6 * P + TOK]
        csq = yt[:, 6:8, :]
        bias = BIAS[:, :].rearrange("p (h n) -> p h n", h=NH)
        cct = CCT[:, :].rearrange("p (c n) -> p c n", c=2)
        ident = CON_[:, 0:P]
        cbias = CON_[:, CON["cbias"]:CON["cbias"] + 256].rearrange("p (i g n) -> p i g n", i=4, g=NKV)
        htok = QA[:, :].rearrange("p (t n) -> p t n", t=5)
        xg = PA[:, 0:2 * D].rearrange("p (s n) -> p s n", s=2)
        xgT = PA[:, 2 * D:3 * D].rearrange("p (k n) -> p k n", k=KD)
        ehT = PA[:, 3 * D:3 * D + 512].rearrange("p (s k n) -> p s k n", s=2, k=2)
        esil = PA[:, 3584:4096].rearrange("p (s n) -> p s n", s=2)
        ehid = PA[:, 4096:4608].rearrange("p (s n) -> p s n", s=2)
        ysb = PA[:, 4608:5632]
        MC = KVZ[:, 0:NMCON]
        RT = KVZ[:, 640:1664]
        wrt = KVZ[:, 1664:1728].rearrange("p (k n) -> p k n", k=KD)
        ygat = X[:, 0:4096].rearrange("p (s w n) -> p s w n", s=2, w=2)
        xf = YT[:, 0:2048].rearrange("p (s n) -> p s n", s=2)
        lnrow = YT[:, 2048:4096].rearrange("p (s n) -> p s n", s=2)
        rstd = lambda t, r: SM[0:r, 2 * (t % 2):2 * (t % 2) + 1]
        shift = lambda t, r: SM[0:r, 2 * (t % 2) + 1:2 * (t % 2) + 2]
        zrow = BIAS[:, 0:D]
        logits = BIAS[0:NE, D:D + TOK]

        def par(name, l, n=0, rows=P):
            at = l * NPAR + PAR[name] + n
            return PAR_[0:rows, at:at + 1]

        def z_pair(name):
            return 2 * (ZI[name] % 4)

        def pair(name, rows=P):
            b = z_pair(name)
            return PS[0:rows, b:b + 2, 0:HALF]

        def less(s, j, n=1):
            return SM[:, 5 * s + j:5 * s + j + n]

        def total(s, j, n=1):
            return SM[:, 64 + 5 * s + j:64 + 5 * s + j + n]

        def flat(ap):
            return ap.rearrange("p (a n) -> p a n", a=2)

        def pieces(name, rows=slice(0, P)):
            b = z_pair(name)
            return [(PS[rows, b, 0:HALF], 0, HALF), (PS[rows, b + 1, 0:SEQ - HALF], HALF, SEQ),
                    (PS[rows, b + 1, SEQ - HALF:HALF], SEQ, TOK)]

        def ev(name):
            return ctx.enter_context(nc.semaphore(name))

        def freed(name):
            n = ZI[name]
            return ln_done(name) if sched[n][1] == "lnc" else sum(o == sched[n][1] for _, o in sched[:n + 1])

        w_loaded = [ctx.enter_context(nc.semaphore(f"w_loaded{i}")) for i in range(3)]
        d_loaded = [ctx.enter_context(nc.semaphore(f"d_loaded{i}")) for i in range(2)]
        half_read = ev("half_read")
        piece_in = [ctx.enter_context(nc.semaphore(f"piece_in{i}")) for i in range(4)]
        mixed_high, mixed_low = ev("mixed_high_ready"), ev("mixed_low_ready")
        w_high, w_low, h_low, hid_low = (ev(n) for n in ("w_high_ready", "w_low_ready", "h_low_ready", "hid_low_ready"))
        z_full = ev("z_full")
        act_own, dve_own, pool_own = (ctx.enter_context(nc.semaphore(n)) for n in ("act_own", "dve_own", "pool_own"))
        consts_in, x_in = (ctx.enter_context(nc.semaphore(n)) for n in ("consts_in", "x_in"))
        states_in, pages_in, mixw_in = (ctx.enter_context(nc.semaphore(n)) for n in ("states_in", "pages_in", "mixw_in"))
        pair_in = [ctx.enter_context(nc.semaphore(f"pair_in{i}")) for i in range(2)]
        pt_in, out_kv, out_state, out_past = (ctx.enter_context(nc.semaphore(n)) for n in ("pt_in", "out_kv", "out_state", "out_past"))
        ones_set, qz_zeroed, zeros_set = ev("ones_set"), ev("qz_zeroed"), ev("zeros_set")
        ln_centered, ln_squared, ln_sq_used, ln_scaled, ln_out = (
            ev(n) for n in ("ln_centered", "ln_squared", "ln_sq_used", "ln_scaled", "ln_out"))
        z_free = {"act": ev("z_free_act"), "dve": ev("z_free_dve"), "lnc": ln_centered}
        conv_done, pooled_ready = (ev(n) for n in ("conv_done", "pooled_ready"))
        s_full, s_read, p_max, p_exp, p_ready, t_full, t_out, av_done, o_out = (
            ev(n) for n in ("s_full", "s_read", "p_max", "p_exp", "p_ready", "t_full", "t_out", "av_done", "o_out"))
        h_scaled, gate_spread = ev("h_scaled"), ev("gate_spread")
        slot_ready, task_ready, route_masks = (ev(n) for n in ("slot_ready", "task_ready", "route_masks"))
        moe_rb, moe_in, xd_zero, scattered = (ctx.enter_context(nc.semaphore(n)) for n in ("moe_rb", "moe_in", "xd_zero", "scattered"))
        x_loaded, y_stored, lnrow_in = (ctx.enter_context(nc.semaphore(n)) for n in ("x_loaded", "y_stored", "lnrow_in"))
        x_turned, xT_ready, e_full, e_silu, e_hid, eT_full, eT_ready, e_down, e_yout = (
            ctx.enter_context(nc.semaphore(n)) for n in ("x_turned", "xT_ready", "e_full", "e_silu", "e_hid", "eT_full",
                                                         "eT_ready", "e_down", "e_yout"))
        ysb_free = ctx.enter_context(nc.semaphore("ysb_free"))
        dve_loop, act_loop = (ctx.enter_context(nc.semaphore(n)) for n in ("dve_loop", "act_loop"))
        y_gathered = [ctx.enter_context(nc.semaphore(f"y_gathered{i}")) for i in range(2)]
        gate_exp, var_ready, dev_ready, stats_ready, normalized, gained, h_alpha = (
            ev(n) for n in ("gate_exp", "var_ready", "dev_ready", "stats_ready", "normalized", "gained", "h_alpha"))
        fin_ready, out_y = ev("fin_ready"), [ctx.enter_context(nc.semaphore(f"out_y{i}")) for i in range(2)]

        chunk_of = {}
        for l in range(DEPTH):
            for n in ["glu", "kcks", "kwp", "cmp0", "cmp1", "q", "cmp2", "cmp3"]:
                chunk_of[n, l] = len(chunk_of)
        NWC = len(chunk_of)
        last_read = {("glu", "a1"), ("kwp", "p1"), ("kcks", "sv"), ("q", "q3"), ("cmp1", "cmp0"), ("cmp3", "cmp1")}
        chunk_read = {}
        for l in range(DEPTH):
            for n, z in last_read:
                chunk_read[chunk_of[n, l]] = z_full, ZI[f"{z}.{l}"] + 1
            for i, n in enumerate(("cmp0", "cmp2")):
                chunk_read[chunk_of[n, l]] = half_read, 2 * l + i + 1
        pieces_of, piece_read, pieces_end = {}, [], []
        for l in range(DEPTH):
            for m in range(KD):
                pieces_of["o", m, l] = len(piece_read)
                piece_read.append(f"o{m}.{l}")
            for c in range(NFC + 1 if l == 0 else 0):
                for name in ("fg0", "fu0", "fg1", "fu1") if c < NFC else ():
                    pieces_of[name, c] = len(piece_read)
                    piece_read.append(f"{name}.{c}")
                for k in range(2 if c > 0 else 0):
                    pieces_of[k, c - 1] = len(piece_read)
                    piece_read.append(f"fd{KD - 1}.{c - 1}")
            pieces_end.append(len(piece_read))
        pieces_start = [0] + pieces_end
        ln_order = [("lm", KD), ("cm.0", 2), ("lm1.0", KD), ("lm2", KD), ("cm.1", 2), ("lm1.1", KD)]
        ln_before = {}
        for i, (n, _) in enumerate(ln_order):
            ln_before[n] = (i, sum(k for _, k in ln_order[:i]))
        LN_ALL = sum(k for _, k in ln_order)

        def ln_done(name):
            i, before = ln_before[name]
            return before + dict(ln_order)[name]

        units = [(i, g, w) for i in range(4) for g in range(NKV) for w in range(2)]
        NU = len(units)
        S_L = NU * GRP + NU // 2 + 3 * NPAIR
        T_P = sum(i + 1 for i, _, _ in units) + NU // 2
        T_L = T_P + 2 * NPAIR

        def tiles_through(u):
            if u >= NU:
                return T_P + u - NU + 1
            return sum(i + 1 + (w == 0) for i, _, w in units[:u + 1])

        U_L = NU + 2 * NPAIR
        O_L = NU // 2 + NPAIR
        block = ctx.enter_context(nc.Block())

        @block.sync
        def _(sp):
            sp.dma_start(x, a["xt"]).then_inc(x_in, 16)
            sp.dma_start(PAR_[:, :], a["par"]).then_inc(consts_in, 16)
            sp.dma_start(CON_[:, :], a["con"]).then_inc(consts_in, 16)
            sp.dma_start(PT[:, :], a["page_table"]).then_inc(pt_in, 16)
            sp.dma_start(BIAS[:, :], a["bias"]).then_inc(consts_in, 16)

            def load_w(key, src, n=4096):
                c = chunk_of[key]
                if c >= 3:
                    done, count = chunk_read[c - 3]
                    sp.wait_ge(done, count)
                if key == ("glu", 1):
                    sp.wait_ge(z_full, ZI[f"fd{KD - 1}.{NFC - 1}"] + 1)
                sp.dma_start(WR[c % 3][:, 0:n], src).then_inc(w_loaded[c % 3], 16)

            sp.wait_ge(pt_in, 16)
            page = [sp.value_load(PT[0:1, n:n + 1], min_val=0, max_val=a["cmp_pages"].shape[1] - 1) for n in range(NB * NPG)]

            def load_pair(l, n):
                if n >= 2:
                    sp.wait_ge(av_done, l * T_L + T_P + 2 * (n - 1))
                elif n == 1:
                    sp.wait_ge(z_full, ZI[f"pw1.{l}"] + 1)
                for b in range(2):
                    for g in range(NPG):
                        sp.dma_start(cpair[:, n % 2, 0, b, g, :],
                                     a["slc_pages"][l, bass.ds(page[(2 * n + b) * NPG + g], 1), :, :].rearrange("a p n -> (a p) n")
                                     ).then_inc(pair_in[n % 2], 16)
                sp.dma_start(cpair[:, n % 2, 1], a["swa_pairs"][l, n]).then_inc(pair_in[n % 2], 16)

            def load_piece(l, p):
                if p >= 4:
                    sp.wait_ge(w_low, p - 3)
                if p == pieces_start[l]:
                    sp.wait_ge(z_full, ZI[f"cmp1.{l}"] + 1)
                sp.dma_start(piece_raw[p % 4], a["split_w"][p]).then_inc(piece_in[p % 4], 16)

            for l in range(DEPTH):
                load_w(("glu", l), a["w_in"][l, 0])
                load_w(("kcks", l), a["w_in"][l, 2])
                load_w(("kwp", l), a["w_in"][l, 1])
                sp.wait_ge(ln_out, ln_done("lm" if l == 0 else "lm2"))
                sp.dma_start(wgate, a["w_gate"][l]).then_inc(states_in, 16)
                for c in range(2):
                    sp.dma_start(ext[:, c, EP:].rearrange("p (b n) -> p b n", b=NB)[:, :, 0:PW - 1],
                                 a["state_pool"][l, :, c]).then_inc(states_in, 16)
                if l == 1:
                    sp.wait_ge(conv_done, 2)
                    sp.wait_ge(out_state, 16 * 8)
                for c in range(2):
                    sp.dma_start(ue[:, c, UP:].rearrange("p (b n) -> p b n", b=NB)[:, :, 0:CW - 1],
                                 a["state_conv"][l, :, c]).then_inc(states_in, 16)
                for b in range(NB):
                    for g in range(NPG):
                        at = NBP + b * NBS + g * (PAGE // LB)
                        sp.dma_start(cmpt[:, :, at:at + PAGE // LB, :],
                                     a["cmp_pages"][l, bass.ds(page[b * NPG + g], 1)].rearrange("a p c n -> (a p) c n")
                                     ).then_inc(pages_in, 16)
                sp.dma_start(cmpt[:, :, NBLK, :], a["pe"][l]).then_inc(pages_in, 16)
                load_w(("cmp0", l), a["cmp_w"][l, 0])
                load_w(("cmp1", l), a["cmp_w"][l, 1])
                if l == 1:
                    sp.wait_ge(z_full, ZI[f"fd{KD - 1}.{NFC - 1}"] + 1)
                sp.dma_start(poolw, a["pool_w"][l]).then_inc(mixw_in, 16)
                sp.dma_start(pww, a["pw_w"][l]).then_inc(mixw_in, 16)
                load_w(("q", l), a["w_in"][l, 3])
                load_w(("cmp2", l), a["cmp_w"][l, 2])
                load_w(("cmp3", l), a["cmp_w"][l, 3])
                load_pair(l, 0)
                sp.dma_start(a["out_past"][l], a["swa_cache"][l, :, TB:PAST, :]).then_inc(out_past, 16)
                for p in range(pieces_start[l], pieces_start[l] + 4):
                    load_piece(l, p)
                load_pair(l, 1)
                load_pair(l, 2)
                load_pair(l, 3)
                for p in range(pieces_start[l] + 4, pieces_end[l]):
                    load_piece(l, p)
            sp.wait_ge(out_kv, 16 * 16)
            sp.wait_ge(av_done, T_L * DEPTH)
            sp.dma_start(MC[:, 0:MCON["rb"]], a["mcon"]).then_inc(moe_in, 16)
            sp.dma_start(wrt, a["w_router"]).then_inc(moe_in, 16)
            sp.dma_start(MC[:, MCON["rb"]:MCON["rb"] + NE], a["rb_row"].broadcast_to([P, NE])).then_inc(moe_rb, 16)
            sp.wait_ge(z_full, ZI["o7.1"] + 1)
            for i in range(2):
                sp.dma_start(lnrow[:, i, :], a["ln_rows"][i:i + 1, :].broadcast_to([P, D])).then_inc(lnrow_in, 16)
            sp.wait_ge(z_full, ZI["o7.1"] + 1)

            def load_up(e, c, t):
                k = NWC + c
                slot = WR[k % 3]
                wide = 4096 if c < NEC - 1 else 2048
                at = slice(0, 1) if t is None else bass.ds(e, 1)
                src = a["moe_gu"][at, c] if c < NEC - 1 else a["moe_gu_last"][at]
                if t is not None:
                    sp.wait_ge(e_full, t * NEC + (c + 1))
                sp.dma_start(slot[:, 0:wide], src.rearrange("a p n -> (a p) n")).then_inc(w_loaded[k % 3], 16)

            load_up(None, 0, None)
            load_up(None, 1, None)
            sp.wait_ge(task_ready, 1)
            T = sp.value_load(TASK[0:1, 2 * NT:2 * NT + 1], min_val=1, max_val=NT)
            sp.wait_ge(x_loaded, 16)
            with sp.Fori(0, T) as t:
                e = sp.value_load(TASK[0:1, bass.ds(t, 1)], min_val=0, max_val=NE - 1)
                e_next = sp.value_load(TASK[0:1, bass.ds(t + 1, 1)], min_val=0, max_val=NE - 1)
                for c in range(NEC):
                    if c + 2 < NEC:
                        load_up(e, c + 2, t)
                    else:
                        load_up(e_next, c + 2 - NEC, t + 1)
                    k = c
                    sp.wait_ge(e_down, t * NEC + (c + 1))
                    src = a["moe_dn"][bass.ds(e, 1), c] if c < NEC - 1 else a["moe_dn_last"][bass.ds(e, 1)]
                    kk = 2 if c < NEC - 1 else 1
                    sp.dma_start(CA[:, (k % 2) * 2048:(k % 2) * 2048 + kk * D],
                                 src.rearrange("a p n -> (a p) n")).then_inc(d_loaded[k % 2], 16)
            for t in range(5):
                r = P if t < 4 else NS
                sp.wait_ge(fin_ready, t + 1)
                sp.dma_start(a["out_y"][t * P:t * P + r, :], xf[0:r, t % 2, :]).then_inc(out_y[t % 2], 16)
            sp.wait_ge(out_y[0], 16 * 3)
            sp.wait_ge(out_y[1], 16 * 2)
            sp.wait_ge(out_past, 16 * DEPTH)
            sp.wait_ge(out_kv, 16 * 16)
            sp.wait_ge(out_state, 16 * 16)

        @block.gpsimd
        def _(pool):
            done = in_order(pool, pool_own)
            done(nc.gpsimd.memset(MEAN[:, :], 1.0 / D))
            done(nc.gpsimd.memset(MEANC[:, :], 1.0 / (2 * P)), ones_set)
            done(nc.gpsimd.memset(ue[:, :, 0:CW - 1], 0.0))
            done(nc.gpsimd.memset(SM[:, :], 0.0))
            done(nc.gpsimd.memset(QA[:, :], 0.0), qz_zeroed)
            pool.wait_ge(consts_in, 48)
            for l in range(DEPTH):
                pool.wait_ge(states_in, 16 * 5 * (l + 1))
                for c in range(2):
                    pool.wait_ge(z_free["dve"], freed(f"a{c}.{l}"))
                    pool.dma_start(a["out_conv_p"][l, c], ue[:, c, SEQ:UP]).then_inc(out_state, 16)
                    pool.dma_start(a["out_conv_s"][l, c],
                                   ue[:, c, UP:].rearrange("p (b n) -> p b n", b=NB)[:, :, TB:US]).then_inc(out_state, 16)
                    pool.wait_ge(z_free["act"], freed(f"p{c}.{l}"))
                    pool.dma_start(a["out_pool_p"][l, c], ext[:, c, SEQ:EP]).then_inc(out_state, 16)
                    pool.dma_start(a["out_pool_s"][l, c],
                                   ext[:, c, EP:].rearrange("p (b n) -> p b n", b=NB)[:, :, TB:ES]).then_inc(out_state, 16)
                if l == 0:
                    pool.wait_ge(z_full, ZI[f"fu1.{NFC - 1}"] + 1)
                    done(nc.gpsimd.memset(QA[:, :], 0.0), qz_zeroed)
            pool.wait_ge(av_done, T_L * DEPTH)
            done(nc.gpsimd.memset(zrow, 0.0), zeros_set)
            pool.dma_start(x_dram[ROWS:ROWS + CH, :], zrow).then_inc(xd_zero, 16)
            pool.dma_start(y_dram[ROWS:ROWS + CH, :], zrow).then_inc(xd_zero, 16)
            pool.wait_ge(slot_ready, 1)
            for t in range(5):
                r = P if t < 4 else NS
                pool.wait_ge(z_free["act"], freed(f"ht{t}"))
                for k in range(2):
                    pool.indirect_dma_start(x_dram[:, :], bass.IndirectOffsetOnAxis(SLOT[0:r, 2 * t + k:2 * t + k + 1], 0),
                                            htok[0:r, t, :], None).then_inc(scattered, 16)
            pool.wait_ge(scattered, 160)
            pool.wait_ge(xd_zero, 32)
            pool.wait_ge(task_ready, 1)
            T = pool.value_load(TASK[0:1, 2 * NT:2 * NT + 1], min_val=1, max_val=NT)
            pool.wait_ge(ln_out, LN_ALL)
            r0 = pool.value_load(TASK[0:1, NT:NT + 1], min_val=0, max_val=ROWS)
            pool.dma_start(xg[:, 0, :], x_dram[bass.ds(r0, CH), :]).then_inc(x_loaded, 16)
            pool.sem_inc(ysb_free, 1)
            with pool.Fori(0, T) as t:
                pool.wait_ge(x_turned, t + 1)
                nxt = pool.value_load(TASK[0:1, bass.ds(t + (NT + 1), 1)], min_val=0, max_val=ROWS)
                pool.dma_start(xg[:, 0, :], x_dram[bass.ds(nxt, CH), :]).then_inc(x_loaded, 16)
                pool.wait_ge(e_yout, t + 2)
                row = pool.value_load(TASK[0:1, bass.ds(t + NT, 1)], min_val=0, max_val=ROWS)
                pool.dma_start(y_dram[bass.ds(row, CH), :], ysb).then_inc(y_stored, 16)
                pool.wait_ge(y_stored, t * 16 + 16)
                pool.sem_inc(ysb_free, 1)
            def gather(t):
                r = P if t < 4 else NS
                for k in range(2):
                    pool.indirect_dma_start(ygat[0:r, t % 2, k, :], None, y_dram[:, :],
                                            bass.IndirectOffsetOnAxis(SLOT[0:r, 2 * t + k:2 * t + k + 1], 0)
                                            ).then_inc(y_gathered[t % 2], 16)

            gather(0)
            gather(1)
            pool.wait_ge(lnrow_in, 32)
            for t in range(5):
                r = P if t < 4 else NS
                if t < 3:
                    pool.wait_ge(var_ready, t + 1)
                    gather(t + 2)
                pool.wait_ge(gained, t + 1)
                done(nc.gpsimd.tensor_tensor(xf[0:r, t % 2, :], xf[0:r, t % 2, :], lnrow[0:r, 1, :], ALU.add), fin_ready)

        @block.scalar
        def _(act):
            done = in_order(act, act_own)

            def wait_z(name):
                act.wait_ge(z_full, ZI[name] + 1)

            def free_z(ins):
                done(ins, z_free["act"])

            def squares(lm, src, K, sq_):
                i, before = ln_before[lm]
                for k in range(K):
                    act.wait_ge(ln_centered, before + k + 1)
                    if k >= 2:
                        act.wait_ge(ln_sq_used, before - i + k - 1)
                    done(nc.scalar.activation(sq_[:, k % 2, :], src[:, k, :], ACT.Square), ln_squared)

            def deviation(lv, std_):
                wait_z(lv)
                free_z(nc.scalar.activation(flat(std_), pair(lv), ACT.Sqrt, bias=eps))

            def affine(lm, src, dst, K, gname, bname, l, func):
                before = ln_before[lm][1]
                for k in range(K):
                    act.wait_ge(ln_scaled, before + k + 1)
                    if gname is None:
                        g, b = PAR_[:, DEPTH * NPAR + k:DEPTH * NPAR + k + 1], PAR_[:, DEPTH * NPAR + KD + k:DEPTH * NPAR + KD + k + 1]
                    else:
                        g, b = par(gname, l, k), par(bname, l, k)
                    done(nc.scalar.activation(dst[:, k, :], src[:, k, :], func, bias=b, scale=g), ln_out)

            def norm(lm, lv, src, dst, K, gname, bname, l, func):
                squares(lm, src, K, sq)
                deviation(lv, std)
                affine(lm, src, dst, K, gname, bname, l, func)

            eps = SM[:, 42:43]
            act.wait_ge(qz_zeroed, 1)
            done(nc.scalar.activation(eps, SM[:, 41:42], ACT.Copy, bias=EPS))
            act.wait_ge(consts_in, 48)
            norm("lm", "lv", x, h, KD, None, None, 0, ACT.Identity)
            for l in range(DEPTH):
                for c in range(2):
                    wait_z(f"g{c}.{l}")
                    free_z(nc.scalar.activation(flat(sig[:, c, :]), pair(f"g{c}.{l}"), ACT.Sigmoid, bias=par("bin", l, c)))
                for c, name in enumerate(("ck", "cv")):
                    wait_z(f"{name}.{l}")
                    if c == 0:
                        act.wait_ge(ln_out, ln_done("lm" if l == 0 else "lm2"))
                        if l == 1:
                            act.wait_ge(out_kv, 16 * 8)
                    for ps, lo, hi in pieces(f"{name}.{l}"):
                        dst = PA[:, c * (NBLK + 1) * LB + lo:c * (NBLK + 1) * LB + hi] if hi <= SEQ else kcs[:, c, :]
                        ins = nc.scalar.activation(dst, ps, ACT.Identity, bias=par("bin", l, 8 + c))
                        (done if hi <= SEQ else free_z)(ins)
                    act.dma_start(a["out_kv"][l, c, :, 0:SEQ], PA[:, c * (NBLK + 1) * LB:c * (NBLK + 1) * LB + SEQ]).then_inc(out_kv, 16)
                    act.dma_start(a["out_kv"][l, c, :, SEQ:TOK], kcs[:, c, :]).then_inc(out_kv, 16)
                for n, name in enumerate(("sk", "sv")):
                    wait_z(f"{name}.{l}")
                    free_z(nc.scalar.activation(flat(kvz[:, 2 + n, :]), pair(f"{name}.{l}"), ACT.Identity, bias=par("bin", l, 10 + n)))
                    act.dma_start(a["out_kv"][l, 2 + n], kvz[:, 2 + n, :]).then_inc(out_kv, 16)
                for n, name in enumerate(("wk", "wv")):
                    wait_z(f"{name}.{l}")
                    free_z(nc.scalar.activation(flat(kvz[:, n, :]), pair(f"{name}.{l}"), ACT.Identity, bias=par("bin", l, 4 + n)))
                    act.dma_start(a["out_kv"][l, 4 + n], kvz[:, n, :]).then_inc(out_kv, 16)
                for c in range(2):
                    wait_z(f"p{c}.{l}")
                    for ps, lo, hi in pieces(f"p{c}.{l}"):
                        if hi <= SEQ:
                            done(nc.scalar.activation(ext[:, c, PW - 1 + lo:PW - 1 + hi], ps, ACT.Identity, bias=par("bin", l, 6 + c)))
                        else:
                            free_z(nc.scalar.activation(
                                ext[:, c, EP:].rearrange("p (b n) -> p b n", b=NB)[:, :, PW - 1:],
                                ps.rearrange("p (b n) -> p b n", b=NB), ACT.Identity, bias=par("bin", l, 6 + c)))
                wait_z(f"gate.{l}")
                free_z(nc.scalar.activation(flat(gT), pair(f"gate.{l}", 24), ACT.Sigmoid, bias=par("bin", l, 16, 24)))
                for a_ in range(NPAIR):
                    src = gT[:, SEQ + 2 * TB * a_:SEQ + 2 * TB * (a_ + 1)].rearrange("p (b n) -> p b n", b=2)
                    ins = nc.scalar.activation(gx[:, a_ * P:(a_ + 1) * P].rearrange("p (b h n) -> p b h n", b=2, h=NH),
                                               src.unsqueeze(2).to_broadcast([24, 2, NH, TB]), ACT.Copy)
                    if a_ == NPAIR - 1:
                        done(ins, gate_spread)
                    else:
                        done(ins)
                squares(f"cm.{l}", conv, 2, csq)
                deviation(f"cvar.{l}", cstd)
                for t in range(5):
                    r = P if t < 4 else NS
                    wait_z(f"vt{t}.{l}")
                    free_z(nc.scalar.activation(vg[0:r, t, :], PS[0:r, z_pair(f"vt{t}.{l}"), 0:280], ACT.Copy))
                affine(f"cm.{l}", conv, conv, 2, "clg", "clb", l, ACT.Silu)
                for c in range(2):
                    wait_z(f"pm{c}.{l}")
                    free_z(nc.scalar.activation(flat(yt[:, 6 + c, :]), pair(f"pm{c}.{l}"), ACT.Identity, scale=par("psc", l, c)))
                wait_z(f"vct.{l}")
                free_z(nc.scalar.activation(VC[:, :], PS[0:NBLK, z_pair(f"vct.{l}"), 0:P], ACT.Copy))
                for c in range(2):
                    wait_z(f"pw{c}.{l}")
                    free_z(nc.scalar.activation(flat(yt[:, c, :]), pair(f"pw{c}.{l}"), ACT.Identity, bias=par("pwb", l, c)))
                def split_high(l, p):
                    if p < pieces_start[l] + 4:
                        wait_z(f"cmp1.{l}")
                    elif p < pieces_end[l]:
                        wait_z(piece_read[p - 4])
                    else:
                        return
                    act.wait_ge(piece_in[p % 4], 16 * (p // 4 + 1))
                    done(nc.scalar.activation(piece_parts[p % 4][0], piece_raw[p % 4], ACT.Copy), w_high)

                tt, pm = [l * T_L], [0]

                def turned(copies):
                    n = tt[0]
                    act.wait_ge(t_full, n + 1)
                    if n - l * T_L >= 3:
                        act.wait_ge(av_done, n - 2)
                    for i, (dst, src) in enumerate(copies(n)):
                        ins = nc.scalar.activation(dst, src, ACT.Copy)
                        if i == len(copies(n)) - 1:
                            done(ins, t_out)
                        else:
                            done(ins)
                    tt[0] += 1

                def exps(u, kind):
                    act.wait_ge(p_max, l * U_L + u + 1)
                    s, pc = u % 4, pcmp[u // 2 % 2]
                    if kind == "prompt":
                        i, g, w = units[u]
                        if w == 0:
                            done(nc.scalar.activation(pc[:, 0:GRP * NBP], pc[:, 0:GRP * NBP], ACT.Exp))
                        for j in range(GRP):
                            ins = nc.scalar.activation(pr[s][:, j, 0:(i + 1) * P], pr[s][:, j, 0:(i + 1) * P], ACT.Exp,
                                                       bias=less(s, j), accum_out=total(s, j))
                            if j == GRP - 1:
                                done(ins, p_exp)
                            else:
                                done(ins)
                    else:
                        if kind == 0:
                            done(nc.scalar.activation(pc[:, 0:NBLK], pc[:, 0:NBLK], ACT.Exp, bias=less(s, 4), accum_out=total(s, 4)))
                        done(nc.scalar.activation(pr[s][:, 0, 0:PAST + NS], pr[s][:, 0, 0:PAST + NS], ACT.Exp,
                                                  bias=less(s, 0), accum_out=total(s, 0)), p_exp)

                def outs(u, kind):
                    if kind == "prompt":
                        i, g, w = units[u]
                        if w == 0:
                            turned(lambda n: [(ptr[0:NBP, n % 3, :], PS[0:NBP, 4 + n % 2, :])])
                        for k in range(i + 1):
                            turned(lambda n: [(ptr[:, n % 3, :], PS[:, 4 + n % 2, :])])
                    else:
                        c = lambda n: [(ptr[:, n % 3, 0:256], PS[:, 4 + n % 2, 0:256]),
                                       (ptr[0:NS, n % 3, 256:384], PS[0:NS, 4 + n % 2, 256:384])] + (
                            [(ptr[0:NBLK, n % 3, 384:512], PS[0:NBLK, 4 + n % 2, 384:512])] if kind == 0 else [])
                        turned(c)

                kinds = ["prompt"] * NU + [0, 1] * NPAIR
                for u in range(U_L + 3):
                    if u >= 3:
                        outs(u - 3, kinds[u - 3])
                    if u < U_L:
                        exps(u, kinds[u])
                    if 4 <= u < 4 + KD:
                        m = u - 4
                        done(nc.scalar.activation(h[:, m, :], h[:, m, :], ACT.Identity, bias=par("bo", l, m), scale=ALPHA), h_scaled)
                    elif NU <= u < NU + 4:
                        split_high(l, pieces_start[l] + u - NU)

                act.wait_ge(o_out, O_L * (l + 1))
                for k in MIXED:
                    done(nc.scalar.activation(mixed_parts[0][:, k, :], yt[:, k, :], ACT.Copy), mixed_high)
                for m in range(KD):
                    split_high(l, pieces_of["o", m, l] + 4)
                norm(f"lm1.{l}", f"lv1.{l}", h, h, KD, "g1", "b1", l, ACT.Identity)
                if l == 0:
                    for c in range(NFC + 1):
                        for m in range(2 if c < NFC else 0):
                            wait_z(f"fg{m}.{c}")
                            if 2 * c + m >= 1:
                                act.wait_ge(z_free["dve"], freed(f"fu{1 - m}.{c - 1 + m}"))
                            free_z(nc.scalar.activation(flat(silu), pair(f"fg{m}.{c}"), ACT.Silu))
                            split_high(l, pieces_of[f"fg{m}", c] + 4)
                            split_high(l, pieces_of[f"fu{m}", c] + 4)
                        for k in range(2 if c > 0 else 0):
                            split_high(l, pieces_of[k, c - 1] + 4)
                    norm("lm2", "lv2", x, h, KD, "g2", "b2", 0, ACT.Identity)
            wait_z("rl")
            free_z(nc.scalar.activation(flat(logits), pair("rl", NE), ACT.Copy))
            for t in range(5):
                r = P if t < 4 else NS
                wait_z(f"ht{t}")
                b = z_pair(f"ht{t}")
                if t == 2:
                    act.wait_ge(route_masks, 1)
                    done(nc.scalar.activation(RT[:, 360:365], RT[:, 365:370], ACT.Exp), gate_exp)
                free_z(nc.scalar.activation(htok[0:r, t, :].rearrange("p (a n) -> p a n", a=2), PS[0:r, b:b + 2, :], ACT.Copy))
            act.wait_ge(scattered, 160)
            for t in range(5):
                r = P if t < 4 else NS
                done(nc.scalar.activation(htok[0:r, t, :], htok[0:r, t, :], ACT.Copy, scale=ALPHA), h_alpha)
            act.wait_ge(task_ready, 1)
            T = act.value_load(TASK[0:1, 2 * NT:2 * NT + 1], min_val=1, max_val=NT)
            rows = xgT.rearrange("p (a k) n -> p a (k n)", a=2)
            act.wait_ge(x_turned, 1)
            done(nc.scalar.activation(rows, PS[:, 0:2, :], ACT.Copy), xT_ready)
            with act.Fori(0, T) as t:
                loop = in_order(act, act_loop)

                def turn_out(c):
                    k = 2 if c < NEC - 1 else 1
                    act.wait_ge(eT_full, t * NEC + (c + 1))
                    act.wait_ge(e_down, t * NEC + (c + 1))
                    loop(nc.scalar.activation(ehT[:, c % 2, 0:k, :],
                                                     PS[:, 4 + c % 2, 0:k * P].rearrange("p (k n) -> p k n", k=k), ACT.Copy), eT_ready, t * NEC)

                for c in range(NEC):
                    w = 256 if c < NEC - 1 else P
                    act.wait_ge(e_full, t * NEC + (c + 4))
                    if c >= 2:
                        act.wait_ge(e_hid, t * NEC + (c - 1))
                    loop(nc.scalar.activation(esil[:, c % 2, 0:w], PS[:, 2 + c % 2, 0:w], ACT.Silu), e_silu, t * NEC)
                    if c > 0:
                        turn_out(c - 1)
                turn_out(NEC - 1)
                act.wait_ge(x_turned, t + 2)
                loop(nc.scalar.activation(rows, PS[:, 0:2, :], ACT.Copy), xT_ready, t + 1)
            for t in range(5):
                r = P if t < 4 else NS
                act.wait_ge(var_ready, t + 1)
                done(nc.scalar.activation(rstd(t, r), RT[0:r, 914:915], ACT.Sqrt), dev_ready)
                act.wait_ge(stats_ready, t + 1)
                if t >= 2:
                    act.wait_ge(out_y[t % 2], 16 * (t // 2))
                done(nc.scalar.activation(xf[0:r, t % 2, :], htok[0:r, t, :], ACT.Identity, bias=shift(t, r), scale=rstd(t, r)), normalized)

        @block.vector
        def _(dve):
            done = in_order(dve, dve_own)
            V = nc.vector

            def wait_z(name):
                dve.wait_ge(z_full, ZI[name] + 1)

            def free_z(ins):
                done(ins, z_free["dve"])

            def center(lm, src, K):
                wait_z(lm)
                for k in range(K):
                    done(V.tensor_tensor(flat(src[:, k, :]), flat(src[:, k, :]), pair(lm), ALU.subtract), ln_centered)

            def scale(lv, src, K, std_):
                dve.wait_ge(z_free["act"], freed(lv))
                done(V.reciprocal(std_, std_))
                for k in range(K):
                    done(V.tensor_tensor(src[:, k, :], src[:, k, :], std_, ALU.mult), ln_scaled)

            def norm(lm, lv, src, K):
                center(lm, src, K)
                scale(lv, src, K, std)

            def samples(ap):
                return ap.rearrange("p (b n) -> p b n", b=NB)

            dve.wait_ge(x_in, 16)
            dve.wait_ge(consts_in, 48)
            norm("lm", "lv", x, KD)
            for l in range(DEPTH):
                if l == 1:
                    dve.wait_ge(out_state, 16 * 8)
                for c in range(2):
                    dve.wait_ge(z_free["act"], freed(f"g{c}.{l}"))
                    wait_z(f"a{c}.{l}")
                    for ps, lo, hi in pieces(f"a{c}.{l}"):
                        if hi <= SEQ:
                            done(V.scalar_tensor_tensor(out=ue[:, c, CW - 1 + lo:CW - 1 + hi], in0=ps, scalar=par("bin", l, 2 + c),
                                                             in1=sig[:, c, lo:hi], op0=ALU.add, op1=ALU.mult))
                        else:
                            free_z(V.scalar_tensor_tensor(out=samples(ue[:, c, UP:])[:, :, CW - 1:], in0=samples(ps),
                                                          scalar=par("bin", l, 2 + c), in1=samples(sig[:, c, lo:hi]),
                                                          op0=ALU.add, op1=ALU.mult))
                dve.wait_ge(states_in, 16 * 5 * (l + 1))
                for c in range(2):
                    views = [(conv[:, c, 0:SEQ], lambda k: ue[:, c, k:k + SEQ]),
                             (samples(conv[:, c, SEQ:TOK]), lambda k: samples(ue[:, c, UP:])[:, :, k:k + TB])]
                    for out_, src in views:
                        done(V.tensor_scalar(out_, src(0), par("cw", l, c * CW), par("cb", l, c), ALU.mult, ALU.add))
                    for k in range(1, CW):
                        for i, (out_, src) in enumerate(views):
                            ins = V.scalar_tensor_tensor(out=out_, in0=src(k), scalar=par("cw", l, c * CW + k), in1=out_,
                                                         op0=ALU.mult, op1=ALU.add)
                            (done(ins, conv_done) if k == CW - 1 and i == 1 else done(ins))
                dve.wait_ge(ln_out, ln_done("lm" if l == 0 else "lm2"))
                done(V.memset(ext[:, :, 0:PW - 1], 0.0))
                dve.wait_ge(states_in, 16 * 5 * (l + 1))
                dve.wait_ge(z_free["act"], freed(f"p1.{l}"))
                done(V.tensor_copy(win_a[:, :, 0:1], ext[:, :, 0:1]))
                done(V.tensor_tensor(win_a[:, :, 1:], ext[:, :, 1:], ext[:, :, 0:EXT - 1], ALU.add))
                done(V.tensor_copy(win_b[:, :, 0:2], win_a[:, :, 0:2]))
                done(V.tensor_tensor(win_b[:, :, 2:], win_a[:, :, 2:], win_a[:, :, 0:EXT - 2], ALU.add))
                done(V.tensor_copy(win_a[:, 1, 0:4], win_b[:, 1, 0:4]))
                done(V.tensor_tensor(win_a[:, 1, 4:], win_b[:, 1, 4:], win_b[:, 1, 0:EXT - 4], ALU.add))
                done(V.tensor_tensor(win_b[64:P, 1, 8:], win_a[64:P, 1, 8:], win_a[64:P, 1, 0:EXT - 8], ALU.add))
                done(V.tensor_copy(win_b[0:64, :, :], win_a[0:64, :, :]))
                for c in range(2):
                    inv = CON_[:, CON["invw"] + c:CON["invw"] + c + 1]
                    done(V.scalar_tensor_tensor(out=pooled[:, c, 0:SEQ], in0=win_b[:, c, PW - 1:EP], scalar=inv,
                                                     in1=ext[:, c, PW - 1:EP], op0=ALU.mult, op1=ALU.subtract))
                    done(V.scalar_tensor_tensor(out=samples(pooled[:, c, SEQ:]), in0=samples(win_b[:, c, EP:])[:, :, PW - 1:],
                                                     scalar=inv, in1=samples(ext[:, c, EP:])[:, :, PW - 1:],
                                                     op0=ALU.mult, op1=ALU.subtract))
                first = pooled[:, :, 0:PW]
                invt = CON_[:, CON["invt"]:CON["invt"] + 2 * PW].rearrange("p (c n) -> p c n", c=2)
                done(V.tensor_tensor(first, win_b[:, :, PW - 1:2 * PW - 1], invt, ALU.mult))
                done(V.tensor_tensor(first, first, ext[:, :, PW - 1:2 * PW - 1], ALU.subtract), pooled_ready)
                def queries(j):
                    name = f"q{j}.{l}"
                    dve.wait_ge(qz_zeroed, l + 1)
                    wait_z(name)
                    for g in range(NKV):
                        rows = slice(HD * g, HD * g + HD)
                        b = PAR_[rows, l * NPAR + PAR["bin"] + 12 + j:l * NPAR + PAR["bin"] + 13 + j]
                        for ps, lo, hi in pieces(name, rows):
                            if hi <= SEQ:
                                done(V.tensor_scalar(qz[rows, g, j, lo:hi], ps, b, HD ** -0.5, ALU.add, ALU.mult))
                            else:
                                for b2 in range(2):
                                    at = b2 * HD + g * 32 + j * TB
                                    ins = V.tensor_scalar(qs[rows, :, b2, at:at + TB],
                                                          ps.rearrange("p (a b n) -> p a b n", a=NPAIR, b=2)[:, :, b2, :],
                                                          b, HD ** -0.5, ALU.add, ALU.mult)
                                    (free_z if g == 1 and b2 == 1 else done)(ins)

                def blocks(c):
                    wait_z(f"cmp{c}.{l}")
                    bk = z_pair(f"cmp{c}.{l}")
                    done(V.tensor_copy(SM[:, 40:41], PS[:, bk, NBLK:NBLK + 1]))
                    free_z(V.tensor_scalar(cct[:, c, :], PS[:, bk, 0:NBLK], SM[:, 40:41], None, ALU.add))

                blocks(0)
                queries(0)
                queries(1)
                center(f"cm.{l}", conv, 2)
                queries(2)
                queries(3)
                scale(f"cvar.{l}", conv, 2, cstd)
                blocks(1)
                wait_z(f"gs.{l}")
                gs = SM[:, 48:60].rearrange("p (a w) -> p a w", a=NPAIR)
                gsel = YT[:, 4 * EXT:4 * EXT + 96].rearrange("p (a h w) -> p a h w", a=NPAIR, h=NH)
                hmask = CON_[:, CON["hmask"]:CON["hmask"] + NH]
                done(V.tensor_tensor(gsel.rearrange("p a h w -> p a w h"),
                                          PS[:, z_pair(f"gs.{l}"), 0:96].rearrange("p (a h w) -> p a w h", a=NPAIR, h=NH),
                                          hmask.unsqueeze(1).unsqueeze(1).to_broadcast([P, NPAIR, 3, NH]), ALU.mult))
                free_z(V.tensor_reduce(gs, gsel.rearrange("p a h w -> p a w h"), AX.X, ALU.add))

                entry, group = [l * S_L], [0]
                dve.wait_ge(out_kv, 16 * 8 * (l + 1))

                def score():
                    e = entry[0]
                    dve.wait_ge(s_full, e + 1)
                    entry[0] += 1
                    return PS[:, e % 4, :]

                mx = SM[:, 44:48]

                def maxes(u):
                    s, pc = u % 4, pcmp[u // 2 % 2]
                    if u >= 4:
                        dve.wait_ge(t_full, l * T_L + tiles_through(u - 4))
                    if u == 3:
                        wait_z(f"pw1.{l}")
                    if u < NU:
                        i, g, w = units[u]
                        n = (i + 1) * P
                        if w == 0:
                            ps = score()
                            pc3 = pc[:, 0:GRP * NBP].rearrange("p (j n) -> p j n", j=GRP)
                            done(V.tensor_tensor(pc[:, 0:GRP * NBP], ps[:, 0:GRP * NBP], cbias[:, i, g, :], ALU.add), s_read)
                            done(V.tensor_reduce(mx, pc3, AX.X, ALU.max))
                            done(V.tensor_scalar(mx, mx, FLOOR, None, ALU.max))
                            done(V.tensor_tensor(pc3, pc3, mx.unsqueeze(2).to_broadcast([P, GRP, NBP]), ALU.subtract))
                        for j in range(GRP):
                            ps = score()
                            done(V.tensor_tensor_reduce(out=pr[s][:, j, 0:n], in0=bias[:, g * GRP + j, SEQ - n:SEQ], in1=ps[:, 0:n],
                                                               scale=1.0, scalar=FLOOR, op0=ALU.add, op1=ALU.max,
                                                               accum_out=mx[:, j:j + 1]), s_read)
                        done(V.tensor_scalar(less(s, 0, GRP), mx, -1.0, None, ALU.mult), p_max)
                    else:
                        a_, w = divmod(u - NU, 2)
                        if w == 0:
                            ps = score()
                            done(V.tensor_tensor_reduce(
                                out=pc[:, 0:NBLK], in0=CON_[:, CON["scmp"] + a_ * NBLK:CON["scmp"] + (a_ + 1) * NBLK], in1=ps[:, 0:NBLK],
                                scale=1.0, scalar=FLOOR, op0=ALU.add, op1=ALU.max, accum_out=mx[:, 0:1]), s_read)
                            done(V.tensor_scalar(less(s, 4), mx[:, 0:1], -1.0, None, ALU.mult))
                        ps = score()
                        done(V.tensor_tensor_reduce(
                            out=pr[s][:, 0, 0:PAST], in0=CON_[:, CON["spast"]:CON["spast"] + PAST], in1=ps[:, 0:PAST],
                            scale=1.0, scalar=FLOOR, op0=ALU.add, op1=ALU.max, accum_out=mx[:, 0:1]))
                        done(V.tensor_tensor_reduce(
                            out=pr[s][:, 0, PAST:PAST + NS], in0=CON_[:, CON["snew"] + a_ * NS:CON["snew"] + (a_ + 1) * NS],
                            in1=ps[:, PAST:PAST + NS], scale=1.0, scalar=FLOOR, op0=ALU.add, op1=ALU.max, accum_out=mx[:, 1:2]), s_read)
                        done(V.tensor_tensor(mx[:, 0:1], mx[:, 0:1], mx[:, 1:2], ALU.max))
                        done(V.tensor_scalar(less(s, 0), mx[:, 0:1], -1.0, None, ALU.mult), p_max)

                def split_low(l, p):
                    if p < pieces_end[l]:
                        dve.wait_ge(w_high, p + 1)
                        hi, lo = piece_parts[p % 4]
                        done(V.tensor_tensor(lo, piece_raw[p % 4], hi.bitcast(F32), ALU.subtract), w_low)

                rs, rc = SM[:, 32:36], SM[:, 36:40]

                def factors(sums, gate, n):
                    done(V.tensor_scalar(rs[:, 0:n], sums, TINY, None, ALU.max))
                    done(V.reciprocal(rc[:, 0:n], rs[:, 0:n]))
                    done(V.tensor_tensor(rc[:, 0:n], rc[:, 0:n], gate, ALU.mult))

                def ready(u):
                    s, pc = u % 4, pcmp[u // 2 % 2]
                    dve.wait_ge(p_exp, l * U_L + u + 1)
                    if u < NU:
                        i, g, w = units[u]
                        n = (i + 1) * P
                        gates = vg[:, i, 256 + 12 * g:268 + 12 * g].rearrange("p (j w) -> p j w", w=3)
                        if w == 0:
                            pc3 = pc[:, 0:GRP * NBP].rearrange("p (j n) -> p j n", j=GRP)
                            done(V.tensor_reduce(mx, pc3, AX.X, ALU.add))
                            factors(mx, gates[:, :, 0], GRP)
                            done(V.tensor_tensor(pc3, pc3, rc.unsqueeze(2).to_broadcast([P, GRP, NBP]), ALU.mult))
                        factors(total(s, 0, GRP), gates[:, :, 1 + w], GRP)
                        for j in range(GRP):
                            ins = V.tensor_scalar(pr[s][:, j, 0:n], pr[s][:, j, 0:n], rc[:, j:j + 1], None, ALU.mult)
                            if j == GRP - 1:
                                done(ins, p_ready)
                            else:
                                done(ins)
                    else:
                        a_, w = divmod(u - NU, 2)
                        if w == 0:
                            factors(total(s, 4), gs[:, a_, 0:1], 1)
                            done(V.tensor_scalar(pc[:, 0:NBLK], pc[:, 0:NBLK], rc[:, 0:1], None, ALU.mult))
                        factors(total(s, 0), gs[:, a_, 1 + w:2 + w], 1)
                        done(V.tensor_scalar(pr[s][:, 0, 0:PAST + NS], pr[s][:, 0, 0:PAST + NS], rc[:, 0:1], None, ALU.mult), p_ready)

                def out(u):
                    o = group[0] + l * O_L
                    dve.wait_ge(av_done, l * T_L + tiles_through(u))
                    ps = PS[:, 6 + o % 2, :]
                    if u < NU:
                        i, g, _ = units[u]
                        rows = slice(HD * g, HD * g + HD)
                        done(V.tensor_copy(yt[rows, 2:6, i * P:(i + 1) * P], ps[rows, :].rearrange("p (j n) -> p j n", j=GRP)), o_out)
                    else:
                        a_ = (u - NU) // 2
                        for g in range(NKV):
                            rows = slice(HD * g, HD * g + HD)
                            ins = V.tensor_copy(
                                yt[rows, 2:6, SEQ + 2 * TB * a_:SEQ + 2 * TB * (a_ + 1)].rearrange("p j (b n) -> p j b n", b=2),
                                ps[rows, 0:P].rearrange("p (b g j n) -> p g j b n", b=2, g=NKV, j=GRP)[:, g])
                            if g == 1:
                                done(ins, o_out)
                            else:
                                done(ins)
                    group[0] += 1

                dve.wait_ge(out_state, 16 * 8 * (l + 1))
                for u in range(U_L + 4):
                    if u < U_L:
                        maxes(u)
                    if 1 <= u <= U_L:
                        ready(u - 1)
                    if u >= 4 and u % 2 == 1:
                        out(u - 4)
                    if NU < u <= NU + 4:
                        split_low(l, pieces_start[l] + u - NU - 1)
                assert entry[0] == (l + 1) * S_L
                dve.wait_ge(h_scaled, KD * (l + 1))
                for i, k in enumerate(MIXED):
                    hi, lo = (part[:, k, :] for part in mixed_parts)
                    dve.wait_ge(mixed_high, KD * l + i + 1)
                    done(V.tensor_tensor(lo, yt[:, k, :], hi.bitcast(F32), ALU.subtract), mixed_low)
                for m in range(KD):
                    wait_z(f"o{m}.{l}")
                    free_z(V.tensor_tensor(flat(h[:, m, :]), flat(h[:, m, :]), pair(f"o{m}.{l}"), ALU.add))
                    split_low(l, pieces_of["o", m, l] + 4)
                norm(f"lm1.{l}", f"lv1.{l}", h, KD)
                if l == 0:
                    before = ln_before["lm1.0"][1]
                    for k in range(KD):
                        dve.wait_ge(ln_out, before + k + 1)
                        done(V.tensor_copy(h_parts[0][:, k, :], h[:, k, :]))
                        done(V.tensor_tensor(h_parts[1][:, k, :], h[:, k, :], h_parts[0][:, k, :].bitcast(F32), ALU.subtract), h_low)
                    dve.wait_ge(out_state, 16 * 8)
                    for c in range(NFC + 1):
                        if c < NFC:
                            for m in range(2):
                                dve.wait_ge(z_free["act"], freed(f"fg{m}.{c}"))
                                wait_z(f"fu{m}.{c}")
                                if c >= 2:
                                    wait_z(f"fd{KD - 1}.{c - 2}")
                                free_z(V.tensor_tensor(flat(hid), flat(silu), pair(f"fu{m}.{c}"), ALU.mult))
                                hi, lo = (part[:, c % 2, m, :] for part in hid_parts)
                                done(V.tensor_copy(hi, hid))
                                done(V.tensor_tensor(lo, hid, hi.bitcast(F32), ALU.subtract), hid_low)
                                split_low(l, pieces_of[f"fg{m}", c] + 4)
                                split_low(l, pieces_of[f"fu{m}", c] + 4)
                        if c > 0:
                            for m in range(KD):
                                wait_z(f"fd{m}.{c - 1}")
                                if c == 1:
                                    dve.wait_ge(ln_out, ln_done("lm1.0"))
                                    free_z(V.scalar_tensor_tensor(out=flat(x[:, m, :]), in0=flat(h[:, m, :]), scalar=ALPHA,
                                                                  in1=pair(f"fd{m}.{c - 1}"), op0=ALU.mult, op1=ALU.add))
                                else:
                                    free_z(V.tensor_tensor(flat(x[:, m, :]), flat(x[:, m, :]), pair(f"fd{m}.{c - 1}"), ALU.add))
                            for k in range(2):
                                split_low(l, pieces_of[k, c - 1] + 4)
                    norm("lm2", "lv2", x, KD)

            dve.wait_ge(moe_in, 32)
            mc = lambda name: MC[:, MCON[name]:MCON[name] + NE]
            cols = lambda i: RT[:, 40 * i:40 * i + 40].rearrange("p (t e) -> p t e", e=NE)
            each = lambda i: RT[:, 320 + 5 * i:325 + 5 * i]
            wide = lambda ap: ap.unsqueeze(2).to_broadcast([P, 5, NE])
            rev = mc("rev").unsqueeze(1).to_broadcast([P, 5, NE])
            lg, a1, a2, tmp, rank, off = (cols(i) for i in range(6))
            m1, m2, r1, ex, g1, g2, nd = each(0), each(1), each(2), each(8), each(3), each(4), each(9)
            dve.wait_ge(moe_rb, 16)
            done(V.memset(RT[:, :], 0.0))
            wait_z("rt")
            bk = z_pair("rt")
            done(V.tensor_tensor(lg[:, 0:4, :], PS[:, bk, 0:32].rearrange("p (t e) -> p t e", e=NE),
                                      mc("rb").unsqueeze(1).to_broadcast([P, 4, NE]), ALU.add))
            free_z(V.tensor_tensor(lg[0:NS, 4, :], PS[0:NS, bk, 32:40], MC[0:NS, MCON["rb"]:MCON["rb"] + NE], ALU.add))
            for a_, m in ((a1, m1), (a2, m2)):
                done(V.tensor_reduce(m, lg, AX.X, ALU.max))
                done(V.tensor_tensor(tmp, lg, wide(m), ALU.is_equal))
                done(V.tensor_tensor(tmp, tmp, rev, ALU.mult))
                done(V.tensor_reduce(r1, tmp, AX.X, ALU.max))
                done(V.tensor_tensor(a_, tmp, wide(r1), ALU.is_equal))
                if a_ is a1:
                    done(V.scalar_tensor_tensor(out=lg, in0=a1, scalar=-BIG, in1=lg, op0=ALU.mult, op1=ALU.add))
            done(V.memset(RT[NS:P, 72:80], 0.0))
            done(V.memset(RT[NS:P, 112:120], 0.0))
            done(V.tensor_tensor(nd, m2, m1, ALU.subtract))
            done(V.tensor_tensor(tmp, a1, a2, ALU.add), route_masks)
            wait_z("rk")
            bk = z_pair("rk")
            done(V.tensor_copy(RT[:, 160:192], PS[:, bk, 0:32]))
            done(V.tensor_copy(RT[0:NS, 192:200], PS[0:NS, bk, 32:40]))
            cnt = RT[:, 400:408]
            free_z(V.tensor_copy(cnt, PS[:, bk, 40:48]))

            def before(dst, src, at):
                s0, s1 = RT[:, at:at + 12], RT[:, at + 12:at + 24]
                done(V.tensor_copy(s0[:, 5:12], src[:, 0:7]))
                done(V.tensor_tensor(s1[:, 4:12], s0[:, 4:12], s0[:, 3:11], ALU.add))
                done(V.tensor_tensor(s0[:, 4:12], s1[:, 4:12], s1[:, 2:10], ALU.add))
                done(V.tensor_tensor(dst, s0[:, 4:12], s0[:, 0:8], ALU.add))

            offs = RT[:, 408:416]
            before(offs, cnt, 420)
            done(V.tensor_tensor(rank, rank, offs.unsqueeze(1).to_broadcast([P, 5, NE]), ALU.add))
            for k, a_ in enumerate((a1, a2)):
                done(V.tensor_tensor(tmp, a_, rank, ALU.mult))
                done(V.tensor_reduce(r1, tmp, AX.X, ALU.add))
                ins = V.tensor_copy(SLOT[:, :].rearrange("p (t k) -> p t k", k=2)[:, :, k], r1)
                (done(ins, slot_ready) if k else done(ins))
            nch, cb, ce, hit = RT[:, 450:458], RT[:, 458:466], RT[:, 466:474], RT[:, 474:482]
            done(V.memset(nch, 1.0))
            for m in range(1, -(-TOK // CH)):
                done(V.tensor_scalar(hit, cnt, float(m * CH), None, ALU.is_gt))
                done(V.tensor_tensor(nch, nch, hit, ALU.add))
            before(cb, nch, 490)
            done(V.tensor_tensor(ce, cb, nch, ALU.add))
            tb = lambda i: RT[0:1, 520 + NT * NE * i:520 + NT * NE * (i + 1)].rearrange("p (t e) -> p t e", e=NE)
            over = lambda ap: ap[0:1, :].unsqueeze(1).to_broadcast([1, NT, NE])
            tk = MC[0:1, MCON["task"]:MCON["task"] + NE * NT].rearrange("p (t e) -> p t e", e=NE)
            ind, sel = tb(0), tb(1)
            done(V.tensor_tensor(ind, tk, over(cb), ALU.is_ge))
            done(V.tensor_tensor(sel, tk, over(ce), ALU.is_lt))
            done(V.tensor_tensor(ind, ind, sel, ALU.mult))
            done(V.tensor_tensor(sel, ind, over(mc("iota")), ALU.mult))
            num = RT[0:1, 800:800 + 2 * NT + 1]
            done(V.tensor_reduce(num[:, 0:NT], sel, AX.X, ALU.add))
            done(V.tensor_tensor(sel, tk, over(cb), ALU.subtract))
            done(V.scalar_tensor_tensor(out=sel, in0=sel, scalar=float(CH), in1=over(offs), op0=ALU.mult, op1=ALU.add))
            done(V.tensor_tensor(sel, sel, ind, ALU.mult))
            done(V.tensor_reduce(num[:, NT:2 * NT], sel, AX.X, ALU.add))
            done(V.tensor_copy(num[:, 2 * NT:2 * NT + 1], ce[0:1, NE - 1:NE]))
            done(V.tensor_copy(TASK[:, :], num), task_ready)
            dve.wait_ge(gate_exp, 1)
            done(V.tensor_scalar(g2, ex, 1.0, None, ALU.add))
            done(V.reciprocal(g1, g2))
            done(V.tensor_tensor(g2, g1, ex, ALU.mult))
            T = dve.value_load(TASK[0:1, 2 * NT:2 * NT + 1], min_val=1, max_val=NT)
            dve.sem_inc(e_yout, 1)
            with dve.Fori(0, T) as t:
                loop = in_order(dve, dve_loop)
                for c in range(NEC):
                    n = 256 if c < NEC - 1 else P
                    dve.wait_ge(e_silu, t * NEC + (c + 1))
                    if c >= 2:
                        dve.wait_ge(eT_full, t * NEC + (c - 1))
                    loop(V.tensor_tensor(ehid[:, c % 2, 0:n], esil[:, c % 2, 0:n], PS[:, 2 + c % 2, n:2 * n], ALU.mult), e_hid, t * NEC)
                dve.wait_ge(e_down, t * NEC + (NEC + 2))
                dve.wait_ge(ysb_free, t + 1)
                loop(V.tensor_copy(ysb.rearrange("p (a n) -> p a n", a=2), PS[:, 6:8, :]), e_yout, t + 1)

            dve.wait_ge(lnrow_in, 32)
            st, ag = RT[:, 900:912], RT[:, 912:916]

            def gain(t):
                r = P if t < 4 else NS
                dve.wait_ge(normalized, t + 1)
                done(V.tensor_tensor(xf[0:r, t % 2, :], xf[0:r, t % 2, :], lnrow[0:r, 0, :], ALU.mult), gained)

            dve.wait_ge(h_alpha, 5)
            for t in range(5):
                r = P if t < 4 else NS
                s = t % 2
                y = htok[0:r, t, :]
                dve.wait_ge(y_gathered[s], 32 * (t // 2 + 1))
                for k, g in enumerate((g1, g2)):
                    done(V.scalar_tensor_tensor(out=y, in0=ygat[0:r, s, k, :], scalar=g[0:r, t:t + 1], in1=y,
                                                     op0=ALU.mult, op1=ALU.add))
                for k in range(2):
                    done(V.bn_stats(st[0:r, 6 * k:6 * k + 6], y[:, 512 * k:512 * k + 512]))
                done(V.bn_aggr(ag[0:r, 0:2], st[0:r, :]))
                done(V.tensor_scalar(ag[0:r, 2:3], ag[0:r, 1:2], EPS, None, ALU.add), var_ready)
                dve.wait_ge(dev_ready, t + 1)
                done(V.reciprocal(rstd(t, r), rstd(t, r)))
                done(V.tensor_scalar(shift(t, r), ag[0:r, 0:1], rstd(t, r), -1.0, ALU.mult, ALU.mult), stats_ready)
                if t > 0:
                    gain(t - 1)
            gain(4)

        @block.tensor
        def _(pe):
            M = nc.tensor.matmul

            def take(name):
                n = ZI[name]
                if n >= 4:
                    prev, owner = sched[n - 4]
                    pe.wait_ge(z_free[owner], freed(prev))
                return z_pair(name)

            def full(ins):
                ins.then_inc(z_full, 1)

            def halves():
                return [(0, slice(0, HALF)), (1, slice(HALF, TOK))]

            def product(name, steps, rows=P, normed=None):
                b = take(name)
                for i, (w, act_) in enumerate(steps):
                    if normed is not None:
                        pe.wait_ge(ln_out, normed + i + 1)
                    for n, cols in halves():
                        last = M(PS[0:rows, b + n, 0:HALF], w, act_[:, cols], start=(i == 0), stop=(i == len(steps) - 1))
                full(last)

            def means(lm, src, K, mean):
                product(lm, [(mean[:, :], src[:, k, :]) for k in range(K)])

            def variances(lm, lv, K, mean, sq_):
                before = ln_before[lm][1]
                b = take(lv)
                for k in range(K):
                    pe.wait_ge(ln_squared, before + k + 1)
                    for n, cols in halves():
                        last = M(PS[:, b + n, 0:HALF], mean[:, :], sq_[:, k % 2, cols], start=(k == 0), stop=(k == K - 1))
                    if k < K - 1:
                        last.then_inc(ln_sq_used, 1)
                full(last)

            def norm(lm, lv, src, K, mean):
                means(lm, src, K, mean)
                variances(lm, lv, K, mean, sq)

            def weights(key):
                c = chunk_of[key]
                pe.wait_ge(w_loaded[c % 3], 16 * (c // 3 + 1))
                return WR[c % 3][:, :].rearrange("p (k n) -> p k n", k=KD)

            pe.wait_ge(x_in, 16)
            pe.wait_ge(ones_set, 1)
            norm("lm", "lv", x, KD, MEAN)
            for l in range(DEPTH):
                def project(key, names, normed=None):
                    w = weights((key, l))
                    for name in names:
                        i = TILES[key].index(name)
                        product(f"{name}.{l}", [(w[:, k, i * P:(i + 1) * P], h[:, k, :]) for k in range(KD)],
                                normed=normed if i == 0 else None)

                def compress(c):
                    b = take(f"cmp{c}.{l}")
                    for n in range(2):
                        ch = chunk_of[f"cmp{2 * c + n}", l]
                        pe.wait_ge(w_loaded[ch % 3], 16 * (ch // 3 + 1))
                        w = WR[ch % 3][:, :].rearrange("p (l n) -> p l n", n=P)
                        for i in range(LB // 2):
                            at = n * (LB // 2) + i
                            last = M(PS[:, b, 0:NBLK + 1], w[:, i, :], cmpt[:, c, :, at], start=(at == 0), stop=(at == LB - 1))
                        if n == 0:
                            last.then_inc(half_read, 1)
                    full(last)

                project("glu", TILES["glu"], normed=ln_before["lm" if l == 0 else "lm2"][1])
                project("kcks", TILES["kcks"])
                project("kwp", TILES["kwp"])
                pe.wait_ge(states_in, 16 * 5 * (l + 1))
                product(f"gate.{l}", [(wgate[:, k, :], h[:, k, :]) for k in range(KD)], rows=24)
                pe.wait_ge(pages_in, 16 * (NB * NPG + 1) * (l + 1))
                pe.wait_ge(z_free["act"], freed(f"cv.{l}"))
                compress(0)
                project("q", ("q0", "q1"))
                pe.wait_ge(conv_done, 2 * (l + 1))
                means(f"cm.{l}", conv, 2, MEANC)
                project("q", ("q2", "q3"))
                variances(f"cm.{l}", f"cvar.{l}", 2, MEANC, csq)
                pe.wait_ge(z_free["act"], freed(f"gate.{l}"))
                for t in range(5):
                    r = P if t < 4 else NS
                    b = take(f"vt{t}.{l}")
                    cols = slice(t * P, t * P + r)
                    nc.tensor.transpose(PS[0:r, b, 0:P], kvz[:, 3, cols], ident)
                    nc.tensor.transpose(PS[0:r, b, P:2 * P], kvz[:, 1, cols], ident)
                    full(nc.tensor.transpose(PS[0:r, b, 256:280], gT[:, cols], ident[0:24, 0:24]))
                compress(1)
                pe.wait_ge(mixw_in, 32 * (l + 1))
                pe.wait_ge(pooled_ready, l + 1)
                for c in range(2):
                    product(f"pm{c}.{l}", [(poolw[:, c, :], pooled[:, c, :])])
                b = take(f"vct.{l}")
                pe.wait_ge(z_free["dve"], freed(f"cmp1.{l}"))
                full(nc.tensor.transpose(PS[0:NBLK, b, 0:P], cct[:, 1, :], ident))
                b = take(f"gs.{l}")
                pe.wait_ge(gate_spread, l + 1)
                for a_ in range(NPAIR):
                    last = nc.tensor.transpose(PS[:, b, 24 * a_:24 * a_ + 24], gx[:, a_ * P:(a_ + 1) * P], ident[0:24, 0:24])
                full(last)
                pe.wait_ge(ln_out, ln_done(f"cm.{l}"))
                for c in range(2):
                    product(f"pw{c}.{l}", [(pww[:, k, c * P:(c + 1) * P], conv[:, k, :]) for k in range(2)])

                pe.wait_ge(z_free["act"], freed(f"pw1.{l}"))
                pe.wait_ge(z_free["dve"], freed(f"gs.{l}"))
                entry, tile = [l * S_L], [l * T_L]

                def score_bank():
                    e = entry[0]
                    if e - l * S_L >= 4:
                        pe.wait_ge(s_read, e - 3)
                    entry[0] += 1
                    return PS[:, e % 4, :]

                def scores(u, e):
                    if u < NU:
                        i, g, w = units[u]
                        cols = slice(i * P, (i + 1) * P)
                        if w == 0 and e == 0:
                            ps = score_bank()
                            for j in range(GRP):
                                last = M(ps[:, NBP * j:NBP * (j + 1)], qz[:, g, j, cols], cct[:, 0, 0:NBP], start=True, stop=True)
                            last.then_inc(s_full, 1)
                        else:
                            j = e - (w == 0)
                            ps = score_bank()
                            M(ps[:, 0:(i + 1) * P], qz[:, g, j, cols], kvz[:, 2 - 2 * w, 0:(i + 1) * P],
                              start=True, stop=True).then_inc(s_full, 1)
                    else:
                        a_, w = divmod(u - NU, 2)
                        if w == 0 and e == 0:
                            pe.wait_ge(pair_in[a_ % 2], 16 * 5 * (l * 2 + a_ // 2 + 1))
                            ps = score_bank()
                            for b2 in range(2):
                                last = M(ps[:, 0:NBLK], qs[:, a_, b2, :], cct[:, 0, :], start=(b2 == 0), stop=(b2 == 1))
                            last.then_inc(s_full, 1)
                            return
                        ps = score_bank()
                        for b2 in range(2):
                            M(ps[:, 0:PAST].rearrange("p (g n) -> p g n", g=NPG), qs[:, a_, b2, :], cpair[:, a_ % 2, w, b2, :, 0:P],
                              start=(b2 == 0), stop=(b2 == 1))
                        for b2 in range(2):
                            last = M(ps[:, PAST:PAST + NS], qs[:, a_, b2, :], kvz[:, 2 - 2 * w, SEQ:TOK], start=(b2 == 0), stop=(b2 == 1))
                        last.then_inc(s_full, 1)

                def turn(u, part):
                    n, s, pc = tile[0], u % 4, pcmp[u // 2 % 2]
                    if n - l * T_L >= 2:
                        pe.wait_ge(t_out, n - 1)
                    ps = PS[:, 4 + n % 2, :]
                    if u < NU:
                        for j in range(GRP):
                            if part < 0:
                                last = nc.tensor.transpose(ps[0:NBP, j * P:(j + 1) * P], pc[:, NBP * j:NBP * (j + 1)], ident)
                            else:
                                last = nc.tensor.transpose(ps[:, j * P:(j + 1) * P], pr[s][:, j, part * P:(part + 1) * P], ident)
                    else:
                        if u % 2 == 0:
                            nc.tensor.transpose(ps[0:NBLK, 384:512], pc[:, 0:NBLK], ident)
                        nc.tensor.transpose(ps[:, 0:P], pr[s][:, 0, 0:P], ident)
                        nc.tensor.transpose(ps[:, P:2 * P], pr[s][:, 0, P:2 * P], ident)
                        last = nc.tensor.transpose(ps[0:NS, 256:384], pr[s][:, 0, 2 * P:2 * P + NS], ident)
                    last.then_inc(t_full, 1)
                    tile[0] += 1

                def add_values(u, part, n, o):
                    pe.wait_ge(t_out, n + 1)
                    ps, p_ = PS[:, 6 + o % 2, :], ptr[:, n % 3, :]
                    if u < NU:
                        i, g, w = units[u]
                        if part < 0:
                            last = M(ps, VC[0:NBP, :], p_[0:NBP, :], start=True, stop=False)
                        else:
                            last = M(ps, vg[:, part, w * P:(w + 1) * P], p_, start=False, stop=(w == 1 and part == i))
                    else:
                        a_, w = divmod(u - NU, 2)
                        out = ps[:, 0:P]
                        if w == 0:
                            M(out, VC[:, :], p_[0:NBLK, 384:512], start=True, stop=False, skip_group_check=True)
                        for g in range(NPG):
                            for b2 in range(2):
                                cols = slice(b2 * HD, (b2 + 1) * HD)
                                M(out[:, cols], cpair[:, a_ % 2, w, b2, g, P:2 * P], p_[:, g * P + b2 * HD:g * P + (b2 + 1) * HD],
                                  start=False, stop=False, skip_group_check=True)
                        last = M(out, vg[0:NS, 4, w * P:(w + 1) * P], p_[0:NS, 256:384], start=False, stop=(w == 1), skip_group_check=True)
                    last.then_inc(av_done, 1)

                for u in range(U_L + 3):
                    v = u - 3
                    n_scores = 0 if u >= U_L else GRP + (units[u][2] == 0) if u < NU else 2 - u % 2
                    at = 0
                    if v >= 0:
                        pe.wait_ge(p_ready, l * U_L + v + 1)
                        o = l * O_L + v // 2
                        if v % 2 == 0 and v >= 4:
                            pe.wait_ge(o_out, o - 1)
                        parts = ([-1] if units[v][2] == 0 else []) + list(range(units[v][0] + 1)) if v < NU else [0]
                        turn(v, parts[0])
                        for i, part in enumerate(parts):
                            n = tile[0] - 1
                            until = 0 if u >= NU else n_scores
                            for e in range(at, until):
                                scores(u, e)
                            at = until
                            if i + 1 < len(parts):
                                turn(v, parts[i + 1])
                            add_values(v, part, n, o)
                    for e in range(at, n_scores):
                        scores(u, e)
                pe.wait_ge(s_read, S_L * (l + 1))
                pe.wait_ge(o_out, O_L * (l + 1))

                def split_product(name, steps, split=None):
                    b = take(name)
                    for i, ((w_hi, w_lo), (a_hi, a_lo)) in enumerate(steps):
                        if split is not None:
                            pe.wait_ge(split[0], split[1] + i + 1)
                        for j, (w, act_) in enumerate(((w_hi, a_hi), (w_hi, a_lo), (w_lo, a_hi))):
                            for n, cols in halves():
                                last = M(PS[:, b + n, 0:HALF], w, act_[:, cols], start=(i == j == 0), stop=(i == len(steps) - 1 and j == 2))
                    full(last)

                def piece(p, at):
                    return tuple(w[:, at:at + P] for w in piece_parts[p % 4])

                for m in range(KD):
                    p = pieces_of["o", m, l]
                    pe.wait_ge(w_low, p + 1)
                    split_product(f"o{m}.{l}", [(piece(p, k * P), [part[:, k, :] for part in mixed_parts]) for k in MIXED],
                                  split=(mixed_low, KD * l) if m == 0 else None)
                pe.wait_ge(z_free["dve"], freed(f"o{KD - 1}.{l}"))
                norm(f"lm1.{l}", f"lv1.{l}", h, KD, MEAN)
                if l == 0:
                    for c in range(NFC + 1):
                        for name in ("fg0", "fu0", "fg1", "fu1") if c < NFC else ():
                            p = pieces_of[name, c]
                            pe.wait_ge(w_low, p + 1)
                            split_product(f"{name}.{c}", [(piece(p, k * P), (h_parts[0][:, k, :], h_parts[1][:, k, :])) for k in range(KD)],
                                          split=(h_low, 0) if c == 0 and name == "fg0" else None)
                        if c > 0:
                            pe.wait_ge(hid_low, 2 * c)
                            pe.wait_ge(w_low, pieces_of[1, c - 1] + 1)
                            for m in range(KD):
                                split_product(f"fd{m}.{c - 1}", [(piece(pieces_of[k, c - 1], m * P), tuple(part[:, (c - 1) % 2, k, :] for part in hid_parts))
                                                                 for k in range(2)])
                    pe.wait_ge(z_free["dve"], freed(f"fd{KD - 1}.{NFC - 1}"))
                    norm("lm2", "lv2", x, KD, MEAN)

            pe.wait_ge(moe_in, 32)
            product("rl", [(wrt[:, k, :], h[:, k, :]) for k in range(KD)], rows=NE, normed=ln_before["lm1.1"][1])

            def turn_tokens(t):
                r = P if t < 4 else NS
                b = take(f"ht{t}")
                for k in range(KD):
                    last = nc.tensor.transpose(PS[0:r, b + k // 4, (k % 4) * P:(k % 4 + 1) * P], h[:, k, t * P:t * P + r], ident)
                full(last)

            b = take("rt")
            pe.wait_ge(z_free["act"], freed("rl"))
            for t in range(5):
                r = P if t < 4 else NS
                last = nc.tensor.transpose(PS[0:r, b, NE * t:NE * (t + 1)], logits[:, t * P:t * P + r], ident[0:NE, 0:NE])
            full(last)
            turn_tokens(0)
            turn_tokens(1)
            b = take("rk")
            pe.wait_ge(route_masks, 1)
            masks = RT[:, 120:160].rearrange("p (t e) -> p t e", e=NE)
            ustrict, ones = MC[:, MCON["ustrict"]:MCON["ustrict"] + P], MC[:, MCON["ones"]:MCON["ones"] + P]
            for t in range(5):
                r = P if t < 4 else NS
                for j in range(t):
                    M(PS[0:r, b, NE * t:NE * (t + 1)], ones[:, 0:r], masks[:, j, :], start=(j == 0), stop=False)
                M(PS[0:r, b, NE * t:NE * (t + 1)], ustrict[:, 0:r], masks[:, t, :], start=(t == 0), stop=True)
            for j in range(5):
                last = M(PS[:, b, 40:48], ones, masks[:, j, :], start=(j == 0), stop=(j == 4))
            full(last)
            for t in range(2, 5):
                turn_tokens(t)
            pe.wait_ge(z_free["dve"], freed("rk"))
            pe.wait_ge(z_free["act"], freed("ht4"))
            pe.wait_ge(task_ready, 1)
            T = pe.value_load(TASK[0:1, 2 * NT:2 * NT + 1], min_val=1, max_val=NT)
            pe.sem_inc(e_full, 3)
            pe.sem_inc(e_down, 2)

            def turn_rows():
                for k in range(KD):
                    last = nc.tensor.transpose(PS[:, k // 4, (k % 4) * P:(k % 4 + 1) * P], xg[:, 0, k * P:(k + 1) * P], ident)
                last.then_inc(x_turned, 1)

            pe.wait_ge(x_loaded, 16)
            turn_rows()
            with pe.Fori(0, T) as t:
                pe.wait_ge(xT_ready, t + 1)

                def up(c):
                    k_ = NWC + c
                    n = 512 if c < NEC - 1 else 256
                    pe.wait_ge(w_loaded[k_ % 3], t * (16 * NEC // 3) + 16 * (k_ // 3 + 1))
                    w = WR[k_ % 3][:, 0:KD * n].rearrange("p (k n) -> p k n", k=KD)
                    for k in range(KD):
                        last = M(PS[:, 2 + c % 2, 0:n], xgT[:, k, :], w[:, k, :], start=(k == 0), stop=(k == KD - 1))
                    last.then_inc(e_full, 1)

                def turn_hidden(c):
                    pe.wait_ge(e_hid, t * NEC + (c + 1))
                    for k in range(2 if c < NEC - 1 else 1):
                        last = nc.tensor.transpose(PS[:, 4 + c % 2, k * P:(k + 1) * P], ehid[:, c % 2, k * P:(k + 1) * P], ident)
                    last.then_inc(eT_full, 1)

                def down(c):
                    k_ = c
                    pe.wait_ge(d_loaded[k_ % 2], t * (16 * NEC // 2) + 16 * (k_ // 2 + 1))
                    pe.wait_ge(eT_ready, t * NEC + (c + 1))
                    if c == 0:
                        pe.wait_ge(e_yout, t + 1)
                    for k in range(2 if c < NEC - 1 else 1):
                        for n in range(2):
                            at = (k_ % 2) * 2048 + k * D + n * 512
                            last = M(PS[:, 6 + n, :], ehT[:, c % 2, k, :], CA[:, at:at + 512], start=(c == 0 and k == 0), stop=(c == NEC - 1))
                    last.then_inc(e_down, 1)

                for c in range(NEC):
                    up(c)
                    if c >= 1:
                        turn_hidden(c - 1)
                    if c >= 2:
                        down(c - 2)
                turn_hidden(NEC - 1)
                pe.wait_ge(x_loaded, t * 16 + 32)
                turn_rows()
                down(NEC - 2)
                down(NEC - 1)


_OUTS = {
    "out_y": (TOK, D), "out_kv": (DEPTH, 6, P, TOK), "out_past": (DEPTH, NB, PAST - TB, 2 * P),
    "out_conv_p": (DEPTH, 2, P, CW - 1), "out_conv_s": (DEPTH, 2, P, NB, CW - 1),
    "out_pool_p": (DEPTH, 2, P, PW - 1), "out_pool_s": (DEPTH, 2, P, NB, PW - 1),
}


def constants():
    f = np.float32
    slope = np.array(SLOPE)
    p = np.arange(P)
    dist = (p[:, None] + 384 - np.arange(SEQ)[None, :]).astype(np.float64)
    bias = -slope[None, :, None] * dist[:, None, :]
    bias = np.where(dist[:, None, :] < 0, -1e30, bias)
    con = np.zeros((P, NCON))

    def put(name, v):
        v = np.asarray(v).reshape(P, -1)
        con[:, CON[name]:CON[name] + v.shape[1]] = v

    put("ident", np.eye(P))
    w = np.array([[WINDOWS[2 * c + (q >= 64)] for c in range(2)] for q in range(P)], float)
    put("invw", 1.0 / w)
    put("invt", 1.0 / np.minimum(np.arange(PW)[None, None, :] + 1, w[:, :, None]))
    row_b, row_h, row_t = p // 64, p % 64 // TB, p % TB
    put("hmask", row_h[:, None] == np.arange(NH)[None, :])
    n = np.arange(NBP)
    pos = (np.arange(4)[:, None] * P + p[None, :]).T
    cd = pos[:, :, None] - (n * LB + (LB - 1) / 2)[None, None, :]
    ok = ((n + 1) * LB - 1)[None, None, :] <= pos[:, :, None]
    cb = -slope[None, None, :, None] * cd[:, :, None, :]
    put("cbias", np.where(ok[:, :, None, :], cb, -1e30))
    sl = slope[row_h]
    put("spast", -sl[:, None] * (PAST + row_t[:, None] - np.arange(PAST)[None, :]))
    key_b, key_t = np.arange(NS) // TB, np.arange(NS) % TB
    seq = 2 * np.arange(NPAIR)[None, :] + row_b[:, None]
    d = row_t[:, None, None] - key_t[None, None, :]
    ok = (key_b[None, None, :] == seq[:, :, None]) & (d >= 0)
    put("snew", np.where(ok, -sl[:, None, None] * d, -1e30))
    blk = np.arange(NBLK)
    blk_b = np.where(blk < NBP, -1, (blk - NBP) // NBS)
    centre = ((blk - NBP) % NBS) * LB + (LB - 1) / 2
    ok = blk_b[None, None, :] == seq[:, :, None]
    sc = -sl[:, None, None] * (PAST + row_t[:, None, None] - centre[None, None, :])
    put("scmp", np.where(ok, sc, -1e30))
    mcon = np.zeros((P, NMCON))
    mcon[:, MCON["ustrict"]:MCON["ustrict"] + P] = p[:, None] < p[None, :]
    mcon[:, MCON["ones"]:MCON["ones"] + P] = 1
    mcon[:, MCON["rev"]:MCON["rev"] + NE] = NE - np.arange(NE)
    mcon[:, MCON["iota"]:MCON["iota"] + NE] = np.arange(NE)
    mcon[:, MCON["task"]:MCON["task"] + NT * NE] = np.repeat(np.arange(NT), NE)
    return bias.astype(f), con.astype(f), mcon[:, 0:MCON["rb"]].astype(f)


def layout(v):
    out = {}
    tok = np.concatenate([v["x_prompt"].reshape(SEQ, D), v["x_sample"].reshape(NS, D)])
    rows = lambda w: np.ascontiguousarray(w.reshape(-1, P, w.shape[-1]).transpose(1, 0, 2))
    out["xt"] = rows(np.ascontiguousarray(tok.T))
    heads = [512 + HD * hh + np.arange(HD) for j in range(GRP) for hh in (j, j + GRP)]
    order = {"glu": np.r_[256:512, 0:256], "kwp": np.r_[1536:1792, 1816:2072], "kcks": np.r_[1024:1536], "q": np.concatenate(heads)}
    gate = np.r_[1792:1816]
    out["w_in"] = np.stack([np.stack([rows(w[:, order[n]]).reshape(P, -1) for n in ("glu", "kwp", "kcks", "q")]) for w in v["w_in"]])
    out["w_gate"] = np.stack([rows(w[:, gate]) for w in v["w_in"]])
    cw = v["cmp_w"].reshape(DEPTH, 2, LB, HD, HD)
    bd = np.zeros((DEPTH, 2, NKV, HD, LB, NKV, HD), np.float32)
    for g in range(NKV):
        bd[:, :, g, :, :, g, :] = cw.transpose(0, 1, 3, 2, 4)
    out["cmp_w"] = np.ascontiguousarray(bd.reshape(DEPTH, 2, P, 2, LB // 2, P).transpose(0, 1, 3, 2, 4, 5)).reshape(DEPTH, 4, P, 4096)
    att = np.concatenate([256 + HD * hh + np.arange(HD) for j in range(GRP) for hh in (j, j + GRP)])
    mixed = np.concatenate([np.arange(256), att, np.arange(768, D)])
    outs = [rows(w[mixed]).reshape(P, KD, KD, P).transpose(2, 0, 1, 3).reshape(KD, P, D) for w in v["w_out"]]
    gu, dn = v["ffn_w_gu"][0], v["ffn_w_dn"][0]
    two = lambda w, f, c, n: np.concatenate([w[:, 256 * c + P * i:256 * c + P * (i + 1)] if s == 0 else w[:, f + 256 * c + P * i:f + 256 * c + P * (i + 1)]
                                             for i in range(n) for s in range(2)], 1)
    ups = [rows(two(gu, DFF, c, 2)).reshape(P, KD, 4, P).transpose(2, 0, 1, 3).reshape(4, P, D) for c in range(NFC)]
    downs = [rows(dn[256 * c:256 * (c + 1)]).transpose(1, 0, 2) for c in range(NFC)]
    ffn = np.concatenate([part for c in range(NFC + 1) for part in (ups[c:c + 1] + (downs[c - 1:c] if c else []))])
    out["split_w"] = np.concatenate([outs[0], ffn, outs[1]])
    mg, md = v["moe_w_gu"][0], v["moe_w_dn"][0]
    gate_up = lambda w, c, n: np.concatenate([w[:, 256 * c:256 * c + n], w[:, DFE + 256 * c:DFE + 256 * c + n]], 1)
    out["moe_gu"] = np.stack([np.stack([rows(gate_up(w, c, 256)).reshape(P, -1) for c in range(NEC - 1)]) for w in mg])
    out["moe_gu_last"] = np.stack([rows(gate_up(w, NEC - 1, P)).reshape(P, -1) for w in mg])
    out["moe_dn"] = np.stack([np.stack([rows(w[256 * c:256 * (c + 1)]).reshape(P, -1) for c in range(NEC - 1)]) for w in md])
    out["moe_dn_last"] = np.stack([rows(w[256 * (NEC - 1):]).reshape(P, -1) for w in md])
    out["w_router"] = rows(v["moe_w_router"][0])
    kt = lambda kv, c: kv[..., :, c, :, :].reshape(*kv.shape[:-4], PAGE, P)
    sw = lambda a: np.swapaxes(a, -1, -2)
    cmp_ = v["cache_cmp_kv"]
    out["cmp_pages"] = np.ascontiguousarray(np.stack([sw(kt(cmp_, 0)), sw(kt(cmp_, 1))], 3))
    slc = v["cache_slc_kv"]
    out["slc_pages"] = np.ascontiguousarray(np.concatenate([sw(kt(slc, 0)), kt(slc, 1)], -1))
    swa = v["cache_swa_kv"].reshape(DEPTH, NPAIR, 2, NPG, PAGE, 2, NKV, HD)
    out["swa_pairs"] = np.ascontiguousarray(np.concatenate([sw(kt(swa, 0)), kt(swa, 1)], -1).transpose(0, 1, 4, 2, 3, 5))
    out["swa_cache"] = v["cache_swa_kv"].reshape(DEPTH, NB, PAST, 2 * P)
    pe = v["cmp_pe"].transpose(0, 3, 1, 2)
    out["pe"] = np.ascontiguousarray(np.concatenate([pe, pe], 1))
    chan = lambda s: np.ascontiguousarray(s.reshape(DEPTH, NB, s.shape[2], 2, P).transpose(0, 4, 3, 1, 2))
    out["state_conv"], out["state_pool"] = chan(v["state_conv"]), chan(v["state_pool"])
    pw = np.zeros((DEPTH, 2, 2, HD, 2, HD), np.float32)
    for g in range(2):
        pw[:, :, g, :, g, :] = v["pool_w"].reshape(DEPTH, 2, 2, HD, HD)[:, :, g]
    out["pool_w"] = np.ascontiguousarray(pw.reshape(DEPTH, 2, P, P).transpose(0, 2, 1, 3))
    out["pw_w"] = np.stack([rows(w) for w in v["conv_pw_w"]])
    col = lambda a: a.reshape(-1, P).T
    parts = []
    for l in range(DEPTH):
        b = v["b_in"][l]
        bg = np.zeros((P, 1), np.float32)
        bg[0:24, 0] = b[gate]
        parts += [col(b[np.concatenate([order[n] for n in ("glu", "kwp", "kcks", "q")])]), bg,
                  np.ascontiguousarray(v["conv_dw_w"][l].reshape(CW, 2, P).transpose(2, 1, 0)).reshape(P, -1)]
        parts += [col(v[n][l]) for n in ("conv_dw_b", "conv_ln_g", "conv_ln_b", "conv_pw_b", "pool_scale", "b_out",
                                         "ln1_g", "ln1_b", "ln2_g", "ln2_b")]
    out["par"] = np.ascontiguousarray(np.concatenate(parts + [col(v["ln_in_g"]), col(v["ln_in_b"])], 1))
    out["ln_rows"] = np.stack([v["ln2_g"][1], v["ln2_b"][1]])
    out["rb_row"] = v["moe_b_router"].reshape(1, NE)
    out["page_table"] = v["page_table"].reshape(1, -1).astype(np.int32)
    out["bias"], out["con"], out["mcon"] = constants()
    return out


def kernel(**inputs):
    from concourse import bacc
    from concourse.bass_utils import run_bass_kernel_spmd

    v = {n: np.asarray(x) for n, x in inputs.items()}
    arrays = {f"in_{n}": np.ascontiguousarray(x) for n, x in layout(v).items()}
    nc = bacc.Bacc("TRN2", target_bir_lowering=False, num_devices=1)
    aps = {n[3:]: nc.dram_tensor(n, x.shape, mybir.dt.from_np(x.dtype), kind="ExternalInput").ap() for n, x in arrays.items()}
    for n, shape in _OUTS.items():
        aps[n] = nc.dram_tensor(n, shape, F32, kind="ExternalOutput").ap()
    program(nc, aps)
    r = run_bass_kernel_spmd(nc, [arrays], core_ids=[0]).results[0]
    y, kv, past = r["out_y"], r["out_kv"], r["out_past"]
    rows = kv.reshape(DEPTH, 3, 2, NKV, HD, TOK).transpose(1, 0, 5, 2, 3, 4)
    prompt, new = rows[:, :, :SEQ], rows[:, :, SEQ:].reshape(3, DEPTH, NB, TB, 2, NKV, HD)
    swa = np.concatenate([past.reshape(DEPTH, NB, PAST - TB, 2, NKV, HD), new[2]], 2)
    back = lambda s: s.transpose(0, 3, 4, 1, 2).reshape(DEPTH, NB, s.shape[4], 2 * P)
    return (y[:SEQ].reshape(1, SEQ, D), y[SEQ:].reshape(NB, TB, D),
            prompt[0][:, None], new[0], prompt[1][:, None], new[1],
            prompt[2][:, None, SEQ - PAST:], swa,
            r["out_conv_p"].transpose(0, 3, 1, 2).reshape(DEPTH, 1, CW - 1, 2 * P), back(r["out_conv_s"]),
            r["out_pool_p"].transpose(0, 3, 1, 2).reshape(DEPTH, 1, PW - 1, 2 * P), back(r["out_pool_s"]))
```
